# Optimizing a Trainium2 kernel written in Bass

```python
import jax, jax.numpy as jnp
from jax import lax
import numpy as np

D_MODEL = 1024
BATCH = 1
SEQ = 512
DEPTH = 1

PLE_DIM = 256
LRU_WIDTH = D_MODEL
LRU_BLOCKS = 16
LRU_BLOCK_DIM = LRU_WIDTH // LRU_BLOCKS
CONV_WIDTH = 4
LRU_C = 8.0
SGU_WIDTH = D_MODEL
SGU_GROUPS = 8
SGU_GROUP_DIM = SGU_WIDTH // SGU_GROUPS
CHUNK = 128
N_GROUPS = 4
EXPERTS_PER_GROUP = 8
N_EXPERTS = N_GROUPS * EXPERTS_PER_GROUP
TOP_K = 2
D_EXPERT = 256
EPS = 1e-6
IN_COLS = 2 * LRU_WIDTH + 2 * SGU_WIDTH + 2 * D_MODEL

kernel_name = "hybrid_rglru_sgu_hmoe_block"

def rmsnorm(x, g):
    xf = x.astype(jnp.float32)
    y = xf * lax.rsqrt(jnp.mean(xf * xf, axis=-1, keepdims=True) + EPS)
    return (y * g.astype(jnp.float32)).astype(x.dtype)

def layernorm(x, g, b):
    xf = x.astype(jnp.float32)
    mu = jnp.mean(xf, axis=-1, keepdims=True)
    xc = xf - mu
    y = xc * lax.rsqrt(jnp.mean(xc * xc, axis=-1, keepdims=True) + EPS)
    return (y * g.astype(jnp.float32) + b.astype(jnp.float32)).astype(x.dtype)

def causal_depthwise_conv(x, w, b):
    s = x.shape[1]
    xp = jnp.pad(x, ((0, 0), (CONV_WIDTH - 1, 0), (0, 0)))
    y = b
    for k in range(CONV_WIDTH):
        y = y + xp[:, k:k + s, :] * w[k]
    return y

def rg_lru(x, w_a, b_a, w_i, b_i, lam):
    bsz, s, w = x.shape
    xb = x.reshape(bsz, s, LRU_BLOCKS, LRU_BLOCK_DIM)
    r = jax.nn.sigmoid(jnp.einsum('bshi,hij->bshj', xb, w_a).reshape(bsz, s, w) + b_a)
    i = jax.nn.sigmoid(jnp.einsum('bshi,hij->bshj', xb, w_i).reshape(bsz, s, w) + b_i)
    log_a = -LRU_C * r.astype(jnp.float32) * jax.nn.softplus(-lam.astype(jnp.float32))
    a = jnp.exp(log_a)
    u = jnp.sqrt(-jnp.expm1(2.0 * log_a)) * (i * x).astype(jnp.float32)

    def combine(left, right):
        a1, b1 = left
        a2, b2 = right
        return a1 * a2, a2 * b1 + b2

    _, h = lax.associative_scan(combine, (a, u), axis=1)
    return h.astype(x.dtype)

def spatial_gating(z, ln_g, ln_b, w_s, b_s):
    bsz, s, _ = z.shape
    u, v = jnp.split(z, 2, axis=-1)
    v = layernorm(v, ln_g, ln_b)
    vb = v.reshape(bsz, s // CHUNK, CHUNK, SGU_GROUPS, SGU_GROUP_DIM)
    mask = jnp.tril(jnp.ones((CHUNK, CHUNK), dtype=bool))
    ws = jnp.where(mask[None], w_s, jnp.zeros_like(w_s))
    sp = jnp.einsum('gts,bcsgd->bctgd', ws, vb) + jnp.transpose(b_s)[None, None, :, :, None]
    return u * sp.reshape(bsz, s, SGU_WIDTH)

def hierarchical_moe(h, w_rg, b_rg, w_re, b_re, w1, w3, w2):
    bsz, s, d = h.shape
    t = h.reshape(bsz * s, d)
    n_tok = t.shape[0]
    g_prob = jax.nn.softmax((t @ w_rg + b_rg).astype(jnp.float32), axis=-1)
    g_top, g_idx = lax.top_k(g_prob, 1)
    e_logits = (t @ w_re + b_re).astype(jnp.float32).reshape(n_tok, N_GROUPS, EXPERTS_PER_GROUP)
    e_sel = jnp.take_along_axis(e_logits, g_idx[:, :, None], axis=1)[:, 0]
    e_prob = jax.nn.softmax(e_sel, axis=-1)
    e_top, e_idx = lax.top_k(e_prob, TOP_K)
    e_top = e_top / jnp.sum(e_top, axis=-1, keepdims=True)
    gate = g_top * e_top
    gid = g_idx * EXPERTS_PER_GROUP + e_idx
    combine = jnp.sum(jax.nn.one_hot(gid, N_EXPERTS, dtype=jnp.float32) * gate[..., None], axis=1)
    hid = jax.nn.silu(jnp.einsum('td,edf->tef', t, w1)) * jnp.einsum('td,edf->tef', t, w3)
    hid = hid * combine[:, :, None].astype(hid.dtype)
    out = jnp.einsum('tef,efd->td', hid, w2)
    return out.reshape(bsz, s, d)

def setup_inputs(seed: int = 0) -> dict:
    key = jax.random.key(seed)
    ks = jax.random.split(key, 32)
    f32 = jnp.float32
    L, D = DEPTH, D_MODEL

    def nrm(k, shape, fan_in):
        return jax.random.normal(k, shape, f32) * (fan_in ** -0.5)

    def gain(k, shape):
        return 1.0 + 0.02 * jax.random.normal(k, shape, f32)

    def bias(k, shape):
        return 0.01 * jax.random.normal(k, shape, f32)

    a_c = jax.random.uniform(ks[9], (L, LRU_WIDTH), f32, 0.9, 0.999)
    a0 = a_c ** (1.0 / LRU_C)
    lam = jnp.log(a0) - jnp.log1p(-a0)

    return {
        "x": jax.random.normal(ks[0], (BATCH, SEQ, D), f32),
        "p": jax.random.normal(ks[1], (DEPTH, BATCH, SEQ, PLE_DIM), f32),
        "mix_norm": gain(ks[2], (L, D)),
        "w_in": nrm(ks[3], (L, D, IN_COLS), D),
        "conv_w": nrm(ks[4], (L, CONV_WIDTH, LRU_WIDTH), CONV_WIDTH),
        "conv_b": bias(ks[5], (L, LRU_WIDTH)),
        "lru_wa": nrm(ks[6], (L, LRU_BLOCKS, LRU_BLOCK_DIM, LRU_BLOCK_DIM), LRU_BLOCK_DIM),
        "lru_ba": bias(ks[7], (L, LRU_WIDTH)),
        "lru_wi": nrm(ks[8], (L, LRU_BLOCKS, LRU_BLOCK_DIM, LRU_BLOCK_DIM), LRU_BLOCK_DIM),
        "lru_bi": bias(ks[10], (L, LRU_WIDTH)),
        "lru_lambda": lam,
        "sgu_ln_g": gain(ks[11], (L, SGU_WIDTH)),
        "sgu_ln_b": bias(ks[12], (L, SGU_WIDTH)),
        "sgu_ws": nrm(ks[13], (L, SGU_GROUPS, CHUNK, CHUNK), CHUNK),
        "sgu_bs": gain(ks[14], (L, SGU_GROUPS, CHUNK)),
        "w_out": nrm(ks[15], (L, D, D), D),
        "ffn_norm": gain(ks[16], (L, D)),
        "router_group_w": nrm(ks[17], (L, D, N_GROUPS), D),
        "router_group_b": bias(ks[18], (L, N_GROUPS)),
        "router_expert_w": nrm(ks[19], (L, D, N_EXPERTS), D),
        "router_expert_b": bias(ks[20], (L, N_EXPERTS)),
        "expert_w1": nrm(ks[21], (L, N_EXPERTS, D, D_EXPERT), D),
        "expert_w3": nrm(ks[22], (L, N_EXPERTS, D, D_EXPERT), D),
        "expert_w2": nrm(ks[23], (L, N_EXPERTS, D_EXPERT, D), D_EXPERT),
        "ple_norm": gain(ks[24], (L, D)),
        "ple_gate_w": nrm(ks[25], (L, D, D), D),
        "ple_up_w": nrm(ks[26], (L, PLE_DIM, D), PLE_DIM),
        "final_norm": gain(ks[27], (D,)),
    }

def reference(x, p, mix_norm, w_in, conv_w, conv_b, lru_wa, lru_ba, lru_wi, lru_bi, lru_lambda,
              sgu_ln_g, sgu_ln_b, sgu_ws, sgu_bs, w_out, ffn_norm, router_group_w, router_group_b,
              router_expert_w, router_expert_b, expert_w1, expert_w3, expert_w2, ple_norm,
              ple_gate_w, ple_up_w, final_norm):
    splits = [LRU_WIDTH, 2 * LRU_WIDTH, 2 * LRU_WIDTH + 2 * SGU_WIDTH]
    for l in range(DEPTH):
        h = rmsnorm(x, mix_norm[l])
        z = h @ w_in[l]
        z_lru, z_gate, z_sgu, z_merge = jnp.split(z, splits, axis=-1)
        xa = causal_depthwise_conv(z_lru, conv_w[l], conv_b[l])
        y_a = rg_lru(xa, lru_wa[l], lru_ba[l], lru_wi[l], lru_bi[l], lru_lambda[l]) * jax.nn.gelu(z_gate)
        y_b = spatial_gating(jax.nn.gelu(z_sgu), sgu_ln_g[l], sgu_ln_b[l], sgu_ws[l], sgu_bs[l])
        m_a, m_b = jnp.split(z_merge, 2, axis=-1)
        merged = jax.nn.sigmoid(m_a) * y_a + jax.nn.sigmoid(m_b) * y_b
        x = x + merged @ w_out[l]
        h = rmsnorm(x, ffn_norm[l])
        x = x + hierarchical_moe(h, router_group_w[l], router_group_b[l], router_expert_w[l],
                                 router_expert_b[l], expert_w1[l], expert_w3[l], expert_w2[l])
        g = jax.nn.sigmoid(rmsnorm(x, ple_norm[l]) @ ple_gate_w[l])
        x = x + g * (p[l] @ ple_up_w[l])
    return rmsnorm(x, final_norm)


_drawn_inputs = setup_inputs


def setup_inputs(seed=0):
    import zlib

    import numpy as np

    out = dict(_drawn_inputs(seed))
    spreads = {}
    factors = {'lru_ba': 64.0,
     'lru_bi': 64.0,
     'sgu_ln_g': 26.92,
     'sgu_ln_b': 48.449,
     'sgu_bs': 19.337,
     'router_group_b': 22.51,
     'router_expert_b': 20.32,
     'ple_norm': 64.0,
     'final_norm': 9.671,
     'conv_b': 6.698,
     'ffn_norm': 5.574}
    for name, (base, spread) in spreads.items():
        noise = np.random.default_rng([zlib.crc32(name.encode()), seed]).standard_normal(out[name].shape)
        drawn = base * np.exp(spread * noise) if base else spread * noise
        out[name] = __import__('jax').numpy.asarray(drawn.astype(out[name].dtype))
    for name, factor in factors.items():
        out[name] = (out[name] * factor).astype(out[name].dtype)
    return out
```

```python
from contextlib import ExitStack

import concourse.bass as bass
from concourse import mybir

F32 = mybir.dt.float32
F32R = mybir.dt.float32r
I32 = mybir.dt.int32
U32 = mybir.dt.uint32
U8 = mybir.dt.uint8
ALU = mybir.AluOpType
ACT = mybir.ActivationFunctionType
AX = mybir.AxisListType

P = 128
KIB = 1024
EPS = 1e-6
LRU_C = 8.0


def hybrid_block_program(nc, A, y_rows, out):
    T, D = A["x"].shape[1:]
    NC = T // P
    NK = D // P
    HALF = D // 2
    PLE = A["p"].shape[3]
    NPK = PLE // P
    E, F = A["expert_w1"].shape[1], A["expert_w1"].shape[3]
    NG = A["router_group_w"].shape[2]
    EG = E // NG
    NR = NG + E
    FC = F // P
    CAP = P // 2
    PAIRS = E // 2
    MAX_JOBS = PAIRS + 2 * T // CAP - 1
    JOBS = MAX_JOBS + 3
    CONV = A["conv_w"].shape[1]
    NB = A["sgu_ws"].shape[1]
    HB = A["lru_wa"].shape[2]
    assert (D, T, NB * P, NC) == (1024, 512, D, 4) and HB * 2 == P and T * 2 == E * 32

    w_in = A["w_in"][0].rearrange("(k p) n -> p k n", p=P)
    w_out = A["w_out"][0].rearrange("(k p) n -> p k n", p=P)
    ple_gate = A["ple_gate_w"][0].rearrange("(k p) n -> p k n", p=P)
    ple_up = A["ple_up_w"][0].rearrange("(k p) n -> p k n", p=P)
    V_COL = 3 * D
    BLOCK_COLS = [0, D, 2 * D, 4 * D, 5 * D]

    PAR = ["mix_norm", "conv_w0", "conv_w1", "conv_w2", "conv_w3", "conv_b", "lru_ba", "lru_bi", "lru_lambda",
           "sgu_ln_g", "sgu_ln_b", "ffn_norm", "ple_norm"]
    pi = {n: i for i, n in enumerate(PAR)}
    N_RAW = len(PAR)
    pi["neg_c"], pi["half_c"] = N_RAW, N_RAW + 1
    N_PAR = N_RAW + 2

    RAW = 5
    N_V, N_BLK = 8, 5
    U_WOUT = N_V + N_BLK * NB
    U_PLE = U_WOUT + 8
    SPLIT = 3
    SPLIT_SLOT = [0, 1, 2, 0, 1]
    SPLIT_AGE = [2, 2, 5, 3, 3]

    ctx = ExitStack()
    with ctx:
        base = nc.sbuf_base
        base += -base % 64
        ARENA = 207 * KIB
        ctx.enter_context(nc.sbuf_tensor("arena", [P, ARENA], U8))

        def at(name, off, shape, dt=F32):
            n = 4
            for s in shape[1:]:
                n *= s
            assert off + n <= ARENA, name
            return nc.alloc_sbuf_tensor_at(name, shape, dt, offset=base + off)

        K = KIB
        x = at("x_res", 0, [P, NC, D])
        raw = [at(f"raw{i}", (16 + 4 * i) * K, [P, D]) for i in range(RAW)]
        w_hi = [at(f"w_hi{i}", (36 + 4 * i) * K, [P, D], F32R) for i in range(SPLIT)]
        w_lo = [at(f"w_lo{i}", (48 + 4 * i) * K, [P, D], F32R) for i in range(SPLIT)]
        hT_hi = at("hT_hi", 108 * K, [P, NK, T], F32R)
        hT_lo = at("hT_lo", 124 * K, [P, NK, T], F32R)
        xn = at("xn", 140 * K, [P, NC, D])
        vm = at("v_then_merged", 140 * K, [P, NB, T])
        o = 156 * K
        tmp = {}
        for n in ["xa", "r", "i", "a", "th", "ga", "gu", "sa", "sb", "s"]:
            tmp[n] = at("t_" + n, o, [P, T])
            o += 2 * K
        z = at("z_lru", o, [P, T + CONV - 1])
        o += 2112
        wa_bd = at("wa_bd", o, [P, NB, P]); o += 4 * K
        wi_bd = at("wi_bd", o, [P, NB, P]); o += 4 * K
        wsT = at("wsT", o, [P, NB, P]); o += 4 * K
        bs_b = at("bs_b", o, [P, NB, P]); o += 4 * K
        rs_b = at("rs_b", o, [P, NB, P]); o += 4 * K
        st_v = at("st_v", o, [P, NC, P]); o += 2 * K
        st_wa = at("st_wa", o, [P, P]); o += 512
        st_wi = at("st_wi", o, [P, P]); o += 512
        st_ws = at("st_ws", o, [P, P]); o += 512
        st_par = at("st_par", o, [P, N_PAR]); o += 64
        ws_raw = at("ws_raw", 160 * K, [P, NB, P])
        par_raw = at("par_raw", 164 * K, [N_RAW * NB, P])
        sq_junk = at("sq_junk", 166 * K, [P, D])
        n2 = at("n2", 36 * K, [P, NC, NK, P])
        junk2 = at("junk2", 52 * K, [P, D])
        h2T = at("h2T", 140 * K, [P, NK, T])
        n2_hi = at("n2_hi", 156 * K, [P, NC, NK, P], F32R)
        n2_lo = at("n2_lo", 172 * K, [P, NC, NK, P], F32R)
        gT = at("gT", 188 * K, [P, NK, P])
        w13 = [[at(f"w13_{s}{e}", (60 + 48 * s + 16 * e) * K, [P, NK, 2, F]) for e in range(2)] for s in range(2)]
        w2 = [at(f"w2_{s}", (92 + 48 * s) * K, [P, 2, FC, D]) for s in range(2)]
        sel = at("sel", 36 * K, [P, NC * 2, CAP], F32R)
        y_sb = at("y_sb", 38 * K, [P, D])
        sil = at("sil", 46 * K, [P, F])
        hid = at("hid", 47 * K, [P, F])
        hidT = at("hidT", 48 * K, [P, FC, P])
        job_cmp = at("job_cmp", 49 * K, [P, JOBS, PAIRS])
        o2 = 192 * K

        def table(name, shape, dt=F32):
            nonlocal o2
            t = at(name, o2, [P] + shape, dt)
            n = 4
            for q in shape:
                n *= q
            o2 += -(-n // 32) * 32
            return t

        w_r = table("w_router", [NK, NR])
        b_r = table("b_router", [NR])
        g2 = table("ffn_norm_cols", [NK])
        upper = table("upper", [P])
        iota_row = table("iota_row", [CAP])
        rank_row = table("rank_row", [EG])
        lg = table("lg", [NC, NR])
        t_g = table("t_g", [NC, NG])
        one_g = table("one_g", [NC, NG])
        t_eg = table("t_eg", [NC, EG, NG])
        es = table("es", [NC, EG])
        es2 = table("es2", [NC, EG])
        t_e = table("t_e", [NC, EG])
        one1 = table("one1", [NC, EG])
        one2 = table("one2", [NC, EG])
        col = table("col", [16, NC])
        M1 = table("M1", [NC, E])
        M2 = table("M2", [NC, E])
        MM = table("MM", [NC, E])
        prod = table("prod", [NC, E])
        posr = table("posr", [PAIRS, NC, 2])
        dstr = table("dstr", [PAIRS, NC, 2])
        dst_st = table("dst_st", [NC, 2], F32R)
        tok_col = table("tok_col", [NC])
        job_row = table("job_row", [JOBS])
        iota_off = table("iota_off", [CAP])
        reps_i = table("reps_i", [PAIRS], I32)
        reps_f = table("reps_f", [PAIRS])
        job_at = table("job_at", [PAIRS + 1])
        job_at_i = table("job_at_i", [PAIRS + 1], I32)
        pair_f = table("pair_f", [JOBS])
        pair_i = table("pair_i", [JOBS], I32)
        job_off = table("job_off", [JOBS])
        row_idx = table("row_idx", [JOBS], U32)
        row_f = table("row_f", [2])
        row_z = table("row_z", [2])
        idx_st = table("idx_st", [1], U32)
        assert o2 <= 201 * K + 512, o2
        yg = [[at(f"yg{c}{t}", (156 + 8 * c + 4 * t) * K, [P, D]) for t in range(2)] for c in range(NC)]
        o_sb = [at(f"o_sb{c}", (156 + 4 * c) * K, [P, D]) for c in range(NC)]
        p_sb = at("p_sb", 60 * K, [P, NC, PLE])
        pT_hi = at("pT_hi", 64 * K, [P, NPK, T], F32R)
        pT_lo = at("pT_lo", 68 * K, [P, NPK, T], F32R)
        n3 = at("n3", 72 * K, [P, NC, D])
        h3 = [at(f"h3_{i}", (88 + 4 * i) * K, [P, NK, P]) for i in range(2)]
        sg = [at(f"sg{i}", (96 + 2 * i) * K, [P, HALF]) for i in range(2)]
        junk3 = at("junk3", 100 * K, [P, D])
        fn_b = at("fn_b", 104 * K, [P, D])
        h3T_hi = at("h3T_hi", 108 * K, [P, NK, T], F32R)
        h3T_lo = at("h3T_lo", 124 * K, [P, NK, T], F32R)
        pu = at("pu", 140 * K, [P, NC, D])
        ident = at("ident", o, [P, P]); o += 512
        ones = at("ones", o, [P, P]); o += 512
        par = at("par", o, [P, N_PAR, NB]); o += 480
        stat = at("stat", o, [P, 64]); o += 256
        sp_t = at("sp_t", o, [P, 6, NB]); o += 192
        bn_s = at("bn_s", o, [P, NC, 2, 6]); o += 192
        bn_m = at("bn_m", o, [P, NC, 2]); o += 32
        assert o <= ARENA, o

        bank = [ctx.enter_context(nc.psum_tensor(f"bank{i}", [P, 512], F32)) for i in range(8)]

        def sem(name):
            return ctx.enter_context(nc.semaphore(name))

        x_loaded = [sem(f"x_loaded{c}") for c in range(NC)]
        par_loaded, ws_loaded, bs_loaded, lruw_loaded = sem("par_loaded"), sem("ws_loaded"), sem("bs_loaded"), sem("lruw_loaded")
        unit_loaded = [sem(f"unit_loaded{i}") for i in range(RAW)]
        stored = sem("stored")
        ident_ready, ones_ready, zeroed, ws_masked = sem("ident_ready"), sem("ones_ready"), sem("zeroed"), sem("ws_masked")
        eps_ready, z_pad_ready = sem("eps_ready"), sem("z_pad_ready")
        par_T, par_ready, ws_T, wsT_ready, rs_done, rs_ready = (sem(n) for n in ["par_T", "par_ready", "ws_T", "wsT_ready", "rs_done", "rs_ready"])
        squares, std_ready, xn_ready, x_T, hT_hi_ready, hT_lo_ready = (sem(n) for n in ["squares", "std_ready", "xn_ready", "x_T", "hT_hi_ready", "hT_lo_ready"])
        hi_split, lo_split, units_done = sem("hi_split"), sem("lo_split"), sem("units_done")
        v_gelu, v_var, v_std, v_normed = sem("v_gelu"), sem("v_var"), sem("v_std"), sem("v_normed")
        c_ready, softplus_abs, softplus_exp = sem("c_ready"), sem("softplus_abs"), sem("softplus_exp")
        staged, staged_v = sem("staged"), sem("staged_v")
        z_copied, conv_done, gates_done, gate_gelu, u_gelu = (sem(n) for n in ["z_copied", "conv_done", "gates_done", "gate_gelu", "u_gelu"])
        ri_sig, tanh_done, ma_sig, decay_ready, root_ready, mb_sig = (sem(n) for n in ["ri_sig", "tanh_done", "ma_sig", "decay_ready", "root_ready", "mb_sig"])
        sgu_done, sp_evac, sp_params, merged_done = sem("sgu_done"), sem("sp_evac"), sem("sp_params"), sem("merged_done")
        y_free = sem("y_free")
        dve_chain, sp_passed, pool_passed = sem("dve_chain"), sem("sp_passed"), sem("pool_passed")
        wout_done, x1_half = sem("wout_done"), sem("x1_half")
        squares2, std2_ready, n2_ready, n2_hi_ready, n2_lo_ready, n2_T, h2T_ready, router_done = (sem(n) for n in [
            "squares2", "std2_ready", "n2_ready", "n2_hi_ready", "n2_lo_ready", "n2_T", "h2T_ready", "router_done"])
        router_loaded, tables_ready, group_shift, group_exp, second_shift, second_exp = (sem(n) for n in [
            "router_loaded", "tables_ready", "group_shift", "group_exp", "second_shift", "second_exp"])
        masks_ready, pos_done, jobs_ready = sem("masks_ready"), sem("pos_done"), sem("jobs_ready")
        w13_loaded = [[sem(f"w13_loaded{s}{e}") for e in range(2)] for s in range(2)]
        w2_loaded = [sem(f"w2_loaded{s}") for s in range(2)]
        sel_ready, gather_done, gT_ready, up_done, silu_done, hid_ready, hidT_done, hidT_ready = (sem(n) for n in [
            "sel_ready", "gather_done", "gT_ready", "up_done", "silu_done", "hid_ready", "hidT_done", "hidT_ready"])
        down0_done, down1_done, y0_ready, y1_ready = sem("down0_done"), sem("down1_done"), sem("y0_ready"), sem("y1_ready")
        y_stored, idx_ready, idx_staged, off_ready, row_z_ready = (sem(n) for n in [
            "y_stored", "idx_ready", "idx_staged", "off_ready", "row_z_ready"])
        yg_loaded = [sem(f"yg_loaded{c}") for c in range(NC)]
        p_loaded, fn_loaded, p_T, pT_hi_ready, pT_lo_ready, pu_ready = (sem(n) for n in [
            "p_loaded", "fn_loaded", "p_T", "pT_hi_ready", "pT_lo_ready", "pu_ready"])
        x2_ready, squares3, std3_ready, n3_ready, n3_T, h3_ready, h3T_hi_ready, h3T_lo_ready = (sem(n) for n in [
            "x2_ready", "squares3", "std3_ready", "n3_ready", "n3_T", "h3_ready", "h3T_hi_ready", "h3T_lo_ready"])
        ple_units_done, gate_sig, x3_ready, squares4, std4_ready, out_ready = (sem(n) for n in [
            "ple_units_done", "gate_sig", "x3_ready", "squares4", "std4_ready", "out_ready"])

        def raw_view(n_or_slot):
            return raw[n_or_slot]

        def split_slot(n):
            return n % SPLIT if n < N_V else SPLIT_SLOT[(n - N_V) % N_BLK]

        START = 1
        started = [gates_done, root_ready, sp_params, sgu_done, conv_done, merged_done, z_copied, gate_gelu, u_gelu,
                   ma_sig, mb_sig, ri_sig, sp_evac, y_free, hid_ready, hidT_done, hidT_ready, y0_ready, y1_ready]

        block = ctx.enter_context(nc.Block())

        def loads_of(n):
            return 16 * (n // RAW + 1)

        N_PLE = 10

        @block.sync
        def _(sp):
            def load_ple(i):
                n = U_PLE + i
                if i >= RAW:
                    sp.wait_ge(lo_split, U_WOUT + i - RAW + 1)
                if i < 2:
                    src = ple_up[:, :, HALF * i:HALF * (i + 1)]
                else:
                    j, q = (i - 2) // 4, (i - 2) % 4
                    src = ple_gate[:, 2 * q:2 * q + 2, HALF * j:HALF * (j + 1)]
                sp.dma_start(raw[n % RAW][:].rearrange("p (k n) -> p k n", k=2), src).then_inc(unit_loaded[n % RAW], 16)

            for c in range(NC):
                sp.dma_start(x[:, c, :], A["x"][0, c * P:(c + 1) * P, :]).then_inc(x_loaded[c], 16)
            for n in range(N_V):
                j, q = n // 4, n % 4
                if n >= RAW:
                    sp.wait_ge(lo_split, n - RAW + 1)
                src = w_in[:, 2 * q:2 * q + 2, V_COL + HALF * j:V_COL + HALF * (j + 1)]
                sp.dma_start(raw[n % RAW][:].rearrange("p (k n) -> p k n", k=2), src).then_inc(unit_loaded[n % RAW], 16)
            with sp.Fori(0, NB) as b:
                for j in range(N_BLK):
                    n = N_V + j
                    sp.wait_ge(lo_split, b * N_BLK + (n - RAW + 1))
                    src = w_in[:, :, bass.ds(b * P + BLOCK_COLS[j], P)]
                    sp.dma_start(raw[n % RAW][:].rearrange("p (k n) -> p k n", k=NK), src).then_inc(unit_loaded[n % RAW], 16)
            for i in range(8):
                n = U_WOUT + i
                j, q = i // 4, i % 4
                if n - RAW < U_WOUT:
                    sp.wait_ge(lo_split, n - RAW + 1)
                else:
                    sp.wait_ge(units_done, n - RAW + 1)
                src = w_out[:, 2 * q:2 * q + 2, HALF * j:HALF * (j + 1)]
                sp.dma_start(raw[n % RAW][:].rearrange("p (k n) -> p k n", k=2), src).then_inc(unit_loaded[n % RAW], 16)

            def load_up(s, e, expert):
                for m, w in enumerate(("expert_w1", "expert_w3")):
                    src = A[w][0, expert].rearrange("a (p k) f -> p k (a f)", k=NK)
                    sp.dma_start(w13[s][e][:, :, m, :], src).then_inc(w13_loaded[s][e], 16)

            def load_down(s, first):
                for e in range(2):
                    src = A["expert_w2"][0, bass.ds(first + e, 1)].rearrange("a (c p) n -> p c (a n)", p=P)
                    sp.dma_start(w2[s][:, e, :, :], src).then_inc(w2_loaded[s], 16)

            def load_pair(s, first, up_free, down_free):
                if up_free is not None:
                    sp.wait_ge(up_done, up_free)
                for e in range(2):
                    load_up(s, e, bass.ds(first + e, 1))
                if down_free is not None:
                    sp.wait_ge(down1_done, down_free)
                load_down(s, first)

            load_pair(0, 0, None, None)
            sp.wait_ge(units_done, U_WOUT)
            for e in range(2):
                load_up(1, e, bass.ds(2 + e, 1))
            sp.wait_ge(router_done, NC)
            load_down(1, 2)
            sp.wait_ge(wout_done, NC)
            for i in range(RAW):
                load_ple(i)
            sp.wait_ge(jobs_ready, 1)
            with sp.Fori(0, PAIRS // 2 - 1) as h:
                for s in range(2):
                    end = sp.value_load(job_at_i[0:1, bass.ds(h * 2 + (s + 1), 1)], min_val=1, max_val=MAX_JOBS)
                    load_pair(s, h * 4 + (4 + 2 * s), end, end)
            jobs = sp.value_load(job_at_i[0:1, PAIRS:PAIRS + 1], min_val=PAIRS, max_val=MAX_JOBS)
            sp.wait_ge(up_done, jobs)
            sp.dma_start(p_sb[:], A["p"][0, 0].rearrange("(c p) n -> p c n", p=P)).then_inc(p_loaded, 16)
            sp.wait_ge(gather_done, jobs + 1)
            sp.sem_inc(sp_passed, 1)
            sp.wait_ge(y_stored, jobs * 16)
            for c in range(NC):
                for t in range(2):
                    sp.dma_start(yg[c][t][:], y_rows[T * t + P * c:T * t + P * (c + 1), :]).then_inc(yg_loaded[c], 16)
            sp.dma_start(fn_b[:], A["final_norm"][None, :].broadcast_to((P, D))).then_inc(fn_loaded, 16)
            for i in range(RAW, N_PLE):
                load_ple(i)
            for c in range(NC):
                sp.wait_ge(out_ready, c + 1)
                sp.dma_start(out[0, c * P:(c + 1) * P, :], o_sb[c][:]).then_inc(stored, 16)
            sp.wait_ge(stored, 16 * NC)

        @block.gpsimd
        def _(pool):
            for s in started:
                pool.sem_inc(s, START)
            nc.gpsimd.memset(ident[:], 0.0).then_inc(zeroed, 1)
            nc.gpsimd.memset(ones[:], 1.0).then_inc(ones_ready, 1)
            nc.gpsimd.memset(stat[:, 0:1], EPS).then_inc(eps_ready, 1)
            pool.wait_ge(zeroed, 1)
            nc.gpsimd.affine_select(out=ident[:], in_=ident[:], compare_op=ALU.not_equal, fill=1.0, base=0,
                                    pattern=[[-1, P]], channel_multiplier=1).then_inc(ident_ready, 1)
            nc.gpsimd.memset(wa_bd[:], 0.0).then_inc(zeroed, 1)
            nc.gpsimd.memset(wi_bd[:], 0.0).then_inc(zeroed, 1)
            pool.wait_ge(zeroed, 3)
            for dst, src in ((wa_bd, A["lru_wa"]), (wi_bd, A["lru_wi"])):
                w = src[0].rearrange("(b two) i j -> two i b j", two=2)
                for h in range(2):
                    pool.dma_start(dst[h * HB:(h + 1) * HB, :, h * HB:(h + 1) * HB], w[h]).then_inc(lruw_loaded, 16)
            pool.wait_ge(ws_loaded, 16)
            nc.gpsimd.affine_select(out=ws_raw[:], in_=ws_raw[:], compare_op=ALU.is_ge, fill=0.0, base=0,
                                    pattern=[[0, NB], [-1, P]], channel_multiplier=1).then_inc(ws_masked, 1)
            nc.gpsimd.memset(z[:, 0:CONV - 1], 0.0).then_inc(z_pad_ready, 1)
            pool.wait_ge(c_ready, 1)
            pool.wait_ge(lruw_loaded, 64)
            pool.wait_ge(wsT_ready, 2)
            with pool.Fori(0, NB) as b:
                pool.wait_ge(gates_done, b + START)
                pool.wait_ge(root_ready, b + START)
                pool.wait_ge(sp_params, b + START)
                nc.gpsimd.tensor_copy(st_par[:], par[:, :, bass.ds(b, 1)].rearrange("p a b -> p (a b)")).then_inc(staged, 1)
                nc.gpsimd.tensor_copy(st_wa[:], wa_bd[:, bass.ds(b, 1), :].rearrange("p a b -> p (a b)")).then_inc(staged, 1)
                nc.gpsimd.tensor_copy(st_wi[:], wi_bd[:, bass.ds(b, 1), :].rearrange("p a b -> p (a b)")).then_inc(staged, 1)
                pool.wait_ge(sgu_done, b + START)
                pool.wait_ge(v_normed, NC)
                nc.gpsimd.tensor_copy(st_ws[:], wsT[:, bass.ds(b, 1), :].rearrange("p a b -> p (a b)")).then_inc(staged_v, 1)
                nc.gpsimd.tensor_copy(st_v[:].rearrange("p c n -> p (c n)"),
                                      vm[:, bass.ds(b, 1), :].rearrange("p a b -> p (a b)")).then_inc(staged_v, 1)

            pool.wait_ge(merged_done, NB + START)
            pool.dma_start(w_r[:, :, 0:NG], A["router_group_w"][0].rearrange("(p k) n -> p k n", k=NK)).then_inc(router_loaded, 16)
            pool.dma_start(w_r[:, :, NG:NR], A["router_expert_w"][0].rearrange("(p k) n -> p k n", k=NK)).then_inc(router_loaded, 16)
            pool.dma_start(b_r[:, 0:NG], A["router_group_b"].broadcast_to((P, NG))).then_inc(router_loaded, 16)
            pool.dma_start(b_r[:, NG:NR], A["router_expert_b"].broadcast_to((P, E))).then_inc(router_loaded, 16)
            pool.dma_start(g2[:], A["ffn_norm"][0].rearrange("(p k) -> p k", k=NK)).then_inc(router_loaded, 16)
            nc.gpsimd.memset(upper[:], 1.0).then_inc(zeroed, 1)
            nc.gpsimd.iota(tok_col[:], [[P, NC]], base=1, channel_multiplier=1,
                           allow_small_or_imprecise_dtypes=True).then_inc(tables_ready, 1)
            nc.gpsimd.iota(iota_row[:], [[1, CAP]], base=0, channel_multiplier=0,
                           allow_small_or_imprecise_dtypes=True).then_inc(tables_ready, 1)
            nc.gpsimd.iota(rank_row[:], [[-1, EG]], base=EG, channel_multiplier=0,
                           allow_small_or_imprecise_dtypes=True).then_inc(tables_ready, 1)
            nc.gpsimd.iota(job_row[:], [[1, JOBS]], base=0, channel_multiplier=0,
                           allow_small_or_imprecise_dtypes=True).then_inc(tables_ready, 1)
            pool.wait_ge(zeroed, 4)
            nc.gpsimd.affine_select(out=upper[:], in_=upper[:], compare_op=ALU.is_gt, fill=0.0, base=0,
                                    pattern=[[1, P]], channel_multiplier=-1).then_inc(tables_ready, 1)
            pool.wait_ge(jobs_ready, 1)
            jobs = pool.value_load(job_at_i[0:1, PAIRS:PAIRS + 1], min_val=PAIRS, max_val=MAX_JOBS)
            last_row = pool.to_reg(2 * T - 1)
            with pool.Fori(0, jobs) as g:
                pool.wait_ge(idx_ready, g * 2 + 2)
                nc.gpsimd.tensor_copy(idx_st[:], row_idx[:, bass.ds(g, 1)]).then_inc(idx_staged, 1)
                pool.wait_ge(idx_staged, g + 1)
                pool.wait_ge(y0_ready, g + 1 + START)
                pool.wait_ge(y1_ready, g + 1 + START)
                pool.sem_inc(pool_passed, 1)
                pool.indirect_dma_start(out=y_rows[:, :], out_offset=bass.IndirectOffsetOnAxis(ap=idx_st[:, 0:1], axis=0),
                                        in_=y_sb[:], in_offset=None, bounds_check=last_row,
                                        oob_is_err=False).then_inc(y_stored, 16)
                pool.wait_ge(y_stored, g * 16 + 16)
                pool.sem_inc(y_free, 1)

        @block.scalar
        def _(act):
            for i, n in enumerate(PAR):
                src = A["conv_w"][0, int(n[-1])] if n.startswith("conv_w") else A[n][0]
                act.dma_start(par_raw[i * NB:(i + 1) * NB, :], src.rearrange("(b c) -> b c", c=P)).then_inc(par_loaded, 16)
            act.dma_start(ws_raw[:], A["sgu_ws"][0].rearrange("g t s -> t g s")).then_inc(ws_loaded, 16)
            act.dma_start(bs_b[:].rearrange("p g t -> p (g t)"),
                          A["sgu_bs"][0].rearrange("g t -> (g t)")[None, :].broadcast_to((P, NB * P))).then_inc(bs_loaded, 16)

            def split_high(n, slot, count, free_after):
                act.wait_ge(unit_loaded[slot[0]], count)
                if free_after is not None:
                    act.wait_ge(units_done, free_after)
                nc.scalar.activation(w_hi[slot[1]][:], raw[slot[0]][:], ACT.Copy).then_inc(hi_split, 1)

            def split_high_v(n):
                age = SPLIT if n <= N_V else None
                free = n - 2 if n >= SPLIT else None
                if n == N_V:
                    free = n - 1
                split_high(n, (n % RAW, split_slot(n)), loads_of(n), free)

            for c in range(NC):
                act.wait_ge(x_loaded[c], 16)
                if c > 0:
                    act.wait_ge(squares, c)
                nc.scalar.activation(sq_junk[:], x[:, c, :], ACT.Square, accum_out=stat[:, 4 + c:5 + c]).then_inc(squares, 1)
                if c == 0:
                    act.wait_ge(eps_ready, 1)
                act.wait_ge(squares, c + 1)
                nc.scalar.activation(stat[:, 8 + c:9 + c], stat[:, 4 + c:5 + c], ACT.Sqrt, bias=stat[:, 0:1],
                                     scale=1.0 / D).then_inc(std_ready, 1)
            for n in range(SPLIT):
                split_high_v(n)
            act.wait_ge(x_T, NC)
            act.wait_ge(par_ready, 1)
            for k in range(NK):
                nc.scalar.activation(hT_hi[:, k, :], bank[k][:], ACT.Copy,
                                     scale=par[:, pi["mix_norm"], k:k + 1]).then_inc(hT_hi_ready, 1)

            def gelu_v(j):
                act.wait_ge(units_done, 4 * (j + 1))
                for c in range(NC):
                    dst = vm[:, 4 * j:4 * j + 4, c * P:(c + 1) * P]
                    nc.scalar.activation(dst, bank[4 * j + c][:].rearrange("p (g n) -> p g n", n=P),
                                         ACT.Gelu_apprx_tanh).then_inc(v_gelu, 1)

            split_high_v(3)
            split_high_v(4)
            split_high_v(5)
            gelu_v(0)
            split_high_v(6)
            split_high_v(7)
            split_high_v(8)
            gelu_v(1)
            lam = par[:, pi["lru_lambda"], :]
            nc.scalar.activation(sp_t[:, 0, :], lam, ACT.Abs).then_inc(softplus_abs, 1)
            act.wait_ge(softplus_abs, 1)
            nc.scalar.activation(sp_t[:, 1, :], sp_t[:, 0, :], ACT.Exp, scale=-1.0).then_inc(softplus_exp, 1)
            act.wait_ge(v_var, NC)
            nc.scalar.activation(stat[:, 16:16 + NC], bn_m[:, :, 1], ACT.Sqrt, bias=stat[:, 0:1]).then_inc(v_std, 1)

            def channel_block(b, last):
                u0 = b * N_BLK + N_V

                def high(j):
                    m = N_V + j
                    act.wait_ge(unit_loaded[m % RAW], b * 16 + loads_of(m))
                    act.wait_ge(units_done, u0 + (j - SPLIT_AGE[j % N_BLK] + 1))
                    nc.scalar.activation(w_hi[SPLIT_SLOT[j % N_BLK]][:], raw[m % RAW][:], ACT.Copy).then_inc(hi_split, 1)

                def par_of(n):
                    return st_par[:, pi[n]:pi[n] + 1]

                high(1)
                act.wait_ge(units_done, u0 + 1)
                act.wait_ge(conv_done, b + START)
                nc.scalar.activation(z[:, CONV - 1:], bank[0][:], ACT.Copy).then_inc(z_copied, 1)
                high(2)
                act.wait_ge(units_done, u0 + 2)
                act.wait_ge(merged_done, b + START)
                nc.scalar.activation(tmp["ga"][:], bank[1][:], ACT.Gelu_apprx_tanh).then_inc(gate_gelu, 1)
                high(3)
                act.wait_ge(units_done, u0 + 3)
                nc.scalar.activation(tmp["gu"][:], bank[2][:], ACT.Gelu_apprx_tanh).then_inc(u_gelu, 1)
                high(4)
                act.wait_ge(staged, b * 3 + 3)
                act.wait_ge(gates_done, b + 1 + START)
                nc.scalar.activation(tmp["r"][:], bank[5][:], ACT.Sigmoid, bias=par_of("lru_ba")).then_inc(ri_sig, 1)
                nc.scalar.activation(tmp["i"][:], bank[6][:], ACT.Sigmoid, bias=par_of("lru_bi")).then_inc(ri_sig, 1)
                act.wait_ge(ri_sig, b * 2 + 1 + START)
                nc.scalar.activation(tmp["th"][:], tmp["r"][:], ACT.Tanh, scale=par_of("half_c")).then_inc(tanh_done, 1)
                act.wait_ge(units_done, u0 + 4)
                nc.scalar.activation(tmp["sa"][:], bank[3][:], ACT.Sigmoid).then_inc(ma_sig, 1)
                if not last:
                    high(5)
                nc.scalar.activation(tmp["a"][:], tmp["r"][:], ACT.Exp, scale=par_of("neg_c")).then_inc(decay_ready, 1)
                act.wait_ge(tanh_done, b + 1)
                nc.scalar.activation(tmp["th"][:], tmp["th"][:], ACT.Sqrt).then_inc(root_ready, 1)
                act.wait_ge(units_done, u0 + 5)
                nc.scalar.activation(tmp["sb"][:], bank[4][:], ACT.Sigmoid).then_inc(mb_sig, 1)

            act.wait_ge(z_pad_ready, 1)
            with act.Fori(0, NB - 1) as b:
                channel_block(b, False)
            channel_block(NB - 1, True)

            for c in range(NC):
                act.wait_ge(x1_half, NC + c + 1)
                if c > 0:
                    act.wait_ge(squares2, c)
                nc.scalar.activation(junk2[:], x[:, c, :], ACT.Square, accum_out=stat[:, 24 + c:25 + c]).then_inc(squares2, 1)
                act.wait_ge(squares2, c + 1)
                nc.scalar.activation(stat[:, 28 + c:29 + c], stat[:, 24 + c:25 + c], ACT.Sqrt, bias=stat[:, 0:1],
                                     scale=1.0 / D).then_inc(std2_ready, 1)
                act.wait_ge(n2_ready, c + 1)
                nc.scalar.activation(n2_hi[:, c, :, :], n2[:, c, :, :], ACT.Copy).then_inc(n2_hi_ready, 1)
            act.wait_ge(group_shift, 1)
            nc.scalar.activation(t_g[:], t_g[:], ACT.Exp).then_inc(group_exp, 1)
            act.wait_ge(second_shift, 1)
            nc.scalar.activation(col[:, 5, :], col[:, 4, :], ACT.Exp).then_inc(second_exp, 1)
            act.wait_ge(jobs_ready, 1)
            jobs = act.value_load(job_at_i[0:1, PAIRS:PAIRS + 1], min_val=PAIRS, max_val=MAX_JOBS)
            with act.Fori(0, jobs) as g:
                act.wait_ge(up_done, g + 1)
                act.wait_ge(hid_ready, g + START)
                nc.scalar.activation(sil[:], bank[0][:, 0:F], ACT.Silu).then_inc(silu_done, 1)
                act.wait_ge(hidT_done, g + 1 + START)
                nc.scalar.activation(hidT[:].rearrange("p c n -> p (c n)"), bank[3][:, 0:F], ACT.Copy).then_inc(hidT_ready, 1)
                act.wait_ge(down0_done, g + 1)
                act.wait_ge(y_free, g + START)
                nc.scalar.activation(y_sb[:, 0:HALF], bank[6][:], ACT.Copy).then_inc(y0_ready, 1)

            def split_high_ple(i):
                n = U_PLE + i
                act.wait_ge(unit_loaded[n % RAW], loads_of(n))
                if i >= SPLIT:
                    act.wait_ge(ple_units_done, i - SPLIT + 1)
                nc.scalar.activation(w_hi[i % SPLIT][:], raw[n % RAW][:], ACT.Copy).then_inc(hi_split, 1)

            act.wait_ge(y_free, jobs + START)
            for i in range(SPLIT):
                split_high_ple(i)
            act.wait_ge(p_T, 1)
            for k in range(NPK):
                nc.scalar.activation(pT_hi[:, k, :], bank[4 + k][:], ACT.Copy).then_inc(pT_hi_ready, 1)
            for c in range(NC):
                act.wait_ge(x2_ready, c + 1)
                if c > 0:
                    act.wait_ge(squares3, c)
                nc.scalar.activation(junk3[:], x[:, c, :], ACT.Square, accum_out=stat[:, 36 + c:37 + c]).then_inc(squares3, 1)
                act.wait_ge(squares3, c + 1)
                nc.scalar.activation(stat[:, 40 + c:41 + c], stat[:, 36 + c:37 + c], ACT.Sqrt, bias=stat[:, 0:1],
                                     scale=1.0 / D).then_inc(std3_ready, 1)
                if c < 2:
                    split_high_ple(SPLIT + c)
                act.wait_ge(h3_ready, 2 * c + 2)
                nc.scalar.activation(h3T_hi[:, :, c * P:(c + 1) * P], h3[c % 2][:], ACT.Copy).then_inc(h3T_hi_ready, 1)
            for i in range(SPLIT + 2, N_PLE):
                split_high_ple(i)
                if i == 7:
                    act.wait_ge(ple_units_done, 6)
                    for c in range(NC):
                        if c >= 2:
                            act.wait_ge(x3_ready, c - 1)
                        nc.scalar.activation(sg[c % 2][:], bank[c][:], ACT.Sigmoid).then_inc(gate_sig, 1)
            act.wait_ge(ple_units_done, N_PLE)
            for c in range(NC):
                act.wait_ge(x3_ready, c + 3)
                nc.scalar.activation(sg[c % 2][:], bank[4 + c][:], ACT.Sigmoid).then_inc(gate_sig, 1)
                if c > 0:
                    act.wait_ge(x3_ready, NC + c)
                    nc.scalar.activation(junk3[:], x[:, c - 1, :], ACT.Square, accum_out=stat[:, 43 + c:44 + c]).then_inc(squares4, 1)
                    act.wait_ge(squares4, c)
            act.wait_ge(x3_ready, 2 * NC)
            nc.scalar.activation(junk3[:], x[:, NC - 1, :], ACT.Square, accum_out=stat[:, 47:48]).then_inc(squares4, 1)
            act.wait_ge(squares4, NC)
            nc.scalar.activation(stat[:, 48:48 + NC], stat[:, 44:44 + NC], ACT.Sqrt, bias=stat[:, 0:1],
                                 scale=1.0 / D).then_inc(std4_ready, 1)

        @block.vector
        def _(dve):
            chain = [0]

            def link(ins):
                ins.then_inc(dve_chain, 1)
                chain[0] = chain[0] + 1
                dve.wait_ge(dve_chain, chain[0])

            tt, ts, stt = nc.vector.tensor_tensor, nc.vector.tensor_scalar, nc.vector.scalar_tensor_tensor
            for c in range(NC):
                dve.wait_ge(std_ready, c + 1)
                link(nc.vector.reciprocal(stat[:, 12 + c:13 + c], stat[:, 8 + c:9 + c]))
                ts(xn[:, c, :], x[:, c, :], stat[:, 12 + c:13 + c], None, ALU.mult).then_inc(xn_ready, 1)
                if c == 0:
                    dve.wait_ge(par_T, 1)
                    nc.vector.tensor_copy(par[:, 0:N_RAW, :].rearrange("p a b -> p (a b)"),
                                          bank[7][:, 0:N_RAW * NB]).then_inc(par_ready, 1)
            for h in range(2):
                dve.wait_ge(ws_T, h + 1)
                nc.vector.tensor_copy(wsT[:, 4 * h:4 * h + 4, :].rearrange("p a b -> p (a b)"), bank[h][:]).then_inc(wsT_ready, 1)
            for h in range(2):
                dve.wait_ge(rs_done, h + 1)
                nc.vector.tensor_copy(rs_b[:, 4 * h:4 * h + 4, :].rearrange("p a b -> p (a b)"), bank[2 + h][:]).then_inc(rs_ready, 1)

            def split_low(slot, n_hi):
                dve.wait_ge(hi_split, n_hi)
                tt(w_lo[slot[1]][:], raw[slot[0]][:], w_hi[slot[1]][:].bitcast(F32), ALU.subtract).then_inc(lo_split, 1)

            def split_low_v(n):
                split_low((n % RAW, split_slot(n)), n + 1)

            for n in range(SPLIT):
                split_low_v(n)
            for k in range(NK):
                dve.wait_ge(hT_hi_ready, k + 1)
                stt(hT_lo[:, k, :], bank[k][:], par[:, pi["mix_norm"], k:k + 1], hT_hi[:, k, :].bitcast(F32),
                    ALU.mult, ALU.subtract).then_inc(hT_lo_ready, 1)
            for n in range(3, N_V + 1):
                split_low_v(n)
            dve.wait_ge(v_gelu, 2 * NC)
            for c in range(NC):
                for h in range(2):
                    nc.vector.bn_stats(bn_s[:, c, h, :], vm[:, 4 * h:4 * h + 4, c * P:(c + 1) * P]).then_inc(dve_chain, 1)
                chain[0] += 2
                dve.wait_ge(dve_chain, chain[0])
                nc.vector.bn_aggr(bn_m[:, c, :], bn_s[:, c, :, :].rearrange("p h s -> p (h s)")).then_inc(v_var, 1)
            dve.wait_ge(v_std, 1)
            link(nc.vector.reciprocal(stat[:, 20:20 + NC], stat[:, 16:16 + NC]))
            for c in range(NC):
                vc = vm[:, :, c * P:(c + 1) * P]
                ts(vc, vc, bn_m[:, c, 0:1], stat[:, 20 + c:21 + c], ALU.subtract, ALU.mult).then_inc(v_normed, 1)
            dve.wait_ge(softplus_exp, 1)
            dve.wait_ge(par_ready, 1)
            e, s_, s2, q = sp_t[:, 1, :], sp_t[:, 2, :], sp_t[:, 3, :], sp_t[:, 4, :]
            link(ts(s_, e, 2.0, None, ALU.add))
            link(nc.vector.reciprocal(s_, s_))
            link(tt(s_, s_, e, ALU.mult))
            link(tt(s2, s_, s_, ALU.mult))
            link(ts(q, s2, 1.0 / 17, None, ALU.mult))
            for odd in (15, 13, 11, 9, 7, 5, 3):
                link(stt(q, q, 1.0 / odd, s2, ALU.add, ALU.mult))
            link(stt(q, q, 1.0, s_, ALU.add, ALU.mult))
            link(ts(s_, par[:, pi["lru_lambda"], :], -1.0, 0.0, ALU.mult, ALU.max))
            link(stt(q, q, 2.0, s_, ALU.mult, ALU.add))
            link(ts(par[:, pi["neg_c"], :], q, -LRU_C, None, ALU.mult))
            ts(par[:, pi["half_c"], :], q, LRU_C / 2, None, ALU.mult).then_inc(c_ready, 1)

            before = chain[0]
            LINKS = 11

            def channel_block(b, last):
                u0 = b * N_BLK + N_V
                chain[0] = b * LINKS + before

                def low(j):
                    m = N_V + j
                    split_low((m % RAW, SPLIT_SLOT[j % N_BLK]), u0 + (j + 1))

                def par_of(n):
                    return st_par[:, pi[n]:pi[n] + 1]

                xa, th, s = tmp["xa"], tmp["th"], tmp["s"]
                low(1)
                dve.wait_ge(staged, b * 3 + 1)
                dve.wait_ge(z_copied, b + 1 + START)
                dve.wait_ge(merged_done, b + START)
                link(ts(xa[:], z[:, CONV - 1:], par_of(f"conv_w{CONV - 1}"), par_of("conv_b"), ALU.mult, ALU.add))
                for t in (CONV - 2, CONV - 3):
                    link(stt(xa[:], z[:, t:t + T], par_of(f"conv_w{t}"), xa[:], ALU.mult, ALU.add))
                stt(xa[:], z[:, 0:T], par_of("conv_w0"), xa[:], ALU.mult, ALU.add).then_inc(conv_done, 1)
                low(2)
                low(3)
                low(4)
                dve.wait_ge(ri_sig, b * 2 + 2 + START)
                link(tt(tmp["i"][:], tmp["i"][:], xa[:], ALU.mult))
                dve.wait_ge(sgu_done, b + 1 + START)
                cb = lambda w: w[:, bass.ds(b, 1), :].broadcast_to((P, NC, P))
                s3 = s[:].rearrange("p (c n) -> p c n", c=NC)
                ins = stt(s3, bank[7][:].rearrange("p (c n) -> p c n", c=NC), par_of("sgu_ln_g"), cb(bs_b), ALU.mult, ALU.add)
                ins.then_inc(sp_evac, 1)
                dve.wait_ge(sp_evac, b + 1 + START)
                ins = stt(s3, cb(rs_b), par_of("sgu_ln_b"), s3, ALU.mult, ALU.add)
                ins.then_inc(sp_params, 1)
                dve.wait_ge(sp_params, b + 1 + START)
                dve.wait_ge(u_gelu, b + 1 + START)
                link(tt(s[:], s[:], tmp["gu"][:], ALU.mult))
                if not last:
                    low(5)
                dve.wait_ge(decay_ready, b + 1)
                dve.wait_ge(root_ready, b + 1 + START)
                link(stt(th[:], tmp["a"][:], 1.0, th[:], ALU.add, ALU.mult))
                link(tt(th[:], th[:], tmp["i"][:], ALU.mult))
                link(nc.vector.tensor_tensor_scan(xa[:], tmp["a"][:], th[:], 0.0, ALU.mult, ALU.add))
                link(tt(xa[:], xa[:], tmp["ga"][:], ALU.mult))
                link(tt(xa[:], xa[:], tmp["sa"][:], ALU.mult))
                dve.wait_ge(mb_sig, b + 1 + START)
                link(tt(s[:], s[:], tmp["sb"][:], ALU.mult))
                tt(vm[:, bass.ds(b, 1), :].rearrange("p a b -> p (a b)"), xa[:], s[:], ALU.add).then_inc(merged_done, 1)
                if isinstance(b, int):
                    assert chain[0] == b * LINKS + before + LINKS, chain[0] - before - b * LINKS

            def second_norm(c):
                dve.wait_ge(std2_ready, c + 1)
                link(nc.vector.reciprocal(stat[:, 32 + c:33 + c], stat[:, 28 + c:29 + c]))
                ts(n2[:, c, :, :], x[:, c, :].rearrange("t (p k) -> t k p", k=NK), stat[:, 32 + c:33 + c], None,
                   ALU.mult).then_inc(n2_ready, 1)
                dve.wait_ge(n2_hi_ready, c + 1)
                tt(n2_lo[:, c, :, :], n2[:, c, :, :], n2_hi[:, c, :, :].bitcast(F32), ALU.subtract).then_inc(n2_lo_ready, 1)
                dve.wait_ge(n2_T, c + 1)
                if c == 0:
                    dve.wait_ge(router_loaded, 16 * 5)
                    dve.wait_ge(tables_ready, 5)
                if c == NC - 1 or True:
                    for h in range(2):
                        src = bank[2 * (c % 2) + h][:].rearrange("p (k t) -> p k t", k=4)
                        tt(h2T[:, 4 * h:4 * h + 4, c * P:(c + 1) * P], src,
                           g2[:, 4 * h:4 * h + 4].unsqueeze(2).broadcast_to((P, 4, P)), ALU.mult).then_inc(h2T_ready, 1)

            def first_of(one, score, top, ranks, v, vmax, n):
                bc = lambda a: a.unsqueeze(2).broadcast_to((P, NC, n))
                link(tt(score, v, bc(vmax), ALU.is_equal))
                link(tt(score, score, ranks.unsqueeze(1).broadcast_to((P, NC, n)), ALU.mult))
                link(nc.vector.tensor_reduce(top, score, axis=AX.X, op=ALU.max))
                link(tt(one, score, bc(top), ALU.is_equal))

            def route():
                red = nc.vector.tensor_reduce
                dve.wait_ge(router_done, NC)
                link(tt(lg[:], bank[4][:, 0:NC * NR].rearrange("p (c n) -> p c n", c=NC),
                        b_r[:].unsqueeze(1).broadcast_to((P, NC, NR)), ALU.add))
                gl = lg[:, :, 0:NG]
                link(red(col[:, 0, :], gl, axis=AX.X, op=ALU.max))
                tt(t_g[:], gl, col[:, 0, :].unsqueeze(2).broadcast_to((P, NC, NG)), ALU.subtract).then_inc(group_shift, 1)
                first_of(one_g[:], t_eg[:, :, 0, :], col[:, 1, :], rank_row[:, EG - NG:EG], gl, col[:, 0, :], NG)
                link(tt(t_eg[:], lg[:, :, NG:NR].rearrange("p c (g e) -> p c e g", g=NG),
                        one_g[:].unsqueeze(2).broadcast_to((P, NC, EG, NG)), ALU.mult))
                link(red(es[:], t_eg[:], axis=AX.X, op=ALU.add))
                link(red(col[:, 2, :], es[:], axis=AX.X, op=ALU.max))
                first_of(one1[:], t_e[:], col[:, 1, :], rank_row[:], es[:], col[:, 2, :], EG)
                link(stt(es2[:], one1[:], -1e30, es[:], ALU.mult, ALU.add))
                link(red(col[:, 3, :], es2[:], axis=AX.X, op=ALU.max))
                tt(col[:, 4, :], col[:, 3, :], col[:, 2, :], ALU.subtract).then_inc(second_shift, 1)
                first_of(one2[:], t_e[:], col[:, 1, :], rank_row[:], es2[:], col[:, 3, :], EG)
                for one, M in ((one1, M1), (one2, M2)):
                    link(tt(M[:].rearrange("p c (g e) -> p c g e", g=NG), one_g[:].unsqueeze(3).broadcast_to((P, NC, NG, EG)),
                            one[:].unsqueeze(2).broadcast_to((P, NC, NG, EG)), ALU.mult))
                tt(MM[:], M1[:], M2[:], ALU.add).then_inc(masks_ready, 1)
                dve.wait_ge(group_exp, 1)
                link(red(col[:, 6, :], t_g[:], axis=AX.X, op=ALU.add))
                link(nc.vector.reciprocal(col[:, 7, :], col[:, 6, :]))
                dve.wait_ge(second_exp, 1)
                link(ts(col[:, 8, :], col[:, 5, :], 1.0, None, ALU.add))
                link(nc.vector.reciprocal(col[:, 9, :], col[:, 8, :]))
                link(tt(col[:, 10, :], col[:, 7, :], col[:, 9, :], ALU.mult))
                link(tt(col[:, 11, :], col[:, 10, :], col[:, 5, :], ALU.mult))
                dve.wait_ge(pos_done, 1)
                dve.wait_ge(masks_ready, 1)
                link(stt(prod[:], bank[5][:, 0:NC * E].rearrange("p (c e) -> p c e", c=NC), 1.0, MM[:], ALU.add, ALU.mult))
                by_pair = lambda w: w[:].rearrange("p c (i t) -> p c i t", t=2)
                link(ts(posr[:].rearrange("p i c t -> p c i t"), by_pair(prod), -1.0, None, ALU.add))
                link(tt(prod[:], MM[:], tok_col[:].unsqueeze(2).broadcast_to((P, NC, E)), ALU.mult))
                link(stt(prod[:], M2[:], float(T), prod[:], ALU.mult, ALU.add))
                link(nc.vector.tensor_copy(dstr[:].rearrange("p i c t -> p c i t"), by_pair(prod)))
                select(0, 0)
                counts = bank[5][:, NC * E:(NC + 1) * E].rearrange("p (i t) -> p i t", t=2)
                link(red(reps_f[:], counts, axis=AX.X, op=ALU.max))
                link(ts(reps_i[:], reps_f[:], float(CAP - 1), None, ALU.add))
                link(ts(reps_i[:], reps_i[:], 6, None, ALU.arith_shift_right))
                link(nc.vector.tensor_copy(reps_f[:], reps_i[:]))
                link(ts(reps_f[:], reps_f[:], 1.0, None, ALU.max))
                link(nc.vector.memset(job_at[:, 0:1], 0.0))
                link(ts(pair_f[:, 0:PAIRS], reps_f[:], 0.0, 1.0, ALU.mult, ALU.add))
                link(nc.vector.tensor_tensor_scan(job_at[:, 1:], pair_f[:, 0:PAIRS], reps_f[:], 0.0, ALU.mult, ALU.add))
                link(nc.vector.tensor_copy(job_at_i[:], job_at[:]))
                bj = lambda a: a.unsqueeze(2).broadcast_to((P, JOBS, PAIRS))
                bp = lambda a: a.unsqueeze(1).broadcast_to((P, JOBS, PAIRS))
                link(tt(job_cmp[:], bj(job_row[:]), bp(job_at[:, 1:]), ALU.is_ge))
                link(red(pair_f[:], job_cmp[:], axis=AX.X, op=ALU.add))
                link(ts(pair_i[:], pair_f[:], float(PAIRS - 1), None, ALU.min))
                link(tt(job_cmp[:], job_cmp[:], bp(reps_f[:]), ALU.mult))
                link(red(job_off[:], job_cmp[:], axis=AX.X, op=ALU.add))
                link(tt(job_off[:], job_row[:], job_off[:], ALU.subtract))
                ts(job_off[:], job_off[:], float(CAP), None, ALU.mult).then_inc(jobs_ready, 1)

            def select(g, pair):
                if pair is None:
                    pair = dve.value_load(pair_i[0:1, bass.ds(g, 1)], min_val=0, max_val=PAIRS - 1)
                    ins = ts(iota_off[:], iota_row[:], job_off[:, bass.ds(g, 1)], None, ALU.add)
                    row = iota_off
                    ins.then_inc(off_ready, 1)
                    dve.wait_ge(off_ready, g)
                else:
                    row = iota_row
                at_pair = lambda w: w[:, bass.ds(pair, 1), :, :].rearrange("p i c t -> p (i c t)")
                nc.vector.tensor_copy(dst_st[:].rearrange("p c t -> p (c t)"), at_pair(dstr)).then_inc(sel_ready, 1)
                tt(sel[:], row[:].unsqueeze(1).broadcast_to((P, 2 * NC, CAP)),
                   at_pair(posr).unsqueeze(2).broadcast_to((P, 2 * NC, CAP)), ALU.is_equal).then_inc(sel_ready, 1)

            def evacuate_gathered(g):
                dve.wait_ge(gather_done, g + 1)
                for h in range(2):
                    ins = tt(gT[:, 4 * h:4 * h + 4, :], bank[1 + h][:].rearrange("p (k t) -> p k t", k=4),
                             g2[:, 4 * h:4 * h + 4].unsqueeze(2).broadcast_to((P, 4, P)), ALU.mult)
                    ins.then_inc(gT_ready, 1)
                for e in range(2):
                    rows = slice(e * CAP, (e + 1) * CAP)
                    ts(row_z[rows, 0:1], bank[4][rows, e:e + 1], 0.0, float(4 * T), ALU.is_equal, ALU.mult).then_inc(row_z_ready, 1)
                    dve.wait_ge(row_z_ready, g * 2 + (e + 1))
                    stt(row_idx[rows, bass.ds(g, 1)], bank[4][rows, e:e + 1], -1.0, row_z[rows, 0:1],
                        ALU.add, ALU.add).then_inc(idx_ready, 1)

            def experts():
                dve.wait_ge(jobs_ready, 1)
                jobs = dve.value_load(job_at_i[0:1, PAIRS:PAIRS + 1], min_val=PAIRS, max_val=MAX_JOBS)
                evacuate_gathered(0)
                select(1, None)
                with dve.Fori(0, jobs) as g:
                    dve.wait_ge(silu_done, g + 1)
                    dve.wait_ge(hidT_done, g + START)
                    tt(hid[:], sil[:], bank[0][:, F:2 * F], ALU.mult).then_inc(hid_ready, 1)
                    evacuate_gathered(g + 1)
                    select(g + 2, None)
                    dve.wait_ge(down1_done, g + 1)
                    dve.wait_ge(y_free, g + START)
                    nc.vector.tensor_copy(y_sb[:, HALF:D], bank[7][:]).then_inc(y1_ready, 1)

            def ple():
                def split_low_ple(i):
                    dve.wait_ge(hi_split, U_WOUT + i + 1)
                    tt(w_lo[i % SPLIT][:], raw[(U_PLE + i) % RAW][:], w_hi[i % SPLIT][:].bitcast(F32),
                       ALU.subtract).then_inc(lo_split, 1)

                for i in range(SPLIT):
                    split_low_ple(i)
                for k in range(NPK):
                    dve.wait_ge(pT_hi_ready, k + 1)
                    tt(pT_lo[:, k, :], bank[4 + k][:], pT_hi[:, k, :].bitcast(F32), ALU.subtract).then_inc(pT_lo_ready, 1)
                for c in range(NC):
                    dve.wait_ge(yg_loaded[c], 32)
                    link(stt(x[:, c, :], yg[c][0][:], col[:, 10, c:c + 1], x[:, c, :], ALU.mult, ALU.add))
                    stt(x[:, c, :], yg[c][1][:], col[:, 11, c:c + 1], x[:, c, :], ALU.mult, ALU.add).then_inc(x2_ready, 1)
                    if c == 0:
                        for j in range(2):
                            dve.wait_ge(ple_units_done, j + 1)
                            for cc in range(NC):
                                nc.vector.tensor_copy(pu[:, cc, HALF * j:HALF * (j + 1)], bank[4 * j + cc][:]).then_inc(pu_ready, 1)
                    dve.wait_ge(std3_ready, c + 1)
                    link(nc.vector.reciprocal(stat[:, 52 + c:53 + c], stat[:, 40 + c:41 + c]))
                    ts(n3[:, c, :], x[:, c, :], stat[:, 52 + c:53 + c], None, ALU.mult).then_inc(n3_ready, 1)
                    if c < 2:
                        split_low_ple(SPLIT + c)
                    dve.wait_ge(n3_T, c + 1)
                    if c >= 2:
                        dve.wait_ge(h3T_lo_ready, c - 1)
                    for h in range(2):
                        g3 = par[:, pi["ple_norm"], 4 * h:4 * h + 4]
                        tt(h3[c % 2][:, 4 * h:4 * h + 4, :], bank[4 + 2 * (c % 2) + h][:].rearrange("p (k t) -> p k t", k=4),
                           g3.unsqueeze(2).broadcast_to((P, 4, P)), ALU.mult).then_inc(h3_ready, 1)
                    dve.wait_ge(h3T_hi_ready, c + 1)
                    cs = slice(c * P, (c + 1) * P)
                    tt(h3T_lo[:, :, cs], h3[c % 2][:], h3T_hi[:, :, cs].bitcast(F32), ALU.subtract).then_inc(h3T_lo_ready, 1)

                def gate(j, c):
                    m = NC * j + c
                    dve.wait_ge(gate_sig, m + 1)
                    ps = pu[:, c, HALF * j:HALF * (j + 1)]
                    xs = x[:, c, HALF * j:HALF * (j + 1)]
                    link(tt(ps, sg[c % 2][:], ps, ALU.mult))
                    tt(xs, xs, ps, ALU.add).then_inc(x3_ready, 1)

                for i in range(SPLIT + 2, N_PLE):
                    split_low_ple(i)
                    if i == 7:
                        dve.wait_ge(pu_ready, 2 * NC)
                        for c in range(NC):
                            gate(0, c)
                for c in range(NC):
                    gate(1, c)
                dve.wait_ge(std4_ready, 1)
                dve.wait_ge(fn_loaded, 16)
                link(nc.vector.reciprocal(stat[:, 56:56 + NC], stat[:, 48:48 + NC]))
                for c in range(NC):
                    stt(o_sb[c][:], x[:, c, :], stat[:, 56 + c:57 + c], fn_b[:], ALU.mult, ALU.mult).then_inc(out_ready, 1)

            dve.wait_ge(bs_loaded, 16)
            dve.wait_ge(rs_ready, 2)
            with dve.Fori(0, NB - 1) as b:
                channel_block(b, False)
            channel_block(NB - 1, True)
            for j in range(2):
                for c in range(NC):
                    if j == 0:
                        dve.wait_ge(units_done, U_WOUT + 4)
                    else:
                        dve.wait_ge(wout_done, c + 1)
                    xs = x[:, c, HALF * j:HALF * (j + 1)]
                    tt(xs, xs, bank[4 * j + c][:], ALU.add).then_inc(x1_half, 1)
                    if j == 1:
                        second_norm(c)
            for c in range(1, NC):
                pass
            route()
            experts()
            ple()

        @block.tensor
        def _(pe):
            mm, tr = nc.tensor.matmul, nc.tensor.transpose

            pe.wait_ge(ident_ready, 1)
            pe.wait_ge(par_loaded, 16 * N_RAW)
            tr(bank[7][:, 0:N_RAW * NB], par_raw[:], ident[0:N_RAW * NB, 0:N_RAW * NB]).then_inc(par_T, 1)
            pe.wait_ge(ws_masked, 1)
            for g in range(NB):
                last = tr(bank[g // 4][:, (g % 4) * P:(g % 4 + 1) * P], ws_raw[:, g, :], ident[:])
                if g % 4 == 3:
                    last.then_inc(ws_T, 1)
            pe.wait_ge(ones_ready, 1)
            for h in range(2):
                pe.wait_ge(wsT_ready, h + 1)
                mm(bank[2 + h][:], ones[:], wsT[:, 4 * h:4 * h + 4, :].rearrange("p a b -> p (a b)"),
                   start=True, stop=True).then_inc(rs_done, 1)
            pe.wait_ge(par_ready, 1)
            pe.wait_ge(rs_ready, 2)
            for c in range(NC):
                pe.wait_ge(xn_ready, c + 1)
                for k in range(NK):
                    last = tr(bank[k][:, c * P:(c + 1) * P], xn[:, c, k * P:(k + 1) * P], ident[:])
                last.then_inc(x_T, 1)

            def products(dst, hi_s, lo_s, hi_m, lo_m, start, stop):
                mm(dst, hi_s, hi_m, start=start, stop=False)
                mm(dst, hi_s, lo_m, start=False, stop=False)
                return mm(dst, lo_s, hi_m, start=False, stop=stop)

            for n in range(N_V):
                j, q = n // 4, n % 4
                pe.wait_ge(lo_split, n + 1)
                if n == 0:
                    pe.wait_ge(hT_lo_ready, 4)
                if n in (1, 2, 3, 4):
                    pe.wait_ge(hT_lo_ready, min(2 * n + 2, NK))
                s = split_slot(n)
                for c in range(NC):
                    for kk in range(2):
                        k = 2 * q + kk
                        cs = slice(c * P, (c + 1) * P)
                        ms = slice(kk * HALF, (kk + 1) * HALF)
                        last = products(bank[4 * j + c][:], hT_hi[:, k, cs], hT_lo[:, k, cs], w_hi[s][:, ms], w_lo[s][:, ms],
                                        k == 0, k == NK - 1)
                last.then_inc(units_done, 1)

            freed = [z_copied, gate_gelu, u_gelu, ma_sig, mb_sig]
            pe.wait_ge(v_gelu, 2 * NC)
            with pe.Fori(0, NB) as b:
                u0 = b * N_BLK + N_V
                for j in range(N_BLK):
                    pe.wait_ge(lo_split, u0 + (j + 1))
                    pe.wait_ge(freed[j], b + START)
                    s = SPLIT_SLOT[j]
                    for k in range(NK):
                        cs = slice(k * P, (k + 1) * P)
                        last = products(bank[j][:], w_hi[s][:, cs], w_lo[s][:, cs], hT_hi[:, k, :], hT_lo[:, k, :],
                                        k == 0, k == NK - 1)
                    last.then_inc(units_done, 1)
                    if j == 1:
                        pe.wait_ge(conv_done, b + 1 + START)
                        pe.wait_ge(staged, b * 3 + 3)
                        pe.wait_ge(ri_sig, b * 2 + START)
                        mm(bank[5][:], st_wa[:], tmp["xa"][:], start=True, stop=True)
                        mm(bank[6][:], st_wi[:], tmp["xa"][:], start=True, stop=True).then_inc(gates_done, 1)
                    if j == 2:
                        pe.wait_ge(staged_v, b * 2 + 2)
                        pe.wait_ge(sp_evac, b + START)
                        for c in range(NC):
                            last = mm(bank[7][:, c * P:(c + 1) * P], st_v[:, c, :], st_ws[:], start=True, stop=True)
                        last.then_inc(sgu_done, 1)
            for q in range(4):
                n = U_WOUT + q
                pe.wait_ge(unit_loaded[n % RAW], loads_of(n))
                pe.wait_ge(merged_done, 2 * q + 2 + START)
                if q == 0:
                    for s in freed[:4]:
                        pe.wait_ge(s, NB + START)
                for c in range(NC):
                    for kk in range(2):
                        k = 2 * q + kk
                        last = mm(bank[c][:], vm[:, k, c * P:(c + 1) * P], raw[n % RAW][:, kk * HALF:(kk + 1) * HALF],
                                  start=(k == 0), stop=(k == NK - 1))
                last.then_inc(units_done, 1)
            pe.wait_ge(mb_sig, NB + START)
            pe.wait_ge(ri_sig, 2 * NB + START)
            pe.wait_ge(sp_evac, NB + START)

            def second_half(c):
                for q in range(4):
                    n = U_WOUT + 4 + q
                    if c == 0:
                        pe.wait_ge(unit_loaded[n % RAW], loads_of(n))
                    for kk in range(2):
                        k = 2 * q + kk
                        last = mm(bank[4 + c][:], vm[:, k, c * P:(c + 1) * P], raw[n % RAW][:, kk * HALF:(kk + 1) * HALF],
                                  start=(k == 0), stop=(k == NK - 1))
                last.then_inc(wout_done, 1)

            def transpose_n2(c):
                pe.wait_ge(n2_ready, c + 1)
                if c >= 2:
                    pe.wait_ge(h2T_ready, 2 * (c - 1))
                for k in range(NK):
                    last = tr(bank[2 * (c % 2) + k // 4][:, (k % 4) * P:(k % 4 + 1) * P], n2[:, c, k, :], ident[:])
                last.then_inc(n2_T, 1)

            def router(c):
                pe.wait_ge(h2T_ready, 2 * c + 2)
                for k in range(NK):
                    last = mm(bank[4][:, c * NR:(c + 1) * NR], h2T[:, k, c * P:(c + 1) * P], w_r[:, k, :],
                              start=(k == 0), stop=(k == NK - 1))
                last.then_inc(router_done, 1)

            second_half(0)
            second_half(1)
            pe.wait_ge(x1_half, NC + 1)
            transpose_n2(0)
            second_half(2)
            transpose_n2(1)
            second_half(3)
            for c in range(NC):
                if c >= 2:
                    transpose_n2(c)
                router(c)
            pe.wait_ge(masks_ready, 1)
            pe.wait_ge(x1_half, NC + 2)
            for c in range(NC + 1):
                for cc in range(min(c + 1, NC)):
                    m = upper if cc == c else ones
                    last = mm(bank[5][:, c * E:(c + 1) * E], m[:], MM[:, cc, :], start=(cc == 0), stop=(cc == min(c, NC - 1)))
            last.then_inc(pos_done, 1)

            def gather(g):
                pe.wait_ge(sel_ready, g * 2 + 2)
                pe.wait_ge(gT_ready, g * 2)
                pe.wait_ge(idx_ready, g * 2)
                for c in range(NC):
                    mm(bank[4][:, 0:2], sel[:, 2 * c:2 * c + 2, :].rearrange("p e n -> p (e n)"), dst_st[:, c, :],
                       start=(c == 0), stop=(c == NC - 1))
                for k in range(NK):
                    dst = bank[1 + k // 4][:, (k % 4) * P:(k % 4 + 1) * P]
                    for c in range(NC):
                        one = sel[:, 2 * c:2 * c + 2, :].rearrange("p e n -> p (e n)")
                        mm(dst, n2_hi[:, c, k, :], one, start=(c == 0), stop=False)
                        last = mm(dst, n2_lo[:, c, k, :], one, start=False, stop=(c == NC - 1))
                last.then_inc(gather_done, 1)

            pe.wait_ge(n2_lo_ready, NC)
            pe.wait_ge(h2T_ready, 2 * NC)
            gather(0)
            pe.wait_ge(jobs_ready, 1)
            rows = [slice(0, CAP), slice(CAP, P)]

            def job(g, s, h):
                pe.wait_ge(gT_ready, g * 2 + 2)
                pe.wait_ge(hid_ready, g + START)
                for e in range(2):
                    pe.wait_ge(w13_loaded[s][e], h * 32 + 32)
                for k in range(NK):
                    for e in range(2):
                        last = mm(bank[0][rows[e], :], gT[:, k, rows[e]], w13[s][e][:, k, :, :].rearrange("p m f -> p (m f)"),
                                  start=(k == 0), stop=(k == NK - 1))
                last.then_inc(up_done, 1)
                gather(g + 1)
                pe.wait_ge(hid_ready, g + 1 + START)
                pe.wait_ge(hidT_ready, g + START)
                for f in range(FC):
                    last = tr(bank[3][:, f * P:(f + 1) * P], hid[:, f * P:(f + 1) * P], ident[:])
                last.then_inc(hidT_done, 1)
                pe.wait_ge(hidT_ready, g + 1 + START)
                pe.wait_ge(w2_loaded[s], h * 32 + 32)
                for j in range(2):
                    pe.wait_ge((y0_ready, y1_ready)[j], g + START)
                    for f in range(FC):
                        for e in range(2):
                            last = mm(bank[6 + j][rows[e], :], hidT[:, f, rows[e]], w2[s][:, e, f, HALF * j:HALF * (j + 1)],
                                      start=(f == 0), stop=(f == FC - 1))
                    last.then_inc((down0_done, down1_done)[j], 1)

            with pe.Fori(0, PAIRS // 2) as h:
                at_job = [pe.value_load(job_at_i[0:1, bass.ds(h * 2 + i, 1)], min_val=0, max_val=MAX_JOBS) for i in range(3)]
                for s in range(2):
                    with pe.Fori(at_job[s], at_job[s + 1]) as g:
                        job(g, s, h)
            jobs = pe.value_load(job_at_i[0:1, PAIRS:PAIRS + 1], min_val=PAIRS, max_val=MAX_JOBS)
            pe.wait_ge(p_loaded, 16)
            pe.wait_ge(gT_ready, jobs * 2 + 2)
            pe.wait_ge(idx_ready, jobs * 2 + 2)
            for k in range(NPK):
                for c in range(NC):
                    last = tr(bank[4 + k][:, c * P:(c + 1) * P], p_sb[:, c, k * P:(k + 1) * P], ident[:])
            last.then_inc(p_T, 1)
            pe.wait_ge(y1_ready, jobs + START)
            pe.wait_ge(y0_ready, jobs + START)
            pe.wait_ge(pT_lo_ready, NPK)
            for j in range(2):
                pe.wait_ge(lo_split, U_WOUT + j + 1)
                for c in range(NC):
                    for k in range(NPK):
                        cs, ms = slice(c * P, (c + 1) * P), slice(k * HALF, (k + 1) * HALF)
                        last = products(bank[4 * j + c][:], pT_hi[:, k, cs], pT_lo[:, k, cs], w_hi[j][:, ms], w_lo[j][:, ms],
                                        k == 0, k == NPK - 1)
                last.then_inc(ple_units_done, 1)
            pe.wait_ge(pu_ready, 2 * NC)
            for c in range(NC):
                pe.wait_ge(n3_ready, c + 1)
                if c >= 2:
                    pe.wait_ge(h3_ready, 2 * (c - 1))
                for k in range(NK):
                    last = tr(bank[4 + 2 * (c % 2) + k // 4][:, (k % 4) * P:(k % 4 + 1) * P], n3[:, c, k * P:(k + 1) * P], ident[:])
                last.then_inc(n3_T, 1)
            pe.wait_ge(h3T_lo_ready, NC)
            for i in range(2, N_PLE):
                j, q = (i - 2) // 4, (i - 2) % 4
                pe.wait_ge(lo_split, U_WOUT + i + 1)
                s = i % SPLIT
                for c in range(NC):
                    for kk in range(2):
                        k = 2 * q + kk
                        cs, ms = slice(c * P, (c + 1) * P), slice(kk * HALF, (kk + 1) * HALF)
                        last = products(bank[4 * j + c][:], h3T_hi[:, k, cs], h3T_lo[:, k, cs], w_hi[s][:, ms], w_lo[s][:, ms],
                                        k == 0, k == NK - 1)
                last.then_inc(ple_units_done, 1)


def kernel(**inputs):
    import numpy as _np
    import concourse.bacc as _bacc
    from concourse import mybir as _mybir
    from concourse.bass_utils import run_bass_kernel_spmd as _run

    nc = _bacc.Bacc("TRN2", target_bir_lowering=False, num_devices=1)
    arrays, args = {}, {}
    for name, a in inputs.items():
        a = _np.ascontiguousarray(a)
        arrays[f"in_{name}_dram"] = a
        args[name] = nc.dram_tensor(f"in_{name}_dram", a.shape, _mybir.dt.from_np(a.dtype), kind="ExternalInput").ap()
    shape = inputs["x"].shape
    out = nc.dram_tensor("out_dram", shape, _mybir.dt.float32, kind="ExternalOutput").ap()
    y_rows = nc.dram_tensor("y_rows", (2 * shape[1], shape[2]), _mybir.dt.float32).ap()
    hybrid_block_program(nc, args, y_rows, out)
    r = _run(nc, [arrays], core_ids=[0])
    return r.results[0]["out_dram"]
```

```python
from contextlib import ExitStack

import concourse.bass as bass
from concourse import mybir

F32 = mybir.dt.float32
F32R = mybir.dt.float32r
I32 = mybir.dt.int32
U32 = mybir.dt.uint32
U8 = mybir.dt.uint8
ALU = mybir.AluOpType
ACT = mybir.ActivationFunctionType
AX = mybir.AxisListType

P = 128
KIB = 1024
EPS = 1e-6
LRU_C = 8.0


def hybrid_block_program(nc, A, n2_rows, y_rows, out):
    T, D = A["x"].shape[1:]
    NC = T // P
    NK = D // P
    HALF = D // 2
    PLE = A["p"].shape[3]
    NPK = PLE // P
    E, F = A["expert_w1"].shape[1], A["expert_w1"].shape[3]
    NG = A["router_group_w"].shape[2]
    EG = E // NG
    NR = NG + E
    FC = F // P
    CAP = P // 2
    PAIRS = E // 2
    MAX_JOBS = PAIRS + 2 * T // CAP - 1
    JOBS = MAX_JOBS + 3
    CONV = A["conv_w"].shape[1]
    NB = A["sgu_ws"].shape[1]
    HB = A["lru_wa"].shape[2]
    assert (D, T, NB * P, NC) == (1024, 512, D, 4) and HB * 2 == P and T * 2 == E * 32

    w_in = A["w_in"][0].rearrange("(k p) n -> p k n", p=P)
    w_out = A["w_out"][0].rearrange("(k p) n -> p k n", p=P)
    ple_gate = A["ple_gate_w"][0].rearrange("(k p) n -> p k n", p=P)
    ple_up = A["ple_up_w"][0].rearrange("(k p) n -> p k n", p=P)
    V_COL = 3 * D
    BLOCK_COLS = [0, D, 2 * D, 4 * D, 5 * D]

    PAR = ["mix_norm", "conv_w0", "conv_w1", "conv_w2", "conv_w3", "conv_b", "lru_ba", "lru_bi", "lru_lambda",
           "sgu_ln_g", "sgu_ln_b", "ffn_norm", "ple_norm"]
    pi = {n: i for i, n in enumerate(PAR)}
    N_RAW = len(PAR)
    pi["neg_c"], pi["half_c"] = N_RAW, N_RAW + 1
    N_PAR = N_RAW + 2

    RAW = 5
    N_V, N_BLK = 8, 5
    U_WOUT = N_V + N_BLK * NB
    SPLIT = 3
    SPLIT_SLOT = [0, 1, 2, 0, 1]
    SPLIT_AGE = [2, 2, 5, 3, 3]

    ctx = ExitStack()
    with ctx:
        base = nc.sbuf_base
        base += -base % 64
        ARENA = 207 * KIB
        ctx.enter_context(nc.sbuf_tensor("arena", [P, ARENA], U8))

        def at(name, off, shape, dt=F32):
            n = 4
            for s in shape[1:]:
                n *= s
            assert off + n <= ARENA, name
            return nc.alloc_sbuf_tensor_at(name, shape, dt, offset=base + off)

        K = KIB
        x = at("x_res", 0, [P, NC, D])
        raw = [at(f"raw{i}", (16 + 4 * i) * K, [P, D]) for i in range(RAW)]
        w_hi = [at(f"w_hi{i}", (36 + 4 * i) * K, [P, D], F32R) for i in range(SPLIT)]
        w_lo = [at(f"w_lo{i}", (48 + 4 * i) * K, [P, D], F32R) for i in range(SPLIT)]
        hT_hi = at("hT_hi", 108 * K, [P, NK, T], F32R)
        hT_lo = at("hT_lo", 124 * K, [P, NK, T], F32R)
        xn = at("xn", 140 * K, [P, NC, D])
        vm = at("v_then_merged", 140 * K, [P, NB, T])
        o = 156 * K
        tmp = {}
        for n in ["xa", "r", "i", "a", "th", "ga", "gu", "sa", "sb", "s"]:
            tmp[n] = at("t_" + n, o, [P, T])
            o += 2 * K
        z = at("z_lru", o, [P, T + CONV - 1])
        o += 2112
        wa_bd = at("wa_bd", o, [P, NB, P]); o += 4 * K
        wi_bd = at("wi_bd", o, [P, NB, P]); o += 4 * K
        wsT = at("wsT", o, [P, NB, P]); o += 4 * K
        bs_b = at("bs_b", o, [P, NB, P]); o += 4 * K
        rs_b = at("rs_b", o, [P, NB, P]); o += 4 * K
        st_v = at("st_v", o, [P, NC, P]); o += 2 * K
        st_wa = at("st_wa", o, [P, P]); o += 512
        st_wi = at("st_wi", o, [P, P]); o += 512
        st_ws = at("st_ws", o, [P, P]); o += 512
        st_par = at("st_par", o, [P, N_PAR]); o += 64
        ws_raw = at("ws_raw", 160 * K, [P, NB, P])
        par_raw = at("par_raw", 164 * K, [N_RAW * NB, P])
        sq_junk = at("sq_junk", 166 * K, [P, D])
        n2 = at("n2", 172 * K, [P, NC, NK, P])
        junk2 = at("junk2", 188 * K, [P, D])
        h2T = at("h2T", 140 * K, [P, NK, T])
        w13 = [[at(f"w13_{s}{e}", (o + 16 * e) * K, [P, NK, 2, F]) for e in range(2)] for s, o in enumerate((60, 108, 16))]
        w2 = [at(f"w2_{s}", o * K, [P, 2, FC, D]) for s, o in enumerate((92, 140, 156))]
        sel = at("sel", 48 * K, [P, NC * 2, CAP], F32R)
        y_sb = at("y_sb", 50 * K, [P, D])
        sil = at("sil", 54 * K, [P, F])
        hid = at("hid", 55 * K, [P, F])
        hidT = at("hidT", 56 * K, [P, FC, P])
        job_cmp = at("job_cmp", 57 * K, [P, JOBS, PAIRS])
        rows_sb = at("rows_sb", 180 * K, [P, NK, P])
        gT = at("gT", 184 * K, [P, NK, P])
        o2 = 192 * K

        def table(name, shape, dt=F32):
            nonlocal o2
            t = at(name, o2, [P] + shape, dt)
            n = 4
            for q in shape:
                n *= q
            o2 += -(-n // 32) * 32
            return t

        w_r = table("w_router", [NK, NR])
        b_r = table("b_router", [NR])
        g2 = table("ffn_norm_cols", [NK])
        upper = table("upper", [P])
        iota_row = table("iota_row", [CAP])
        rank_row = table("rank_row", [EG])
        lg = table("lg", [NC, NR])
        t_g = table("t_g", [NC, NG])
        one_g = table("one_g", [NC, NG])
        t_eg = table("t_eg", [NC, EG, NG])
        es = table("es", [NC, EG])
        es2 = table("es2", [NC, EG])
        t_e = table("t_e", [NC, EG])
        one1 = table("one1", [NC, EG])
        one2 = table("one2", [NC, EG])
        col = table("col", [16, NC])
        M1 = table("M1", [NC, E])
        M2 = table("M2", [NC, E])
        MM = table("MM", [NC, E])
        prod = table("prod", [NC, E])
        posr = table("posr", [PAIRS, NC, 2])
        dstr = table("dstr", [PAIRS, NC, 2])
        dst_st = table("dst_st", [NC, 2], F32R)
        tok_col = table("tok_col", [NC])
        job_row = table("job_row", [JOBS])
        iota_off = table("iota_off", [CAP])
        reps_i = table("reps_i", [PAIRS], I32)
        reps_f = table("reps_f", [PAIRS])
        job_at = table("job_at", [PAIRS + 1])
        job_at_i = table("job_at_i", [PAIRS + 1], I32)
        pair_f = table("pair_f", [JOBS])
        pair_i = table("pair_i", [JOBS], I32)
        job_off = table("job_off", [JOBS])
        row_idx = table("row_idx", [JOBS], U32)
        row_f = table("row_f", [2])
        row_z = table("row_z", [2])
        tok_idx = table("tok_idx", [JOBS], U32)
        src_st = table("src_st", [1], U32)
        dst_idx_st = table("dst_idx_st", [1], U32)
        assert o2 <= 201 * K + 512, o2
        gate_raw = at("gate_raw", 108 * K, [P, NK, D])
        gate_lo = at("gate_lo", 108 * K, [P, NK, D], F32R)
        gate_hi = at("gate_hi", 16 * K, [P, NK, D], F32R)
        up_raw = at("up_raw", 140 * K, [P, NPK, D])
        up_lo = at("up_lo", 140 * K, [P, NPK, D], F32R)
        up_hi = at("up_hi", 156 * K, [P, NPK, D], F32R)
        p_sb = at("p_sb", 148 * K, [P, NC, PLE])
        fn_b = at("fn_b", 152 * K, [P, D])
        pT_hi = at("pT_hi", 164 * K, [P, NPK, T], F32R)
        pT_lo = at("pT_lo", 168 * K, [P, NPK, T], F32R)
        pu = at("pu", 60 * K, [P, NC, D])
        yg = [[at(f"yg{c}{t}", (76 + 8 * c + 4 * t) * K, [P, D]) for t in range(2)] for c in range(NC)]
        o_sb = [at(f"o_sb{c}", (76 + 8 * c) * K, [P, D]) for c in range(NC)]
        n3 = [at(f"n3_{c}", (80 + 8 * c) * K, [P, D]) for c in range(NC)]
        h3 = at("h3", 52 * K, [P, NK, P])
        sg = [at(f"sg{i}", (56 + 2 * i) * K, [P, HALF]) for i in range(2)]
        h3T_hi = [at(f"h3T_hi{i}", (172 + 8 * i) * K, [P, NK, P], F32R) for i in range(2)]
        h3T_lo = [at(f"h3T_lo{i}", (176 + 8 * i) * K, [P, NK, P], F32R) for i in range(2)]
        junk3 = at("junk3", 188 * K, [P, D])
        ident = at("ident", o, [P, P]); o += 512
        ones = at("ones", o, [P, P]); o += 512
        par = at("par", o, [P, N_PAR, NB]); o += 480
        stat = at("stat", o, [P, 64]); o += 256
        sp_t = at("sp_t", o, [P, 6, NB]); o += 192
        bn_s = at("bn_s", o, [P, NC, 2, 6]); o += 192
        bn_m = at("bn_m", o, [P, NC, 2]); o += 32
        assert o <= ARENA, o

        bank = [ctx.enter_context(nc.psum_tensor(f"bank{i}", [P, 512], F32)) for i in range(8)]

        def sem(name):
            return ctx.enter_context(nc.semaphore(name))

        x_loaded = [sem(f"x_loaded{c}") for c in range(NC)]
        par_loaded, ws_loaded, bs_loaded, lruw_loaded = sem("par_loaded"), sem("ws_loaded"), sem("bs_loaded"), sem("lruw_loaded")
        unit_loaded = [sem(f"unit_loaded{i}") for i in range(RAW)]
        stored = sem("stored")
        ident_ready, ones_ready, zeroed, ws_masked = sem("ident_ready"), sem("ones_ready"), sem("zeroed"), sem("ws_masked")
        eps_ready, z_pad_ready = sem("eps_ready"), sem("z_pad_ready")
        par_T, par_ready, ws_T, wsT_ready, rs_done, rs_ready = (sem(n) for n in ["par_T", "par_ready", "ws_T", "wsT_ready", "rs_done", "rs_ready"])
        squares, std_ready, xn_ready, x_T, hT_hi_ready, hT_lo_ready = (sem(n) for n in ["squares", "std_ready", "xn_ready", "x_T", "hT_hi_ready", "hT_lo_ready"])
        hi_split, lo_split, units_done = sem("hi_split"), sem("lo_split"), sem("units_done")
        v_gelu, v_var, v_std, v_normed = sem("v_gelu"), sem("v_var"), sem("v_std"), sem("v_normed")
        c_ready, softplus_abs, softplus_exp = sem("c_ready"), sem("softplus_abs"), sem("softplus_exp")
        staged, staged_v = sem("staged"), sem("staged_v")
        z_copied, conv_done, gates_done, gate_gelu, u_gelu = (sem(n) for n in ["z_copied", "conv_done", "gates_done", "gate_gelu", "u_gelu"])
        ri_sig, tanh_done, ma_sig, decay_ready, root_ready, mb_sig = (sem(n) for n in ["ri_sig", "tanh_done", "ma_sig", "decay_ready", "root_ready", "mb_sig"])
        sgu_done, sp_evac, sp_params, merged_done = sem("sgu_done"), sem("sp_evac"), sem("sp_params"), sem("merged_done")
        y_free = sem("y_free")
        dve_chain, sp_passed, pool_passed = sem("dve_chain"), sem("sp_passed"), sem("pool_passed")
        wout_done, x1_half = sem("wout_done"), sem("x1_half")
        squares2, std2_ready, n2_ready, n2_stored, n2_T, h2T_ready, router_done = (sem(n) for n in [
            "squares2", "std2_ready", "n2_ready", "n2_stored", "n2_T", "h2T_ready", "router_done"])
        router_loaded, tables_ready, group_shift, group_exp, second_shift, second_exp = (sem(n) for n in [
            "router_loaded", "tables_ready", "group_shift", "group_exp", "second_shift", "second_exp"])
        masks_ready, pos_done, jobs_ready = sem("masks_ready"), sem("pos_done"), sem("jobs_ready")
        pair_loaded = [[sem(f"pair_loaded{s}{i}") for i in range(6)] for s in range(3)]
        sel_ready, idx_summed, rows_cleared, rows_loaded, rows_T, gT_ready, up_done, silu_done, hid_ready, hidT_done, hidT_ready = (sem(n) for n in [
            "sel_ready", "idx_summed", "rows_cleared", "rows_loaded", "rows_T", "gT_ready", "up_done", "silu_done", "hid_ready", "hidT_done", "hidT_ready"])
        down0_done, down1_done, y0_ready, y1_ready = sem("down0_done"), sem("down1_done"), sem("y0_ready"), sem("y1_ready")
        y_stored, idx_ready, src_staged, dst_staged, off_ready, row_z_ready, row_idx_ready = (sem(n) for n in [
            "y_stored", "idx_ready", "src_staged", "dst_staged", "off_ready", "row_z_ready", "row_idx_ready"])
        yg_loaded = [sem(f"yg_loaded{c}") for c in range(NC)]
        up_loaded, gate_loaded = sem("up_loaded"), [sem(f"gate_loaded{q}") for q in range(4)]
        ple_hi, ple_lo = sem("ple_hi"), sem("ple_lo")
        p_loaded, fn_loaded, p_T, pT_hi_ready, pT_lo_ready, pu_done, pu_ready = (sem(n) for n in [
            "p_loaded", "fn_loaded", "p_T", "pT_hi_ready", "pT_lo_ready", "pu_done", "pu_ready"])
        x2_ready, squares3, std3_ready, n3_ready, n3_T, h3_ready, h3T_hi_ready, h3T_lo_ready = (sem(n) for n in [
            "x2_ready", "squares3", "std3_ready", "n3_ready", "n3_T", "h3_ready", "h3T_hi_ready", "h3T_lo_ready"])
        gate_done, gate_sig, x3_ready, squares4, std4_ready, out_ready = (sem(n) for n in [
            "gate_done", "gate_sig", "x3_ready", "squares4", "std4_ready", "out_ready"])

        def split_slot(n):
            return n % SPLIT if n < N_V else SPLIT_SLOT[(n - N_V) % N_BLK]

        START = 1
        started = [gates_done, root_ready, sp_params, sgu_done, conv_done, merged_done, z_copied, gate_gelu, u_gelu,
                   ma_sig, mb_sig, ri_sig, sp_evac, y_free, hid_ready, hidT_done, hidT_ready, y0_ready, y1_ready]

        block = ctx.enter_context(nc.Block())

        def loads_of(n):
            return 16 * (n // RAW + 1)

        LAST_SLOT = (PAIRS - 1) % 3
        N_PLE = NPK + NK
        N_MID = NPK

        @block.sync
        def _(sp):
            for c in range(NC):
                sp.dma_start(x[:, c, :], A["x"][0, c * P:(c + 1) * P, :]).then_inc(x_loaded[c], 16)
            for n in range(N_V):
                j, q = n // 4, n % 4
                if n >= RAW:
                    sp.wait_ge(lo_split, n - RAW + 1)
                src = w_in[:, 2 * q:2 * q + 2, V_COL + HALF * j:V_COL + HALF * (j + 1)]
                sp.dma_start(raw[n % RAW][:].rearrange("p (k n) -> p k n", k=2), src).then_inc(unit_loaded[n % RAW], 16)
            with sp.Fori(0, NB) as b:
                for j in range(N_BLK):
                    n = N_V + j
                    sp.wait_ge(lo_split, b * N_BLK + (n - RAW + 1))
                    src = w_in[:, :, bass.ds(b * P + BLOCK_COLS[j], P)]
                    sp.dma_start(raw[n % RAW][:].rearrange("p (k n) -> p k n", k=NK), src).then_inc(unit_loaded[n % RAW], 16)
            for i in range(8):
                n = U_WOUT + i
                j, q = i // 4, i % 4
                if n - RAW < U_WOUT:
                    sp.wait_ge(lo_split, n - RAW + 1)
                else:
                    sp.wait_ge(units_done, n - RAW + 1)
                src = w_out[:, 2 * q:2 * q + 2, HALF * j:HALF * (j + 1)]
                sp.dma_start(raw[n % RAW][:].rearrange("p (k n) -> p k n", k=2), src).then_inc(unit_loaded[n % RAW], 16)

            def load(s, i, first):
                if i < 4:
                    e, m = i // 2, i % 2
                    src = A[("expert_w1", "expert_w3")[m]][0, bass.ds(first + e, 1)].rearrange("a (p k) f -> p k (a f)", k=NK)
                    sp.dma_start(w13[s][e][:, :, m, :], src).then_inc(pair_loaded[s][i], 16)
                else:
                    e = i - 4
                    src = A["expert_w2"][0, bass.ds(first + e, 1)].rearrange("a (c p) n -> p c (a n)", p=P)
                    sp.dma_start(w2[s][:, e, :, :], src).then_inc(pair_loaded[s][i], 16)

            def load_pair(s, first, free, h):
                sp.wait_ge(up_done, free)
                for i in range(6):
                    if i >= 2:
                        sp.wait_ge(pair_loaded[s][i - 2], h * 16 + 16)
                    elif s > 0:
                        sp.wait_ge(pair_loaded[s - 1][i + 4], h * 16 + 16)
                    else:
                        sp.wait_ge(pair_loaded[2][i + 4], h * 16)
                    if i == 4:
                        sp.wait_ge(down1_done, free)
                    load(s, i, first)

            for i in range(6):
                load(0, i, 0)
            sp.wait_ge(units_done, U_WOUT)
            for i in range(4):
                load(1, i, 2)
            sp.wait_ge(merged_done, NB + START)
            for i in (4, 5):
                load(2, i, 4)
            sp.wait_ge(wout_done, NC)
            for i in range(4):
                load(2, i, 4)
            sp.wait_ge(router_done, NC)
            for i in (4, 5):
                load(1, i, 2)
            sp.wait_ge(jobs_ready, 1)

            def end_of(pair):
                return sp.value_load(job_at_i[0:1, bass.ds(pair + 1, 1)], min_val=1, max_val=MAX_JOBS)

            with sp.Fori(0, PAIRS // 3 - 1) as h:
                for s in range(3):
                    load_pair(s, h * 6 + (6 + 2 * s), end_of(h * 3 + s), h + 1)
            load_pair(LAST_SLOT, E - 2, end_of(PAIRS - 4), PAIRS // 3)
            end = end_of(PAIRS - 3)
            sp.wait_ge(up_done, end)
            sp.wait_ge(down1_done, end)
            sp.dma_start(up_raw[:], ple_up).then_inc(up_loaded, 16)
            sp.dma_start(p_sb[:], A["p"][0, 0].rearrange("(c p) n -> p c n", p=P)).then_inc(p_loaded, 16)
            for q in range(4):
                sp.dma_start(gate_raw[:, 2 * q:2 * q + 2, :], ple_gate[:, 2 * q:2 * q + 2, :]).then_inc(gate_loaded[q], 16)
            sp.dma_start(fn_b[:], A["final_norm"][None, :].broadcast_to((P, D))).then_inc(fn_loaded, 16)
            jobs = sp.value_load(job_at_i[0:1, PAIRS:PAIRS + 1], min_val=PAIRS, max_val=MAX_JOBS)
            sp.wait_ge(y_free, jobs + START)
            sp.wait_ge(down1_done, jobs)
            for c in range(NC):
                for t in range(2):
                    sp.dma_start(yg[c][t][:], y_rows[T * t + P * c:T * t + P * (c + 1), :]).then_inc(yg_loaded[c], 16)
            for c in range(NC):
                sp.wait_ge(out_ready, c + 1)
                sp.dma_start(out[0, c * P:(c + 1) * P, :], o_sb[c][:]).then_inc(stored, 16)
            sp.wait_ge(stored, 16 * NC)

        @block.gpsimd
        def _(pool):
            for s in started:
                pool.sem_inc(s, START)
            nc.gpsimd.memset(ident[:], 0.0).then_inc(zeroed, 1)
            nc.gpsimd.memset(ones[:], 1.0).then_inc(ones_ready, 1)
            nc.gpsimd.memset(stat[:, 0:1], EPS).then_inc(eps_ready, 1)
            pool.wait_ge(zeroed, 1)
            nc.gpsimd.affine_select(out=ident[:], in_=ident[:], compare_op=ALU.not_equal, fill=1.0, base=0,
                                    pattern=[[-1, P]], channel_multiplier=1).then_inc(ident_ready, 1)
            nc.gpsimd.memset(wa_bd[:], 0.0).then_inc(zeroed, 1)
            nc.gpsimd.memset(wi_bd[:], 0.0).then_inc(zeroed, 1)
            pool.wait_ge(zeroed, 3)
            for dst, src in ((wa_bd, A["lru_wa"]), (wi_bd, A["lru_wi"])):
                w = src[0].rearrange("(b two) i j -> two i b j", two=2)
                for h in range(2):
                    pool.dma_start(dst[h * HB:(h + 1) * HB, :, h * HB:(h + 1) * HB], w[h]).then_inc(lruw_loaded, 16)
            pool.wait_ge(ws_loaded, 16)
            nc.gpsimd.affine_select(out=ws_raw[:], in_=ws_raw[:], compare_op=ALU.is_ge, fill=0.0, base=0,
                                    pattern=[[0, NB], [-1, P]], channel_multiplier=1).then_inc(ws_masked, 1)
            nc.gpsimd.memset(z[:, 0:CONV - 1], 0.0).then_inc(z_pad_ready, 1)
            pool.wait_ge(c_ready, 1)
            pool.wait_ge(lruw_loaded, 64)
            pool.wait_ge(wsT_ready, 2)
            with pool.Fori(0, NB) as b:
                pool.wait_ge(gates_done, b + START)
                pool.wait_ge(root_ready, b + START)
                pool.wait_ge(sp_params, b + START)
                nc.gpsimd.tensor_copy(st_par[:], par[:, :, bass.ds(b, 1)].rearrange("p a b -> p (a b)")).then_inc(staged, 1)
                nc.gpsimd.tensor_copy(st_wa[:], wa_bd[:, bass.ds(b, 1), :].rearrange("p a b -> p (a b)")).then_inc(staged, 1)
                nc.gpsimd.tensor_copy(st_wi[:], wi_bd[:, bass.ds(b, 1), :].rearrange("p a b -> p (a b)")).then_inc(staged, 1)
                pool.wait_ge(sgu_done, b + START)
                pool.wait_ge(v_normed, NC)
                nc.gpsimd.tensor_copy(st_ws[:], wsT[:, bass.ds(b, 1), :].rearrange("p a b -> p (a b)")).then_inc(staged_v, 1)
                nc.gpsimd.tensor_copy(st_v[:].rearrange("p c n -> p (c n)"),
                                      vm[:, bass.ds(b, 1), :].rearrange("p a b -> p (a b)")).then_inc(staged_v, 1)

            pool.wait_ge(merged_done, NB + START)
            pool.dma_start(w_r[:, :, 0:NG], A["router_group_w"][0].rearrange("(p k) n -> p k n", k=NK)).then_inc(router_loaded, 16)
            pool.dma_start(w_r[:, :, NG:NR], A["router_expert_w"][0].rearrange("(p k) n -> p k n", k=NK)).then_inc(router_loaded, 16)
            pool.dma_start(b_r[:, 0:NG], A["router_group_b"].broadcast_to((P, NG))).then_inc(router_loaded, 16)
            pool.dma_start(b_r[:, NG:NR], A["router_expert_b"].broadcast_to((P, E))).then_inc(router_loaded, 16)
            pool.dma_start(g2[:], A["ffn_norm"][0].rearrange("(p k) -> p k", k=NK)).then_inc(router_loaded, 16)
            nc.gpsimd.memset(upper[:], 1.0).then_inc(zeroed, 1)
            nc.gpsimd.iota(tok_col[:], [[P, NC]], base=1, channel_multiplier=1,
                           allow_small_or_imprecise_dtypes=True).then_inc(tables_ready, 1)
            nc.gpsimd.iota(iota_row[:], [[1, CAP]], base=0, channel_multiplier=0,
                           allow_small_or_imprecise_dtypes=True).then_inc(tables_ready, 1)
            nc.gpsimd.iota(rank_row[:], [[-1, EG]], base=EG, channel_multiplier=0,
                           allow_small_or_imprecise_dtypes=True).then_inc(tables_ready, 1)
            nc.gpsimd.iota(job_row[:], [[1, JOBS]], base=0, channel_multiplier=0,
                           allow_small_or_imprecise_dtypes=True).then_inc(tables_ready, 1)
            pool.wait_ge(zeroed, 4)
            nc.gpsimd.affine_select(out=upper[:], in_=upper[:], compare_op=ALU.is_gt, fill=0.0, base=0,
                                    pattern=[[1, P]], channel_multiplier=-1).then_inc(tables_ready, 1)
            last_token, last_row = pool.to_reg(T - 1), pool.to_reg(2 * T - 1)

            def gather():
                pool.indirect_dma_start(out=rows_sb[:].rearrange("p k n -> p (k n)"), out_offset=None, in_=n2_rows[:, :],
                                        in_offset=bass.IndirectOffsetOnAxis(ap=src_st[:, 0:1], axis=0),
                                        bounds_check=last_token, oob_is_err=False).then_inc(rows_loaded, 16)

            pool.wait_ge(n2_T, NC)
            pool.wait_ge(n2_stored, 16 * NC)
            nc.gpsimd.memset(rows_sb[:], 0.0).then_inc(rows_cleared, 1)
            for g in range(2):
                pool.wait_ge(idx_ready, g + 1)
                if g > 0:
                    pool.wait_ge(rows_loaded, 16 * g)
                nc.gpsimd.tensor_copy(src_st[:], tok_idx[:, g:g + 1]).then_inc(src_staged, 1)
                pool.wait_ge(src_staged, g + 1)
                if g == 0:
                    pool.wait_ge(rows_cleared, 1)
                else:
                    pool.wait_ge(rows_T, g)
                gather()
            pool.wait_ge(jobs_ready, 1)
            jobs = pool.value_load(job_at_i[0:1, PAIRS:PAIRS + 1], min_val=PAIRS, max_val=MAX_JOBS)
            with pool.Fori(0, jobs) as g:
                pool.wait_ge(idx_ready, g + 3)
                pool.wait_ge(rows_loaded, g * 16 + 32)
                nc.gpsimd.tensor_copy(src_st[:], tok_idx[:, bass.ds(g + 2, 1)]).then_inc(src_staged, 1)
                pool.wait_ge(src_staged, g + 3)
                pool.wait_ge(rows_T, g + 2)
                pool.sem_inc(pool_passed, 1)
                gather()
                nc.gpsimd.tensor_copy(dst_idx_st[:], row_idx[:, bass.ds(g, 1)]).then_inc(dst_staged, 1)
                pool.wait_ge(dst_staged, g + 1)
                pool.wait_ge(y0_ready, g + 1 + START)
                pool.wait_ge(y1_ready, g + 1 + START)
                pool.sem_inc(pool_passed, 1)
                pool.indirect_dma_start(out=y_rows[:, :], out_offset=bass.IndirectOffsetOnAxis(ap=dst_idx_st[:, 0:1], axis=0),
                                        in_=y_sb[:], in_offset=None, bounds_check=last_row,
                                        oob_is_err=False).then_inc(y_stored, 16)
                pool.wait_ge(y_stored, g * 16 + 16)
                pool.sem_inc(y_free, 1)

        @block.scalar
        def _(act):
            for i, n in enumerate(PAR):
                src = A["conv_w"][0, int(n[-1])] if n.startswith("conv_w") else A[n][0]
                act.dma_start(par_raw[i * NB:(i + 1) * NB, :], src.rearrange("(b c) -> b c", c=P)).then_inc(par_loaded, 16)
            act.dma_start(ws_raw[:], A["sgu_ws"][0].rearrange("g t s -> t g s")).then_inc(ws_loaded, 16)
            act.dma_start(bs_b[:].rearrange("p g t -> p (g t)"),
                          A["sgu_bs"][0].rearrange("g t -> (g t)")[None, :].broadcast_to((P, NB * P))).then_inc(bs_loaded, 16)

            def split_high(n, slot, count, free_after):
                act.wait_ge(unit_loaded[slot[0]], count)
                if free_after is not None:
                    act.wait_ge(units_done, free_after)
                nc.scalar.activation(w_hi[slot[1]][:], raw[slot[0]][:], ACT.Copy).then_inc(hi_split, 1)

            def split_high_v(n):
                age = SPLIT if n <= N_V else None
                free = n - 2 if n >= SPLIT else None
                if n == N_V:
                    free = n - 1
                split_high(n, (n % RAW, split_slot(n)), loads_of(n), free)

            for c in range(NC):
                act.wait_ge(x_loaded[c], 16)
                if c > 0:
                    act.wait_ge(squares, c)
                nc.scalar.activation(sq_junk[:], x[:, c, :], ACT.Square, accum_out=stat[:, 4 + c:5 + c]).then_inc(squares, 1)
                if c == 0:
                    act.wait_ge(eps_ready, 1)
                act.wait_ge(squares, c + 1)
                nc.scalar.activation(stat[:, 8 + c:9 + c], stat[:, 4 + c:5 + c], ACT.Sqrt, bias=stat[:, 0:1],
                                     scale=1.0 / D).then_inc(std_ready, 1)
            for n in range(SPLIT):
                split_high_v(n)
            act.wait_ge(x_T, NC)
            act.wait_ge(par_ready, 1)
            for k in range(NK):
                nc.scalar.activation(hT_hi[:, k, :], bank[k][:], ACT.Copy,
                                     scale=par[:, pi["mix_norm"], k:k + 1]).then_inc(hT_hi_ready, 1)

            def gelu_v(j):
                act.wait_ge(units_done, 4 * (j + 1))
                for c in range(NC):
                    dst = vm[:, 4 * j:4 * j + 4, c * P:(c + 1) * P]
                    nc.scalar.activation(dst, bank[4 * j + c][:].rearrange("p (g n) -> p g n", n=P),
                                         ACT.Gelu_apprx_tanh).then_inc(v_gelu, 1)

            split_high_v(3)
            split_high_v(4)
            split_high_v(5)
            gelu_v(0)
            split_high_v(6)
            split_high_v(7)
            split_high_v(8)
            gelu_v(1)
            lam = par[:, pi["lru_lambda"], :]
            nc.scalar.activation(sp_t[:, 0, :], lam, ACT.Abs).then_inc(softplus_abs, 1)
            act.wait_ge(softplus_abs, 1)
            nc.scalar.activation(sp_t[:, 1, :], sp_t[:, 0, :], ACT.Exp, scale=-1.0).then_inc(softplus_exp, 1)
            act.wait_ge(v_var, NC)
            nc.scalar.activation(stat[:, 16:16 + NC], bn_m[:, :, 1], ACT.Sqrt, bias=stat[:, 0:1]).then_inc(v_std, 1)

            def channel_block(b, last):
                u0 = b * N_BLK + N_V

                def high(j):
                    m = N_V + j
                    act.wait_ge(unit_loaded[m % RAW], b * 16 + loads_of(m))
                    act.wait_ge(units_done, u0 + (j - SPLIT_AGE[j % N_BLK] + 1))
                    nc.scalar.activation(w_hi[SPLIT_SLOT[j % N_BLK]][:], raw[m % RAW][:], ACT.Copy).then_inc(hi_split, 1)

                def par_of(n):
                    return st_par[:, pi[n]:pi[n] + 1]

                high(1)
                act.wait_ge(units_done, u0 + 1)
                act.wait_ge(conv_done, b + START)
                nc.scalar.activation(z[:, CONV - 1:], bank[0][:], ACT.Copy).then_inc(z_copied, 1)
                high(2)
                act.wait_ge(units_done, u0 + 2)
                act.wait_ge(merged_done, b + START)
                nc.scalar.activation(tmp["ga"][:], bank[1][:], ACT.Gelu_apprx_tanh).then_inc(gate_gelu, 1)
                high(3)
                act.wait_ge(units_done, u0 + 3)
                nc.scalar.activation(tmp["gu"][:], bank[2][:], ACT.Gelu_apprx_tanh).then_inc(u_gelu, 1)
                high(4)
                act.wait_ge(staged, b * 3 + 3)
                act.wait_ge(gates_done, b + 1 + START)
                nc.scalar.activation(tmp["r"][:], bank[5][:], ACT.Sigmoid, bias=par_of("lru_ba")).then_inc(ri_sig, 1)
                nc.scalar.activation(tmp["i"][:], bank[6][:], ACT.Sigmoid, bias=par_of("lru_bi")).then_inc(ri_sig, 1)
                act.wait_ge(ri_sig, b * 2 + 1 + START)
                nc.scalar.activation(tmp["th"][:], tmp["r"][:], ACT.Tanh, scale=par_of("half_c")).then_inc(tanh_done, 1)
                act.wait_ge(units_done, u0 + 4)
                nc.scalar.activation(tmp["sa"][:], bank[3][:], ACT.Sigmoid).then_inc(ma_sig, 1)
                if not last:
                    high(5)
                nc.scalar.activation(tmp["a"][:], tmp["r"][:], ACT.Exp, scale=par_of("neg_c")).then_inc(decay_ready, 1)
                act.wait_ge(tanh_done, b + 1)
                nc.scalar.activation(tmp["th"][:], tmp["th"][:], ACT.Sqrt).then_inc(root_ready, 1)
                act.wait_ge(units_done, u0 + 5)
                nc.scalar.activation(tmp["sb"][:], bank[4][:], ACT.Sigmoid).then_inc(mb_sig, 1)

            act.wait_ge(z_pad_ready, 1)
            with act.Fori(0, NB - 1) as b:
                channel_block(b, False)
            channel_block(NB - 1, True)

            for c in range(NC):
                act.wait_ge(x1_half, NC + c + 1)
                if c > 0:
                    act.wait_ge(squares2, c)
                nc.scalar.activation(junk2[:], x[:, c, :], ACT.Square, accum_out=stat[:, 24 + c:25 + c]).then_inc(squares2, 1)
                act.wait_ge(squares2, c + 1)
                nc.scalar.activation(stat[:, 28 + c:29 + c], stat[:, 24 + c:25 + c], ACT.Sqrt, bias=stat[:, 0:1],
                                     scale=1.0 / D).then_inc(std2_ready, 1)
                act.wait_ge(n2_ready, c + 1)
                act.dma_start(n2_rows[c * P:(c + 1) * P, :], n2[:, c, :, :].rearrange("p k n -> p (k n)")).then_inc(n2_stored, 16)
            act.wait_ge(group_shift, 1)
            nc.scalar.activation(t_g[:], t_g[:], ACT.Exp).then_inc(group_exp, 1)
            act.wait_ge(second_shift, 1)
            nc.scalar.activation(col[:, 5, :], col[:, 4, :], ACT.Exp).then_inc(second_exp, 1)
            act.wait_ge(jobs_ready, 1)

            def job(g):
                act.wait_ge(up_done, g + 1)
                act.wait_ge(hid_ready, g + START)
                nc.scalar.activation(sil[:], bank[0][:, 0:F], ACT.Silu).then_inc(silu_done, 1)
                act.wait_ge(hidT_done, g + 1 + START)
                nc.scalar.activation(hidT[:].rearrange("p c n -> p (c n)"), bank[3][:, 0:F], ACT.Copy).then_inc(hidT_ready, 1)
                act.wait_ge(down0_done, g + 1)
                act.wait_ge(y_free, g + START)
                nc.scalar.activation(y_sb[:, 0:HALF], bank[6][:], ACT.Copy).then_inc(y0_ready, 1)

            def split_high_ple(i):
                if i < NPK:
                    act.wait_ge(up_loaded, 16)
                    nc.scalar.activation(up_hi[:, i, :], up_raw[:, i, :], ACT.Copy).then_inc(ple_hi, 1)
                else:
                    k = i - NPK
                    act.wait_ge(gate_loaded[k // 2], 16)
                    nc.scalar.activation(gate_hi[:, k, :], gate_raw[:, k, :], ACT.Copy).then_inc(ple_hi, 1)

            last_pair = act.value_load(job_at_i[0:1, PAIRS - 1:PAIRS], min_val=PAIRS - 1, max_val=MAX_JOBS)
            with act.Fori(0, last_pair) as g:
                job(g)
            act.wait_ge(down1_done, last_pair)
            for i in range(N_MID):
                split_high_ple(i)
            jobs = act.value_load(job_at_i[0:1, PAIRS:PAIRS + 1], min_val=PAIRS, max_val=MAX_JOBS)
            with act.Fori(last_pair, jobs) as g:
                job(g)
            act.wait_ge(p_T, 1)
            for k in range(NPK):
                nc.scalar.activation(pT_hi[:, k, :], bank[4 + k][:], ACT.Copy).then_inc(pT_hi_ready, 1)
            for i in range(N_MID, N_PLE):
                split_high_ple(i)

            def norm3(c):
                act.wait_ge(x2_ready, c + 1)
                if c > 0:
                    act.wait_ge(squares3, c)
                nc.scalar.activation(junk3[:], x[:, c, :], ACT.Square, accum_out=stat[:, 36 + c:37 + c]).then_inc(squares3, 1)
                act.wait_ge(squares3, c + 1)
                nc.scalar.activation(stat[:, 40 + c:41 + c], stat[:, 36 + c:37 + c], ACT.Sqrt, bias=stat[:, 0:1],
                                     scale=1.0 / D).then_inc(std3_ready, 1)

            def high3(c):
                act.wait_ge(h3_ready, 2 * c + 2)
                if c >= 2:
                    act.wait_ge(gate_done, 2 * (c - 1))
                nc.scalar.activation(h3T_hi[c % 2][:], h3[:], ACT.Copy).then_inc(h3T_hi_ready, 1)

            def finish(c):
                for j in range(2):
                    act.wait_ge(gate_done, 2 * c + j + 1)
                    if c > 0:
                        act.wait_ge(x3_ready, 2 * c + j - 1)
                    nc.scalar.activation(sg[j][:], bank[2 * (c % 2) + j][:], ACT.Sigmoid).then_inc(gate_sig, 1)
                act.wait_ge(x3_ready, 2 * c + 2)
                act.wait_ge(squares3, NC)
                if c > 0:
                    act.wait_ge(squares4, c)
                nc.scalar.activation(junk3[:], x[:, c, :], ACT.Square, accum_out=stat[:, 44 + c:45 + c]).then_inc(squares4, 1)
                act.wait_ge(squares4, c + 1)
                nc.scalar.activation(stat[:, 48 + c:49 + c], stat[:, 44 + c:45 + c], ACT.Sqrt, bias=stat[:, 0:1],
                                     scale=1.0 / D).then_inc(std4_ready, 1)

            for c in range(NC):
                act.wait_ge(pu_done, c + 1)
                for j in range(2):
                    nc.scalar.activation(pu[:, c, HALF * j:HALF * (j + 1)], bank[2 * (c % 2) + j][:], ACT.Copy).then_inc(pu_ready, 1)
            norm3(0)
            norm3(1)
            high3(0)
            norm3(2)
            high3(1)
            norm3(3)
            for c in range(NC):
                finish(c)
                if c + 2 < NC:
                    high3(c + 2)

        @block.vector
        def _(dve):
            chain = [0]

            def link(ins):
                ins.then_inc(dve_chain, 1)
                chain[0] = chain[0] + 1
                dve.wait_ge(dve_chain, chain[0])

            tt, ts, stt = nc.vector.tensor_tensor, nc.vector.tensor_scalar, nc.vector.scalar_tensor_tensor
            for c in range(NC):
                dve.wait_ge(std_ready, c + 1)
                link(nc.vector.reciprocal(stat[:, 12 + c:13 + c], stat[:, 8 + c:9 + c]))
                ts(xn[:, c, :], x[:, c, :], stat[:, 12 + c:13 + c], None, ALU.mult).then_inc(xn_ready, 1)
                if c == 0:
                    dve.wait_ge(par_T, 1)
                    nc.vector.tensor_copy(par[:, 0:N_RAW, :].rearrange("p a b -> p (a b)"),
                                          bank[7][:, 0:N_RAW * NB]).then_inc(par_ready, 1)
            for h in range(2):
                dve.wait_ge(ws_T, h + 1)
                nc.vector.tensor_copy(wsT[:, 4 * h:4 * h + 4, :].rearrange("p a b -> p (a b)"), bank[h][:]).then_inc(wsT_ready, 1)
            for h in range(2):
                dve.wait_ge(rs_done, h + 1)
                nc.vector.tensor_copy(rs_b[:, 4 * h:4 * h + 4, :].rearrange("p a b -> p (a b)"), bank[2 + h][:]).then_inc(rs_ready, 1)

            def split_low(slot, n_hi):
                dve.wait_ge(hi_split, n_hi)
                tt(w_lo[slot[1]][:], raw[slot[0]][:], w_hi[slot[1]][:].bitcast(F32), ALU.subtract).then_inc(lo_split, 1)

            def split_low_v(n):
                split_low((n % RAW, split_slot(n)), n + 1)

            for n in range(SPLIT):
                split_low_v(n)
            for k in range(NK):
                dve.wait_ge(hT_hi_ready, k + 1)
                stt(hT_lo[:, k, :], bank[k][:], par[:, pi["mix_norm"], k:k + 1], hT_hi[:, k, :].bitcast(F32),
                    ALU.mult, ALU.subtract).then_inc(hT_lo_ready, 1)
            for n in range(3, N_V + 1):
                split_low_v(n)
            dve.wait_ge(v_gelu, 2 * NC)
            for c in range(NC):
                for h in range(2):
                    nc.vector.bn_stats(bn_s[:, c, h, :], vm[:, 4 * h:4 * h + 4, c * P:(c + 1) * P]).then_inc(dve_chain, 1)
                chain[0] += 2
                dve.wait_ge(dve_chain, chain[0])
                nc.vector.bn_aggr(bn_m[:, c, :], bn_s[:, c, :, :].rearrange("p h s -> p (h s)")).then_inc(v_var, 1)
            dve.wait_ge(v_std, 1)
            link(nc.vector.reciprocal(stat[:, 20:20 + NC], stat[:, 16:16 + NC]))
            for c in range(NC):
                vc = vm[:, :, c * P:(c + 1) * P]
                ts(vc, vc, bn_m[:, c, 0:1], stat[:, 20 + c:21 + c], ALU.subtract, ALU.mult).then_inc(v_normed, 1)
            dve.wait_ge(softplus_exp, 1)
            dve.wait_ge(par_ready, 1)
            e, s_, s2, q = sp_t[:, 1, :], sp_t[:, 2, :], sp_t[:, 3, :], sp_t[:, 4, :]
            link(ts(s_, e, 2.0, None, ALU.add))
            link(nc.vector.reciprocal(s_, s_))
            link(tt(s_, s_, e, ALU.mult))
            link(tt(s2, s_, s_, ALU.mult))
            link(ts(q, s2, 1.0 / 17, None, ALU.mult))
            for odd in (15, 13, 11, 9, 7, 5, 3):
                link(stt(q, q, 1.0 / odd, s2, ALU.add, ALU.mult))
            link(stt(q, q, 1.0, s_, ALU.add, ALU.mult))
            link(ts(s_, par[:, pi["lru_lambda"], :], -1.0, 0.0, ALU.mult, ALU.max))
            link(stt(q, q, 2.0, s_, ALU.mult, ALU.add))
            link(ts(par[:, pi["neg_c"], :], q, -LRU_C, None, ALU.mult))
            ts(par[:, pi["half_c"], :], q, LRU_C / 2, None, ALU.mult).then_inc(c_ready, 1)

            before = chain[0]
            LINKS = 11

            def channel_block(b, last):
                u0 = b * N_BLK + N_V
                chain[0] = b * LINKS + before

                def low(j):
                    m = N_V + j
                    split_low((m % RAW, SPLIT_SLOT[j % N_BLK]), u0 + (j + 1))

                def par_of(n):
                    return st_par[:, pi[n]:pi[n] + 1]

                xa, th, s = tmp["xa"], tmp["th"], tmp["s"]
                low(1)
                dve.wait_ge(staged, b * 3 + 1)
                dve.wait_ge(z_copied, b + 1 + START)
                dve.wait_ge(merged_done, b + START)
                link(ts(xa[:], z[:, CONV - 1:], par_of(f"conv_w{CONV - 1}"), par_of("conv_b"), ALU.mult, ALU.add))
                for t in (CONV - 2, CONV - 3):
                    link(stt(xa[:], z[:, t:t + T], par_of(f"conv_w{t}"), xa[:], ALU.mult, ALU.add))
                stt(xa[:], z[:, 0:T], par_of("conv_w0"), xa[:], ALU.mult, ALU.add).then_inc(conv_done, 1)
                low(2)
                low(3)
                low(4)
                dve.wait_ge(ri_sig, b * 2 + 2 + START)
                link(tt(tmp["i"][:], tmp["i"][:], xa[:], ALU.mult))
                dve.wait_ge(sgu_done, b + 1 + START)
                cb = lambda w: w[:, bass.ds(b, 1), :].broadcast_to((P, NC, P))
                s3 = s[:].rearrange("p (c n) -> p c n", c=NC)
                ins = stt(s3, bank[7][:].rearrange("p (c n) -> p c n", c=NC), par_of("sgu_ln_g"), cb(bs_b), ALU.mult, ALU.add)
                ins.then_inc(sp_evac, 1)
                dve.wait_ge(sp_evac, b + 1 + START)
                ins = stt(s3, cb(rs_b), par_of("sgu_ln_b"), s3, ALU.mult, ALU.add)
                ins.then_inc(sp_params, 1)
                dve.wait_ge(sp_params, b + 1 + START)
                dve.wait_ge(u_gelu, b + 1 + START)
                link(tt(s[:], s[:], tmp["gu"][:], ALU.mult))
                if not last:
                    low(5)
                dve.wait_ge(decay_ready, b + 1)
                dve.wait_ge(root_ready, b + 1 + START)
                link(stt(th[:], tmp["a"][:], 1.0, th[:], ALU.add, ALU.mult))
                link(tt(th[:], th[:], tmp["i"][:], ALU.mult))
                link(nc.vector.tensor_tensor_scan(xa[:], tmp["a"][:], th[:], 0.0, ALU.mult, ALU.add))
                link(tt(xa[:], xa[:], tmp["ga"][:], ALU.mult))
                link(tt(xa[:], xa[:], tmp["sa"][:], ALU.mult))
                dve.wait_ge(mb_sig, b + 1 + START)
                link(tt(s[:], s[:], tmp["sb"][:], ALU.mult))
                tt(vm[:, bass.ds(b, 1), :].rearrange("p a b -> p (a b)"), xa[:], s[:], ALU.add).then_inc(merged_done, 1)
                if isinstance(b, int):
                    assert chain[0] == b * LINKS + before + LINKS, chain[0] - before - b * LINKS

            def second_norm(c):
                dve.wait_ge(std2_ready, c + 1)
                link(nc.vector.reciprocal(stat[:, 32 + c:33 + c], stat[:, 28 + c:29 + c]))
                ts(n2[:, c, :, :], x[:, c, :].rearrange("t (p k) -> t k p", k=NK), stat[:, 32 + c:33 + c], None,
                   ALU.mult).then_inc(n2_ready, 1)
                dve.wait_ge(n2_T, c + 1)
                if c == 0:
                    dve.wait_ge(router_loaded, 16 * 5)
                    dve.wait_ge(tables_ready, 5)
                for h in range(2):
                    src = bank[2 * (c % 2) + h][:].rearrange("p (k t) -> p k t", k=4)
                    tt(h2T[:, 4 * h:4 * h + 4, c * P:(c + 1) * P], src,
                       g2[:, 4 * h:4 * h + 4].unsqueeze(2).broadcast_to((P, 4, P)), ALU.mult).then_inc(h2T_ready, 1)

            def first_of(one, score, top, ranks, v, vmax, n):
                bc = lambda a: a.unsqueeze(2).broadcast_to((P, NC, n))
                link(tt(score, v, bc(vmax), ALU.is_equal))
                link(tt(score, score, ranks.unsqueeze(1).broadcast_to((P, NC, n)), ALU.mult))
                link(nc.vector.tensor_reduce(top, score, axis=AX.X, op=ALU.max))
                link(tt(one, score, bc(top), ALU.is_equal))

            def route():
                red = nc.vector.tensor_reduce
                dve.wait_ge(router_done, NC)
                link(tt(lg[:], bank[4][:, 0:NC * NR].rearrange("p (c n) -> p c n", c=NC),
                        b_r[:].unsqueeze(1).broadcast_to((P, NC, NR)), ALU.add))
                gl = lg[:, :, 0:NG]
                link(red(col[:, 0, :], gl, axis=AX.X, op=ALU.max))
                tt(t_g[:], gl, col[:, 0, :].unsqueeze(2).broadcast_to((P, NC, NG)), ALU.subtract).then_inc(group_shift, 1)
                first_of(one_g[:], t_eg[:, :, 0, :], col[:, 1, :], rank_row[:, EG - NG:EG], gl, col[:, 0, :], NG)
                link(tt(t_eg[:], lg[:, :, NG:NR].rearrange("p c (g e) -> p c e g", g=NG),
                        one_g[:].unsqueeze(2).broadcast_to((P, NC, EG, NG)), ALU.mult))
                link(red(es[:], t_eg[:], axis=AX.X, op=ALU.add))
                link(red(col[:, 2, :], es[:], axis=AX.X, op=ALU.max))
                first_of(one1[:], t_e[:], col[:, 1, :], rank_row[:], es[:], col[:, 2, :], EG)
                link(stt(es2[:], one1[:], -1e30, es[:], ALU.mult, ALU.add))
                link(red(col[:, 3, :], es2[:], axis=AX.X, op=ALU.max))
                tt(col[:, 4, :], col[:, 3, :], col[:, 2, :], ALU.subtract).then_inc(second_shift, 1)
                first_of(one2[:], t_e[:], col[:, 1, :], rank_row[:], es2[:], col[:, 3, :], EG)
                for one, M in ((one1, M1), (one2, M2)):
                    link(tt(M[:].rearrange("p c (g e) -> p c g e", g=NG), one_g[:].unsqueeze(3).broadcast_to((P, NC, NG, EG)),
                            one[:].unsqueeze(2).broadcast_to((P, NC, NG, EG)), ALU.mult))
                tt(MM[:], M1[:], M2[:], ALU.add).then_inc(masks_ready, 1)
                dve.wait_ge(group_exp, 1)
                link(red(col[:, 6, :], t_g[:], axis=AX.X, op=ALU.add))
                link(nc.vector.reciprocal(col[:, 7, :], col[:, 6, :]))
                dve.wait_ge(second_exp, 1)
                link(ts(col[:, 8, :], col[:, 5, :], 1.0, None, ALU.add))
                link(nc.vector.reciprocal(col[:, 9, :], col[:, 8, :]))
                link(tt(col[:, 10, :], col[:, 7, :], col[:, 9, :], ALU.mult))
                link(tt(col[:, 11, :], col[:, 10, :], col[:, 5, :], ALU.mult))
                dve.wait_ge(pos_done, 1)
                dve.wait_ge(masks_ready, 1)
                link(stt(prod[:], bank[5][:, 0:NC * E].rearrange("p (c e) -> p c e", c=NC), 1.0, MM[:], ALU.add, ALU.mult))
                by_pair = lambda w: w[:].rearrange("p c (i t) -> p c i t", t=2)
                link(ts(posr[:].rearrange("p i c t -> p c i t"), by_pair(prod), -1.0, None, ALU.add))
                link(tt(prod[:], MM[:], tok_col[:].unsqueeze(2).broadcast_to((P, NC, E)), ALU.mult))
                link(stt(prod[:], M2[:], float(T), prod[:], ALU.mult, ALU.add))
                link(nc.vector.tensor_copy(dstr[:].rearrange("p i c t -> p c i t"), by_pair(prod)))
                select(0, 0)
                counts = bank[5][:, NC * E:(NC + 1) * E].rearrange("p (i t) -> p i t", t=2)
                link(red(reps_f[:], counts, axis=AX.X, op=ALU.max))
                link(ts(reps_i[:], reps_f[:], float(CAP - 1), None, ALU.add))
                link(ts(reps_i[:], reps_i[:], 6, None, ALU.arith_shift_right))
                link(nc.vector.tensor_copy(reps_f[:], reps_i[:]))
                link(ts(reps_f[:], reps_f[:], 1.0, None, ALU.max))
                link(nc.vector.memset(job_at[:, 0:1], 0.0))
                link(ts(pair_f[:, 0:PAIRS], reps_f[:], 0.0, 1.0, ALU.mult, ALU.add))
                link(nc.vector.tensor_tensor_scan(job_at[:, 1:], pair_f[:, 0:PAIRS], reps_f[:], 0.0, ALU.mult, ALU.add))
                link(nc.vector.tensor_copy(job_at_i[:], job_at[:]))
                bj = lambda a: a.unsqueeze(2).broadcast_to((P, JOBS, PAIRS))
                bp = lambda a: a.unsqueeze(1).broadcast_to((P, JOBS, PAIRS))
                link(tt(job_cmp[:], bj(job_row[:]), bp(job_at[:, 1:]), ALU.is_ge))
                link(red(pair_f[:], job_cmp[:], axis=AX.X, op=ALU.add))
                link(ts(pair_i[:], pair_f[:], float(PAIRS - 1), None, ALU.min))
                link(tt(job_cmp[:], job_cmp[:], bp(reps_f[:]), ALU.mult))
                link(red(job_off[:], job_cmp[:], axis=AX.X, op=ALU.add))
                link(tt(job_off[:], job_row[:], job_off[:], ALU.subtract))
                ts(job_off[:], job_off[:], float(CAP), None, ALU.mult).then_inc(jobs_ready, 1)

            def select(g, pair):
                if pair is None:
                    pair = dve.value_load(pair_i[0:1, bass.ds(g, 1)], min_val=0, max_val=PAIRS - 1)
                    ins = ts(iota_off[:], iota_row[:], job_off[:, bass.ds(g, 1)], None, ALU.add)
                    row = iota_off
                    ins.then_inc(off_ready, 1)
                    dve.wait_ge(off_ready, g)
                else:
                    row = iota_row
                at_pair = lambda w: w[:, bass.ds(pair, 1), :, :].rearrange("p i c t -> p (i c t)")
                nc.vector.tensor_copy(dst_st[:].rearrange("p c t -> p (c t)"), at_pair(dstr)).then_inc(sel_ready, 1)
                tt(sel[:], row[:].unsqueeze(1).broadcast_to((P, 2 * NC, CAP)),
                   at_pair(posr).unsqueeze(2).broadcast_to((P, 2 * NC, CAP)), ALU.is_equal).then_inc(sel_ready, 1)

            def indices(g):
                dve.wait_ge(idx_summed, g + 1)
                for e in range(2):
                    rows = slice(e * CAP, (e + 1) * CAP)
                    ts(row_z[rows, 0:1], bank[4][rows, e:e + 1], 0.0, float(4 * T), ALU.is_equal, ALU.mult).then_inc(row_z_ready, 1)
                    dve.wait_ge(row_z_ready, g * 2 + (e + 1))
                    stt(row_idx[rows, bass.ds(g, 1)], bank[4][rows, e:e + 1], -1.0, row_z[rows, 0:1],
                        ALU.add, ALU.add).then_inc(row_idx_ready, 1)
                dve.wait_ge(row_idx_ready, g * 2 + 2)
                ts(tok_idx[:, bass.ds(g, 1)], row_idx[:, bass.ds(g, 1)], 3 * T - 1, None, ALU.bitwise_and).then_inc(idx_ready, 1)

            def evacuate_gathered(g):
                dve.wait_ge(rows_T, g + 1)
                for h in range(2):
                    tt(gT[:, 4 * h:4 * h + 4, :], bank[1 + h][:].rearrange("p (k t) -> p k t", k=4),
                       g2[:, 4 * h:4 * h + 4].unsqueeze(2).broadcast_to((P, 4, P)), ALU.mult).then_inc(gT_ready, 1)

            def job(g):
                dve.wait_ge(silu_done, g + 1)
                dve.wait_ge(hidT_done, g + START)
                tt(hid[:], sil[:], bank[0][:, F:2 * F], ALU.mult).then_inc(hid_ready, 1)
                evacuate_gathered(g + 1)
                indices(g + 2)
                select(g + 3, None)
                dve.wait_ge(down1_done, g + 1)
                dve.wait_ge(y_free, g + START)
                nc.vector.tensor_copy(y_sb[:, HALF:D], bank[7][:]).then_inc(y1_ready, 1)

            def split_low_ple(i):
                dve.wait_ge(ple_hi, i + 1)
                k = i - NPK
                raw_w, hi, lo = (up_raw[:, i, :], up_hi[:, i, :], up_lo[:, i, :]) if i < NPK else (
                    gate_raw[:, k, :], gate_hi[:, k, :], gate_lo[:, k, :])
                tt(lo, raw_w, hi.bitcast(F32), ALU.subtract).then_inc(ple_lo, 1)

            def experts():
                indices(0)
                select(1, None)
                indices(1)
                select(2, None)
                evacuate_gathered(0)
                last_pair = dve.value_load(job_at_i[0:1, PAIRS - 1:PAIRS], min_val=PAIRS - 1, max_val=MAX_JOBS)
                with dve.Fori(0, last_pair) as g:
                    job(g)
                for i in range(N_MID):
                    split_low_ple(i)
                jobs = dve.value_load(job_at_i[0:1, PAIRS:PAIRS + 1], min_val=PAIRS, max_val=MAX_JOBS)
                with dve.Fori(last_pair, jobs) as g:
                    job(g)

            def ple():
                for k in range(NPK):
                    dve.wait_ge(pT_hi_ready, k + 1)
                    tt(pT_lo[:, k, :], bank[4 + k][:], pT_hi[:, k, :].bitcast(F32), ALU.subtract).then_inc(pT_lo_ready, 1)
                for i in range(N_MID, N_PLE):
                    split_low_ple(i)

                def norm3(c):
                    dve.wait_ge(yg_loaded[c], 32)
                    link(stt(x[:, c, :], yg[c][0][:], col[:, 10, c:c + 1], x[:, c, :], ALU.mult, ALU.add))
                    stt(x[:, c, :], yg[c][1][:], col[:, 11, c:c + 1], x[:, c, :], ALU.mult, ALU.add).then_inc(x2_ready, 1)
                    dve.wait_ge(std3_ready, c + 1)
                    link(nc.vector.reciprocal(stat[:, 52 + c:53 + c], stat[:, 40 + c:41 + c]))
                    dve.wait_ge(x2_ready, c + 1)
                    ts(n3[c][:], x[:, c, :], stat[:, 52 + c:53 + c], None, ALU.mult).then_inc(n3_ready, 1)

                def low3(c):
                    dve.wait_ge(n3_T, c + 1)
                    if c > 0:
                        dve.wait_ge(h3T_lo_ready, c)
                    for h in range(2):
                        g3 = par[:, pi["ple_norm"], 4 * h:4 * h + 4]
                        tt(h3[:, 4 * h:4 * h + 4, :], bank[6 + h][:].rearrange("p (k t) -> p k t", k=4),
                           g3.unsqueeze(2).broadcast_to((P, 4, P)), ALU.mult).then_inc(h3_ready, 1)
                    dve.wait_ge(h3T_hi_ready, c + 1)
                    tt(h3T_lo[c % 2][:], h3[:], h3T_hi[c % 2][:].bitcast(F32), ALU.subtract).then_inc(h3T_lo_ready, 1)

                def finish(c):
                    dve.wait_ge(pu_ready, 2 * c + 2)
                    for j in range(2):
                        dve.wait_ge(gate_sig, 2 * c + j + 1)
                        ps = pu[:, c, HALF * j:HALF * (j + 1)]
                        xs = x[:, c, HALF * j:HALF * (j + 1)]
                        link(tt(ps, sg[j][:], ps, ALU.mult))
                        tt(xs, xs, ps, ALU.add).then_inc(x3_ready, 1)
                    dve.wait_ge(std4_ready, c + 1)
                    dve.wait_ge(fn_loaded, 16)
                    link(nc.vector.reciprocal(stat[:, 56 + c:57 + c], stat[:, 48 + c:49 + c]))
                    stt(o_sb[c][:], x[:, c, :], stat[:, 56 + c:57 + c], fn_b[:], ALU.mult, ALU.mult).then_inc(out_ready, 1)

                norm3(0)
                norm3(1)
                low3(0)
                norm3(2)
                low3(1)
                norm3(3)
                for c in range(NC):
                    finish(c)
                    if c + 2 < NC:
                        low3(c + 2)

            dve.wait_ge(bs_loaded, 16)
            dve.wait_ge(rs_ready, 2)
            with dve.Fori(0, NB - 1) as b:
                channel_block(b, False)
            channel_block(NB - 1, True)
            for j in range(2):
                for c in range(NC):
                    if j == 0:
                        dve.wait_ge(units_done, U_WOUT + 4)
                    else:
                        dve.wait_ge(wout_done, c + 1)
                    xs = x[:, c, HALF * j:HALF * (j + 1)]
                    tt(xs, xs, bank[4 * j + c][:], ALU.add).then_inc(x1_half, 1)
                    if j == 1:
                        second_norm(c)
            route()
            experts()
            ple()

        @block.tensor
        def _(pe):
            mm, tr = nc.tensor.matmul, nc.tensor.transpose

            pe.wait_ge(ident_ready, 1)
            pe.wait_ge(par_loaded, 16 * N_RAW)
            tr(bank[7][:, 0:N_RAW * NB], par_raw[:], ident[0:N_RAW * NB, 0:N_RAW * NB]).then_inc(par_T, 1)
            pe.wait_ge(ws_masked, 1)
            for g in range(NB):
                last = tr(bank[g // 4][:, (g % 4) * P:(g % 4 + 1) * P], ws_raw[:, g, :], ident[:])
                if g % 4 == 3:
                    last.then_inc(ws_T, 1)
            pe.wait_ge(ones_ready, 1)
            for h in range(2):
                pe.wait_ge(wsT_ready, h + 1)
                mm(bank[2 + h][:], ones[:], wsT[:, 4 * h:4 * h + 4, :].rearrange("p a b -> p (a b)"),
                   start=True, stop=True).then_inc(rs_done, 1)
            pe.wait_ge(par_ready, 1)
            pe.wait_ge(rs_ready, 2)
            for c in range(NC):
                pe.wait_ge(xn_ready, c + 1)
                for k in range(NK):
                    last = tr(bank[k][:, c * P:(c + 1) * P], xn[:, c, k * P:(k + 1) * P], ident[:])
                last.then_inc(x_T, 1)

            def products(dst, hi_s, lo_s, hi_m, lo_m, start, stop):
                mm(dst, hi_s, hi_m, start=start, stop=False)
                mm(dst, hi_s, lo_m, start=False, stop=False)
                return mm(dst, lo_s, hi_m, start=False, stop=stop)

            for n in range(N_V):
                j, q = n // 4, n % 4
                pe.wait_ge(lo_split, n + 1)
                if n == 0:
                    pe.wait_ge(hT_lo_ready, 4)
                if n in (1, 2, 3, 4):
                    pe.wait_ge(hT_lo_ready, min(2 * n + 2, NK))
                s = split_slot(n)
                for c in range(NC):
                    for kk in range(2):
                        k = 2 * q + kk
                        cs = slice(c * P, (c + 1) * P)
                        ms = slice(kk * HALF, (kk + 1) * HALF)
                        last = products(bank[4 * j + c][:], hT_hi[:, k, cs], hT_lo[:, k, cs], w_hi[s][:, ms], w_lo[s][:, ms],
                                        k == 0, k == NK - 1)
                last.then_inc(units_done, 1)

            freed = [z_copied, gate_gelu, u_gelu, ma_sig, mb_sig]
            pe.wait_ge(v_gelu, 2 * NC)
            with pe.Fori(0, NB) as b:
                u0 = b * N_BLK + N_V
                for j in range(N_BLK):
                    pe.wait_ge(lo_split, u0 + (j + 1))
                    pe.wait_ge(freed[j], b + START)
                    s = SPLIT_SLOT[j]
                    for k in range(NK):
                        cs = slice(k * P, (k + 1) * P)
                        last = products(bank[j][:], w_hi[s][:, cs], w_lo[s][:, cs], hT_hi[:, k, :], hT_lo[:, k, :],
                                        k == 0, k == NK - 1)
                    last.then_inc(units_done, 1)
                    if j == 1:
                        pe.wait_ge(conv_done, b + 1 + START)
                        pe.wait_ge(staged, b * 3 + 3)
                        pe.wait_ge(ri_sig, b * 2 + START)
                        mm(bank[5][:], st_wa[:], tmp["xa"][:], start=True, stop=True)
                        mm(bank[6][:], st_wi[:], tmp["xa"][:], start=True, stop=True).then_inc(gates_done, 1)
                    if j == 2:
                        pe.wait_ge(staged_v, b * 2 + 2)
                        pe.wait_ge(sp_evac, b + START)
                        for c in range(NC):
                            last = mm(bank[7][:, c * P:(c + 1) * P], st_v[:, c, :], st_ws[:], start=True, stop=True)
                        last.then_inc(sgu_done, 1)
            for q in range(4):
                n = U_WOUT + q
                pe.wait_ge(unit_loaded[n % RAW], loads_of(n))
                pe.wait_ge(merged_done, 2 * q + 2 + START)
                if q == 0:
                    for s in freed[:4]:
                        pe.wait_ge(s, NB + START)
                for c in range(NC):
                    for kk in range(2):
                        k = 2 * q + kk
                        last = mm(bank[c][:], vm[:, k, c * P:(c + 1) * P], raw[n % RAW][:, kk * HALF:(kk + 1) * HALF],
                                  start=(k == 0), stop=(k == NK - 1))
                last.then_inc(units_done, 1)
            pe.wait_ge(mb_sig, NB + START)
            pe.wait_ge(ri_sig, 2 * NB + START)
            pe.wait_ge(sp_evac, NB + START)

            def second_half(c):
                for q in range(4):
                    n = U_WOUT + 4 + q
                    if c == 0:
                        pe.wait_ge(unit_loaded[n % RAW], loads_of(n))
                    for kk in range(2):
                        k = 2 * q + kk
                        last = mm(bank[4 + c][:], vm[:, k, c * P:(c + 1) * P], raw[n % RAW][:, kk * HALF:(kk + 1) * HALF],
                                  start=(k == 0), stop=(k == NK - 1))
                last.then_inc(wout_done, 1)

            def transpose_n2(c):
                pe.wait_ge(n2_ready, c + 1)
                if c >= 2:
                    pe.wait_ge(h2T_ready, 2 * (c - 1))
                for k in range(NK):
                    last = tr(bank[2 * (c % 2) + k // 4][:, (k % 4) * P:(k % 4 + 1) * P], n2[:, c, k, :], ident[:])
                last.then_inc(n2_T, 1)

            def router(c):
                pe.wait_ge(h2T_ready, 2 * c + 2)
                for k in range(NK):
                    last = mm(bank[4][:, c * NR:(c + 1) * NR], h2T[:, k, c * P:(c + 1) * P], w_r[:, k, :],
                              start=(k == 0), stop=(k == NK - 1))
                last.then_inc(router_done, 1)

            second_half(0)
            second_half(1)
            pe.wait_ge(x1_half, NC + 1)
            transpose_n2(0)
            second_half(2)
            transpose_n2(1)
            second_half(3)
            for c in range(NC):
                if c >= 2:
                    transpose_n2(c)
                router(c)
            pe.wait_ge(masks_ready, 1)
            pe.wait_ge(x1_half, NC + 2)
            for c in range(NC + 1):
                for cc in range(min(c + 1, NC)):
                    m = upper if cc == c else ones
                    last = mm(bank[5][:, c * E:(c + 1) * E], m[:], MM[:, cc, :], start=(cc == 0), stop=(cc == min(c, NC - 1)))
            last.then_inc(pos_done, 1)

            def index_sums(g):
                pe.wait_ge(sel_ready, g * 2 + 2)
                if not isinstance(g, int) or g > 0:
                    pe.wait_ge(idx_ready, g)
                for c in range(NC):
                    last = mm(bank[4][:, 0:2], sel[:, 2 * c:2 * c + 2, :].rearrange("p e n -> p (e n)"), dst_st[:, c, :],
                              start=(c == 0), stop=(c == NC - 1))
                last.then_inc(idx_summed, 1)

            def transpose_rows(g):
                pe.wait_ge(rows_loaded, g * 16 + 16)
                if not isinstance(g, int):
                    pe.wait_ge(gT_ready, g * 2)
                for k in range(NK):
                    last = tr(bank[1 + k // 4][:, (k % 4) * P:(k % 4 + 1) * P], rows_sb[:, k, :], ident[:])
                last.then_inc(rows_T, 1)

            pe.wait_ge(h2T_ready, 2 * NC)
            index_sums(0)
            index_sums(1)
            transpose_rows(0)
            pe.wait_ge(jobs_ready, 1)
            rows = [slice(0, CAP), slice(CAP, P)]

            def job(g, s, h):
                pe.wait_ge(gT_ready, g * 2 + 2)
                pe.wait_ge(hid_ready, g + START)
                for i in range(4):
                    pe.wait_ge(pair_loaded[s][i], h * 16 + 16)
                for k in range(NK):
                    for e in range(2):
                        last = mm(bank[0][rows[e], :], gT[:, k, rows[e]], w13[s][e][:, k, :, :].rearrange("p m f -> p (m f)"),
                                  start=(k == 0), stop=(k == NK - 1))
                last.then_inc(up_done, 1)
                index_sums(g + 2)
                transpose_rows(g + 1)
                pe.wait_ge(hid_ready, g + 1 + START)
                pe.wait_ge(hidT_ready, g + START)
                for f in range(FC):
                    last = tr(bank[3][:, f * P:(f + 1) * P], hid[:, f * P:(f + 1) * P], ident[:])
                last.then_inc(hidT_done, 1)
                pe.wait_ge(hidT_ready, g + 1 + START)
                for i in (4, 5):
                    pe.wait_ge(pair_loaded[s][i], h * 16 + 16)
                for j in range(2):
                    pe.wait_ge((y0_ready, y1_ready)[j], g + START)
                    for f in range(FC):
                        for e in range(2):
                            last = mm(bank[6 + j][rows[e], :], hidT[:, f, rows[e]], w2[s][:, e, f, HALF * j:HALF * (j + 1)],
                                      start=(f == 0), stop=(f == FC - 1))
                    last.then_inc((down0_done, down1_done)[j], 1)

            def pair_jobs(s, pair, h):
                first, end = (pe.value_load(job_at_i[0:1, bass.ds(pair + i, 1)], min_val=0, max_val=MAX_JOBS) for i in range(2))
                with pe.Fori(first, end) as g:
                    job(g, s, h)

            with pe.Fori(0, PAIRS // 3) as h:
                for s in range(3):
                    pair_jobs(s, h * 3 + s, h)
            pair_jobs(LAST_SLOT, PAIRS - 1, PAIRS // 3)
            jobs = pe.value_load(job_at_i[0:1, PAIRS:PAIRS + 1], min_val=PAIRS, max_val=MAX_JOBS)
            pe.wait_ge(p_loaded, 16)
            pe.wait_ge(idx_ready, jobs + 2)
            for k in range(NPK):
                for c in range(NC):
                    last = tr(bank[4 + k][:, c * P:(c + 1) * P], p_sb[:, c, k * P:(k + 1) * P], ident[:])
            last.then_inc(p_T, 1)
            pe.wait_ge(hid_ready, jobs + START)
            pe.wait_ge(gT_ready, jobs * 2 + 2)
            pe.wait_ge(hidT_ready, jobs + START)
            pe.wait_ge(pT_lo_ready, NPK)
            pe.wait_ge(ple_lo, NPK)
            for c in range(NC):
                if c >= 2:
                    pe.wait_ge(pu_ready, 2 * (c - 1))
                for j in range(2):
                    for k in range(NPK):
                        cs, ms = slice(c * P, (c + 1) * P), slice(j * HALF, (j + 1) * HALF)
                        last = products(bank[2 * (c % 2) + j][:], pT_hi[:, k, cs], pT_lo[:, k, cs], up_hi[:, k, ms],
                                        up_lo[:, k, ms], k == 0, k == NPK - 1)
                last.then_inc(pu_done, 1)
            pe.wait_ge(y0_ready, jobs + START)
            pe.wait_ge(y1_ready, jobs + START)

            def transpose_n3(c):
                pe.wait_ge(n3_ready, c + 1)
                if c > 0:
                    pe.wait_ge(h3_ready, 2 * c)
                for k in range(NK):
                    last = tr(bank[6 + k // 4][:, (k % 4) * P:(k % 4 + 1) * P], n3[c][:, k * P:(k + 1) * P], ident[:])
                last.then_inc(n3_T, 1)

            transpose_n3(0)
            transpose_n3(1)
            for c in range(NC):
                if c == 0:
                    pe.wait_ge(ple_lo, N_PLE)
                pe.wait_ge(h3T_lo_ready, c + 1)
                if c < 2:
                    pe.wait_ge(pu_ready, 2 * (c + 3))
                else:
                    pe.wait_ge(gate_sig, 2 * (c - 1))
                for j in range(2):
                    for k in range(NK):
                        ms = slice(j * HALF, (j + 1) * HALF)
                        last = products(bank[2 * (c % 2) + j][:], h3T_hi[c % 2][:, k, :], h3T_lo[c % 2][:, k, :],
                                        gate_hi[:, k, ms], gate_lo[:, k, ms], k == 0, k == NK - 1)
                    last.then_inc(gate_done, 1)
                    if j == 0 and 0 < c < NC - 1:
                        transpose_n3(c + 1)

def kernel(**inputs):
    import numpy as _np
    import concourse.bacc as _bacc
    from concourse import mybir as _mybir
    from concourse.bass_utils import run_bass_kernel_spmd as _run

    nc = _bacc.Bacc("TRN2", target_bir_lowering=False, num_devices=1)
    arrays, args = {}, {}
    for name, a in inputs.items():
        a = _np.ascontiguousarray(a)
        arrays[f"in_{name}_dram"] = a
        args[name] = nc.dram_tensor(f"in_{name}_dram", a.shape, _mybir.dt.from_np(a.dtype), kind="ExternalInput").ap()
    shape = inputs["x"].shape
    out = nc.dram_tensor("out_dram", shape, _mybir.dt.float32, kind="ExternalOutput").ap()
    y_rows = nc.dram_tensor("y_rows", (2 * shape[1], shape[2]), _mybir.dt.float32).ap()
    n2_rows = nc.dram_tensor("n2_rows", shape[1:], _mybir.dt.float32).ap()
    hybrid_block_program(nc, args, n2_rows, y_rows, out)
    r = _run(nc, [arrays], core_ids=[0])
    return r.results[0]["out_dram"]
```

```python
from contextlib import ExitStack

import concourse.bass as bass
from concourse import mybir

F32 = mybir.dt.float32
F32R = mybir.dt.float32r
I32 = mybir.dt.int32
U32 = mybir.dt.uint32
U8 = mybir.dt.uint8
ALU = mybir.AluOpType
ACT = mybir.ActivationFunctionType
AX = mybir.AxisListType

P = 128
KIB = 1024
EPS = 1e-6
LRU_C = 8.0


def hybrid_block_program(nc, A, n2_rows, y_rows, out):
    T, D = A["x"].shape[1:]
    NC = T // P
    NK = D // P
    HALF = D // 2
    PLE = A["p"].shape[3]
    NPK = PLE // P
    E, F = A["expert_w1"].shape[1], A["expert_w1"].shape[3]
    NG = A["router_group_w"].shape[2]
    EG = E // NG
    NR = NG + E
    FC = F // P
    CAP = P // 2
    PAIRS = E // 2
    MAX_JOBS = PAIRS + 2 * T // CAP - 1
    JOBS = MAX_JOBS + 3
    CONV = A["conv_w"].shape[1]
    NB = A["sgu_ws"].shape[1]
    HB = A["lru_wa"].shape[2]
    assert (D, T, NB * P, NC) == (1024, 512, D, 4) and HB * 2 == P and T * 2 == E * 32

    w_in = A["w_in"][0].rearrange("(k p) n -> p k n", p=P)
    w_out = A["w_out"][0].rearrange("(k p) n -> p k n", p=P)
    ple_gate = A["ple_gate_w"][0].rearrange("(k p) n -> p k n", p=P)
    ple_up = A["ple_up_w"][0].rearrange("(k p) n -> p k n", p=P)
    V_COL = 3 * D
    BLOCK_COLS = [0, D, 2 * D, 4 * D, 5 * D]

    PAR = ["mix_norm", "conv_w0", "conv_w1", "conv_w2", "conv_w3", "conv_b", "lru_ba", "lru_bi", "lru_lambda",
           "sgu_ln_g", "sgu_ln_b", "ffn_norm", "ple_norm"]
    PAR_INPUTS = [n for n in PAR if not n.startswith("conv_w")] + ["conv_w"]
    pi = {n: i for i, n in enumerate(PAR)}
    N_RAW = len(PAR)
    pi["neg_c"], pi["half_c"] = N_RAW, N_RAW + 1
    N_PAR = N_RAW + 2

    RING = 5
    N_V, N_BLK = 8, 5
    U_WOUT = N_V + N_BLK * NB
    N_UNITS = U_WOUT + 8

    ctx = ExitStack()
    with ctx:
        base = nc.sbuf_base
        base += -base % 64
        ARENA = 207 * KIB
        ctx.enter_context(nc.sbuf_tensor("arena", [P, ARENA], U8))

        def at(name, off, shape, dt=F32):
            n = 4
            for s in shape[1:]:
                n *= s
            assert off + n <= ARENA, name
            return nc.alloc_sbuf_tensor_at(name, shape, dt, offset=base + off)

        K = KIB
        x = at("x_res", 0, [P, NC, D])
        raw = [at(f"raw{i}", (16 + 4 * i) * K, [P, D]) for i in range(RING)]
        w_lo = [at(f"w_lo{i}", (16 + 4 * i) * K, [P, D], F32R) for i in range(RING)]
        w_hi = [at(f"w_hi{i}", (36 + 4 * i) * K, [P, D], F32R) for i in range(RING)]
        hT_hi = at("hT_hi", 108 * K, [P, NK, T], F32R)
        hT_lo = at("hT_lo", 124 * K, [P, NK, T], F32R)
        xn = at("xn", 140 * K, [P, NC, D])
        vm = at("v", 140 * K, [P, NB, T])
        m_hi = at("merged_hi", 140 * K, [P, NB, T], F32R)
        m_lo = at("merged_lo", 92 * K, [P, NB, T], F32R)
        o = 156 * K
        tmp = {}
        for n in ["xa", "r", "i", "a", "th", "ga", "gu", "sa", "sb", "s"]:
            tmp[n] = at("t_" + n, o, [P, T])
            o += 2 * K
        z = at("z_lru", o, [P, T + CONV - 1])
        o += 2112
        wa_bd = at("wa_bd", o, [P, NB, P]); o += 4 * K
        wi_bd = at("wi_bd", o, [P, NB, P]); o += 4 * K
        wsT = at("wsT", o, [P, NB, P]); o += 4 * K
        bs_b = at("bs_b", o, [P, NB, P]); o += 4 * K
        rs_b = at("rs_b", o, [P, NB, P]); o += 4 * K
        st_v = at("st_v", o, [P, NC, P]); o += 2 * K
        st_wa = at("st_wa", o, [P, P]); o += 512
        st_wi = at("st_wi", o, [P, P]); o += 512
        st_ws = at("st_ws", o, [P, P]); o += 512
        st_par = at("st_par", o, [P, N_PAR]); o += 64
        ws_raw = at("ws_raw", 160 * K, [P, NB, P])
        par_raw = at("par_raw", 164 * K, [N_RAW * NB, P])
        sq_junk = at("sq_junk", 166 * K, [P, D])
        n2 = at("n2", 172 * K, [P, NC, NK, P])
        junk2 = at("junk2", 188 * K, [P, D])
        h2T = at("h2T", 140 * K, [P, NK, T])
        w13 = [[at(f"w13_{s}{e}", (o + 16 * e) * K, [P, 2, NK, F]) for e in range(2)] for s, o in enumerate((60, 108, 16))]
        w2 = [at(f"w2_{s}", o * K, [P, 2, FC, D]) for s, o in enumerate((92, 140, 156))]
        sel = at("sel", 48 * K, [P, NC * 2, CAP], F32R)
        y_sb = at("y_sb", 50 * K, [P, D])
        sil = at("sil", 54 * K, [P, F])
        hid = at("hid", 55 * K, [P, F])
        hidT = at("hidT", 56 * K, [P, FC, P])
        upper_r = at("upper_r", 57 * K, [P, P], F32R)
        ones_r = at("ones_r", 57 * K + 512, [P, P], F32R)
        job_cmp = at("job_cmp", 50 * K, [P, JOBS, PAIRS])
        rows_sb = at("rows_sb", 180 * K, [P, NK, P])
        gT = at("gT", 184 * K, [P, NK, P])
        o2 = 192 * K

        def table(name, shape, dt=F32):
            nonlocal o2
            t = at(name, o2, [P] + shape, dt)
            n = 4
            for q in shape:
                n *= q
            o2 += -(-n // 32) * 32
            return t

        w_r = table("w_router", [NK, NR])
        b_r = table("b_router", [NR])
        g2 = table("ffn_norm_cols", [NK])
        upper = table("upper", [P])
        iota_row = table("iota_row", [CAP])
        rank_row = table("rank_row", [EG])
        lg = table("lg", [NC, NR])
        t_g = table("t_g", [NC, NG])
        one_g = table("one_g", [NC, NG])
        t_eg = table("t_eg", [NC, EG, NG])
        es = table("es", [NC, EG])
        es2 = table("es2", [NC, EG])
        t_e = table("t_e", [NC, EG])
        one1 = table("one1", [NC, EG])
        one2 = table("one2", [NC, EG])
        col = table("col", [16, NC])
        M1 = table("M1", [NC, E])
        M2 = table("M2", [NC, E])
        MM = table("MM", [NC, E], F32R)
        prod = table("prod", [NC, E])
        posr = table("posr", [PAIRS, NC, 2])
        dstr = table("dstr", [PAIRS, NC, 2])
        dst_st = table("dst_st", [NC, 2], F32R)
        tok_col = table("tok_col", [NC])
        job_row = table("job_row", [JOBS])
        iota_off = table("iota_off", [CAP])
        reps_i = table("reps_i", [PAIRS], I32)
        reps_f = table("reps_f", [PAIRS])
        job_at = table("job_at", [PAIRS + 1])
        job_at_i = table("job_at_i", [PAIRS + 1], I32)
        pair_f = table("pair_f", [JOBS])
        pair_i = table("pair_i", [JOBS], I32)
        job_off = table("job_off", [JOBS])
        row_idx = table("row_idx", [JOBS], U32)
        row_z = table("row_z", [2])
        tok_idx = table("tok_idx", [JOBS], U32)
        src_st = table("src_st", [1], U32)
        dst_idx_st = table("dst_idx_st", [1], U32)
        assert o2 <= o, (o2, o)
        gate_raw = at("gate_raw", 108 * K, [P, NK, D])
        gate_lo = at("gate_lo", 108 * K, [P, NK, D], F32R)
        gate_hi = at("gate_hi", 16 * K, [P, NK, D], F32R)
        up_raw = at("up_raw", 172 * K, [P, NPK, D])
        up_lo = at("up_lo", 172 * K, [P, NPK, D], F32R)
        up_hi = at("up_hi", 156 * K, [P, NPK, D], F32R)
        p_sb = at("p_sb", 188 * K, [P, NC, PLE])
        fn_b = at("fn_b", 140 * K, [P, D])
        pT_hi = at("pT_hi", 164 * K, [P, NPK, T], F32R)
        pT_lo = at("pT_lo", 168 * K, [P, NPK, T], F32R)
        pu = at("pu", 60 * K, [P, NC, D])
        yg = [[at(f"yg{c}{t}", (76 + 8 * c + 4 * t) * K, [P, D]) for t in range(2)] for c in range(NC)]
        o_sb = [at(f"o_sb{c}", (76 + 8 * c) * K, [P, D]) for c in range(NC)]
        h3 = at("h3", 52 * K, [P, NK, P])
        sg = [at(f"sg{i}", (56 + 2 * i) * K, [P, HALF]) for i in range(2)]
        h3T_hi = [at(f"h3T_hi{i}", (172 + 8 * i) * K, [P, NK, P], F32R) for i in range(2)]
        h3T_lo = [at(f"h3T_lo{i}", (176 + 8 * i) * K, [P, NK, P], F32R) for i in range(2)]
        junk3 = at("junk3", 188 * K, [P, D])
        ident = at("ident", o, [P, P]); o += 512
        ones = at("ones", o, [P, P]); o += 512
        par = at("par", o, [P, N_PAR, NB]); o += 480
        stat = at("stat", o, [P, 64]); o += 256
        sp_t = at("sp_t", o, [P, 6, NB]); o += 192
        bn_s = at("bn_s", o, [P, NC, 2, 6]); o += 192
        bn_m = at("bn_m", o, [P, NC, 2]); o += 32
        assert o <= ARENA, o

        bank = [ctx.enter_context(nc.psum_tensor(f"bank{i}", [P, 512], F32)) for i in range(8)]

        def sem(name):
            return ctx.enter_context(nc.semaphore(name))

        x_loaded = [sem(f"x_loaded{c}") for c in range(NC)]
        par_loaded, ws_loaded, bs_loaded, lruw_loaded = sem("par_loaded"), sem("ws_loaded"), sem("bs_loaded"), sem("lruw_loaded")
        unit_loaded = [sem(f"unit_loaded{i}") for i in range(RING)]
        stored = sem("stored")
        ident_ready, ones_ready, zeroed, ws_masked = sem("ident_ready"), sem("ones_ready"), sem("zeroed"), sem("ws_masked")
        eps_ready, z_pad_ready = sem("eps_ready"), sem("z_pad_ready")
        par_T, par_ready, ws_T, wsT_ready, rs_done, rs_ready = (sem(n) for n in ["par_T", "par_ready", "ws_T", "wsT_ready", "rs_done", "rs_ready"])
        squares, std_ready, xn_ready, x_T, hT_hi_ready, hT_lo_ready = (sem(n) for n in ["squares", "std_ready", "xn_ready", "x_T", "hT_hi_ready", "hT_lo_ready"])
        hi_split, lo_split, units_done = sem("hi_split"), sem("lo_split"), sem("units_done")
        v_gelu, v_var, v_std, v_normed = sem("v_gelu"), sem("v_var"), sem("v_std"), sem("v_normed")
        c_ready, softplus_abs, softplus_exp = sem("c_ready"), sem("softplus_abs"), sem("softplus_exp")
        staged, staged_v = sem("staged"), sem("staged_v")
        z_copied, conv_done, gates_done, gate_gelu, u_gelu = (sem(n) for n in ["z_copied", "conv_done", "gates_done", "gate_gelu", "u_gelu"])
        ri_sig, tanh_done, ma_sig, decay_ready, root_ready, mb_sig = (sem(n) for n in ["ri_sig", "tanh_done", "ma_sig", "decay_ready", "root_ready", "mb_sig"])
        sgu_done, sp_evac, sp_params, merged_done = sem("sgu_done"), sem("sp_evac"), sem("sp_params"), sem("merged_done")
        m_hi_ready, m_lo_ready = sem("m_hi_ready"), sem("m_lo_ready")
        y_free = sem("y_free")
        dve_chain, pool_passed = sem("dve_chain"), sem("pool_passed")
        wout_done, x1_half = sem("wout_done"), sem("x1_half")
        squares2, std2_ready, n2_ready, n2_stored, x1_T, h2T_ready, router_done = (sem(n) for n in [
            "squares2", "std2_ready", "n2_ready", "n2_stored", "x1_T", "h2T_ready", "router_done"])
        router_loaded, tables_ready, group_shift, group_exp, second_shift, second_exp = (sem(n) for n in [
            "router_loaded", "tables_ready", "group_shift", "group_exp", "second_shift", "second_exp"])
        counters_ready = sem("counters_ready")
        masks_ready, pos_done, jobs_ready = sem("masks_ready"), sem("pos_done"), sem("jobs_ready")
        pair_loaded = [[sem(f"pair_loaded{s}{i}") for i in range(6)] for s in range(3)]
        sel_ready, idx_summed, rows_cleared, rows_loaded, rows_T, gT_ready, up_done, silu_done, hid_ready, hidT_done, hidT_ready = (sem(n) for n in [
            "sel_ready", "idx_summed", "rows_cleared", "rows_loaded", "rows_T", "gT_ready", "up_done", "silu_done", "hid_ready", "hidT_done", "hidT_ready"])
        down0_done, down1_done, y0_ready, y1_ready = sem("down0_done"), sem("down1_done"), sem("y0_ready"), sem("y1_ready")
        y_stored, idx_ready, src_staged, dst_staged, off_ready, row_z_ready, row_idx_ready = (sem(n) for n in [
            "y_stored", "idx_ready", "src_staged", "dst_staged", "off_ready", "row_z_ready", "row_idx_ready"])
        yg_loaded = [sem(f"yg_loaded{c}") for c in range(NC)]
        up_loaded, gate_loaded = sem("up_loaded"), [sem(f"gate_loaded{q}") for q in range(4)]
        ple_hi, ple_lo = sem("ple_hi"), sem("ple_lo")
        p_loaded, fn_loaded, p_T, pT_hi_ready, pT_lo_ready, pu_done, pu_ready = (sem(n) for n in [
            "p_loaded", "fn_loaded", "p_T", "pT_hi_ready", "pT_lo_ready", "pu_done", "pu_ready"])
        x2_ready, squares3, std3_ready, rstd3_ready, x2_T, h3_ready, h3T_hi_ready, h3T_lo_ready = (sem(n) for n in [
            "x2_ready", "squares3", "std3_ready", "rstd3_ready", "x2_T", "h3_ready", "h3T_hi_ready", "h3T_lo_ready"])
        root_loaded = sem("root_loaded")
        gate_done, gate_sig, x3_ready, squares4, std4_ready, out_ready = (sem(n) for n in [
            "gate_done", "gate_sig", "x3_ready", "squares4", "std4_ready", "out_ready"])

        START = 1
        started = [gates_done, root_ready, sp_params, sgu_done, conv_done, merged_done, z_copied, gate_gelu, u_gelu,
                   ma_sig, mb_sig, ri_sig, sp_evac, y_free, hid_ready, hidT_done, hidT_ready, y0_ready, y1_ready,
                   m_lo_ready]

        block = ctx.enter_context(nc.Block())

        def loads_of(n):
            return 16 * (n // RING + 1)

        ROOTS_OF = [None, 0, 2, 3]
        LAST_SLOT = (PAIRS - 1) % 3
        N_PLE = NPK + NK
        N_MID = NPK

        @block.sync
        def _(sp):
            def load(s, i, first):
                if i < 4:
                    e, m = i // 2, i % 2
                    src = A[("expert_w1", "expert_w3")[m]][0, bass.ds(first + e, 1)].rearrange("a (p k) f -> p k (a f)", k=NK)
                    sp.dma_start(w13[s][e][:, m, :, :], src).then_inc(pair_loaded[s][i], 16)
                else:
                    e = i - 4
                    src = A["expert_w2"][0, bass.ds(first + e, 1)].rearrange("a (c p) n -> p c (a n)", p=P)
                    sp.dma_start(w2[s][:, e, :, :], src).then_inc(pair_loaded[s][i], 16)

            for c in range(NC):
                sp.dma_start(x[:, c, :], A["x"][0, c * P:(c + 1) * P, :]).then_inc(x_loaded[c], 16)
            for name in PAR_INPUTS:
                first, src = (pi["conv_w0"], A[name][0]) if name == "conv_w" else (pi[name], A[name])
                rows = src.shape[0] * NB
                sp.dma_start(par_raw[first * NB:first * NB + rows, :],
                             src.rearrange("w (b c) -> (w b) c", c=P)).then_inc(par_loaded, 16)
            sp.dma_start(ws_raw[:], A["sgu_ws"][0].rearrange("g t s -> t g s")).then_inc(ws_loaded, 16)

            def load_unit(n, src, parts):
                sp.dma_start(raw[n % RING][:].rearrange("p (k n) -> p k n", k=parts), src).then_inc(unit_loaded[n % RING], 16)

            for n in range(N_V):
                j, q = n // 4, n % 4
                if n >= RING:
                    sp.wait_ge(units_done, n - RING + 1)
                load_unit(n, w_in[:, 2 * q:2 * q + 2, V_COL + HALF * j:V_COL + HALF * (j + 1)], 2)
                if n == RING - 1:
                    sp.dma_start(bs_b[:].rearrange("p g t -> p (g t)"),
                                 A["sgu_bs"][0].rearrange("g t -> (g t)")[None, :].broadcast_to((P, NB * P))).then_inc(bs_loaded, 16)
            with sp.Fori(0, NB) as b:
                for j in range(N_BLK):
                    n = N_V + j
                    sp.wait_ge(units_done, b * N_BLK + (n - RING + 1))
                    load_unit(n, w_in[:, :, bass.ds(b * P + BLOCK_COLS[j], P)], NK)
            for n in range(U_WOUT, N_UNITS):
                j, q = (n - U_WOUT) // 4, (n - U_WOUT) % 4
                sp.wait_ge(units_done, n - RING + 1)
                load_unit(n, w_out[:, 2 * q:2 * q + 2, HALF * j:HALF * (j + 1)], 2)
                if n == U_WOUT + 1:
                    for i in range(4):
                        load(0, i, 0)

            def load_pair(s, first, free, h):
                sp.wait_ge(up_done, free)
                for i in range(6):
                    if i >= 2:
                        sp.wait_ge(pair_loaded[s][i - 2], h * 16 + 16)
                    elif s > 0:
                        sp.wait_ge(pair_loaded[s - 1][i + 4], h * 16 + 16)
                    else:
                        sp.wait_ge(pair_loaded[2][i + 4], h * 16)
                    if i == 4:
                        sp.wait_ge(down1_done, free)
                    load(s, i, first)

            sp.wait_ge(units_done, U_WOUT)
            for i in range(4):
                load(1, i, 2)
            sp.wait_ge(merged_done, NB + START)
            for i in (4, 5):
                load(2, i, 4)
            sp.wait_ge(wout_done, NC)
            for i in (4, 5):
                load(0, i, 0)
            for i in range(4):
                load(2, i, 4)
            sp.wait_ge(router_done, NC)
            for i in (4, 5):
                load(1, i, 2)
            sp.wait_ge(n2_stored, 16 * NC)
            sp.wait_ge(rows_loaded, 16)
            sp.dma_start(up_raw[:], ple_up).then_inc(up_loaded, 16)
            sp.dma_start(p_sb[:], A["p"][0, 0].rearrange("(c p) n -> p c n", p=P)).then_inc(p_loaded, 16)
            sp.wait_ge(jobs_ready, 1)

            def end_of(pair):
                return sp.value_load(job_at_i[0:1, bass.ds(pair + 1, 1)], min_val=1, max_val=MAX_JOBS)

            with sp.Fori(0, PAIRS // 3 - 1) as h:
                for s in range(3):
                    load_pair(s, h * 6 + (6 + 2 * s), end_of(h * 3 + s), h + 1)
            load_pair(LAST_SLOT, E - 2, end_of(PAIRS - 4), PAIRS // 3)
            end = end_of(PAIRS - 3)
            sp.wait_ge(up_done, end)
            sp.wait_ge(down1_done, end)
            for q in range(4):
                if q >= 2:
                    sp.wait_ge(gate_loaded[q - 2], 16)
                sp.dma_start(gate_raw[:, 2 * q:2 * q + 2, :], ple_gate[:, 2 * q:2 * q + 2, :]).then_inc(gate_loaded[q], 16)
            jobs = sp.value_load(job_at_i[0:1, PAIRS:PAIRS + 1], min_val=PAIRS, max_val=MAX_JOBS)
            sp.wait_ge(y_free, jobs + START)
            sp.wait_ge(down1_done, jobs)
            for c in range(NC):
                for t in range(2):
                    sp.dma_start(yg[c][t][:], y_rows[T * t + P * c:T * t + P * (c + 1), :]).then_inc(yg_loaded[c], 16)
            sp.dma_start(fn_b[:], A["final_norm"][None, :].broadcast_to((P, D))).then_inc(fn_loaded, 16)
            for c in range(NC):
                sp.wait_ge(out_ready, c + 1)
                sp.dma_start(out[0, c * P:(c + 1) * P, :], o_sb[c][:]).then_inc(stored, 16)
            sp.wait_ge(stored, 16 * NC)

        @block.gpsimd
        def _(pool):
            for s in started:
                pool.sem_inc(s, START)
            nc.gpsimd.memset(ident[:], 0.0).then_inc(zeroed, 1)
            nc.gpsimd.memset(ones[:], 1.0).then_inc(ones_ready, 1)
            nc.gpsimd.memset(stat[:, 0:1], EPS).then_inc(eps_ready, 1)
            pool.wait_ge(zeroed, 1)
            nc.gpsimd.affine_select(out=ident[:], in_=ident[:], compare_op=ALU.not_equal, fill=1.0, base=0,
                                    pattern=[[-1, P]], channel_multiplier=1).then_inc(ident_ready, 1)
            nc.gpsimd.memset(wa_bd[:], 0.0).then_inc(zeroed, 1)
            nc.gpsimd.memset(wi_bd[:], 0.0).then_inc(zeroed, 1)
            pool.wait_ge(zeroed, 3)
            for dst, src in ((wa_bd, A["lru_wa"]), (wi_bd, A["lru_wi"])):
                w = src[0].rearrange("(b two) i j -> two i b j", two=2)
                for h in range(2):
                    pool.dma_start(dst[h * HB:(h + 1) * HB, :, h * HB:(h + 1) * HB], w[h]).then_inc(lruw_loaded, 16)
            pool.wait_ge(ws_loaded, 16)
            nc.gpsimd.affine_select(out=ws_raw[:], in_=ws_raw[:], compare_op=ALU.is_ge, fill=0.0, base=0,
                                    pattern=[[0, NB], [-1, P]], channel_multiplier=1).then_inc(ws_masked, 1)
            nc.gpsimd.memset(z[:, 0:CONV - 1], 0.0).then_inc(z_pad_ready, 1)
            pool.wait_ge(c_ready, 1)
            pool.wait_ge(lruw_loaded, 64)
            pool.wait_ge(wsT_ready, 2)
            with pool.Fori(0, NB) as b:
                pool.wait_ge(gates_done, b + START)
                pool.wait_ge(root_ready, b + START)
                pool.wait_ge(sp_params, b + START)
                nc.gpsimd.tensor_copy(st_par[:], par[:, :, bass.ds(b, 1)].rearrange("p a b -> p (a b)")).then_inc(staged, 1)
                nc.gpsimd.tensor_copy(st_wa[:], wa_bd[:, bass.ds(b, 1), :].rearrange("p a b -> p (a b)")).then_inc(staged, 1)
                nc.gpsimd.tensor_copy(st_wi[:], wi_bd[:, bass.ds(b, 1), :].rearrange("p a b -> p (a b)")).then_inc(staged, 1)
                pool.wait_ge(sgu_done, b + START)
                pool.wait_ge(v_normed, NC)
                nc.gpsimd.tensor_copy(st_ws[:], wsT[:, bass.ds(b, 1), :].rearrange("p a b -> p (a b)")).then_inc(staged_v, 1)
                nc.gpsimd.tensor_copy(st_v[:].rearrange("p c n -> p (c n)"),
                                      vm[:, bass.ds(b, 1), :].rearrange("p a b -> p (a b)")).then_inc(staged_v, 1)

            pool.wait_ge(merged_done, NB + START)
            pool.dma_start(w_r[:, :, 0:NG], A["router_group_w"][0].rearrange("(k p) n -> p k n", p=P)).then_inc(router_loaded, 16)
            pool.dma_start(w_r[:, :, NG:NR], A["router_expert_w"][0].rearrange("(k p) n -> p k n", p=P)).then_inc(router_loaded, 16)
            pool.dma_start(b_r[:, 0:NG], A["router_group_b"].broadcast_to((P, NG))).then_inc(router_loaded, 16)
            pool.dma_start(b_r[:, NG:NR], A["router_expert_b"].broadcast_to((P, E))).then_inc(router_loaded, 16)
            pool.dma_start(g2[:], A["ffn_norm"][0].rearrange("(p k) -> p k", k=NK)).then_inc(router_loaded, 16)
            nc.gpsimd.memset(upper[:], 1.0).then_inc(zeroed, 1)
            nc.gpsimd.iota(tok_col[:], [[P, NC]], base=1, channel_multiplier=1,
                           allow_small_or_imprecise_dtypes=True).then_inc(tables_ready, 1)
            nc.gpsimd.iota(iota_row[:], [[1, CAP]], base=0, channel_multiplier=0,
                           allow_small_or_imprecise_dtypes=True).then_inc(tables_ready, 1)
            nc.gpsimd.iota(rank_row[:], [[-1, EG]], base=EG, channel_multiplier=0,
                           allow_small_or_imprecise_dtypes=True).then_inc(tables_ready, 1)
            nc.gpsimd.iota(job_row[:], [[1, JOBS]], base=0, channel_multiplier=0,
                           allow_small_or_imprecise_dtypes=True).then_inc(tables_ready, 1)
            pool.wait_ge(zeroed, 4)
            nc.gpsimd.affine_select(out=upper[:], in_=upper[:], compare_op=ALU.is_gt, fill=0.0, base=0,
                                    pattern=[[1, P]], channel_multiplier=-1).then_inc(tables_ready, 1)
            last_token, last_row = pool.to_reg(T - 1), pool.to_reg(2 * T - 1)

            def gather():
                pool.indirect_dma_start(out=rows_sb[:].rearrange("p k n -> p (k n)"), out_offset=None, in_=n2_rows[:, :],
                                        in_offset=bass.IndirectOffsetOnAxis(ap=src_st[:, 0:1], axis=0),
                                        bounds_check=last_token, oob_is_err=False).then_inc(rows_loaded, 16)

            pool.wait_ge(n2_stored, 16 * NC)
            nc.gpsimd.memset(rows_sb[:], 0.0).then_inc(rows_cleared, 1)
            for g in range(2):
                pool.wait_ge(idx_ready, g + 1)
                if g > 0:
                    pool.wait_ge(rows_loaded, 16 * g)
                nc.gpsimd.tensor_copy(src_st[:], tok_idx[:, g:g + 1]).then_inc(src_staged, 1)
                pool.wait_ge(src_staged, g + 1)
                if g == 0:
                    pool.wait_ge(rows_cleared, 1)
                else:
                    pool.wait_ge(rows_T, g)
                gather()
            pool.wait_ge(jobs_ready, 1)
            jobs = pool.value_load(job_at_i[0:1, PAIRS:PAIRS + 1], min_val=PAIRS, max_val=MAX_JOBS)

            def scatter(g):
                nc.gpsimd.tensor_copy(dst_idx_st[:], row_idx[:, bass.ds(g, 1)]).then_inc(dst_staged, 1)
                pool.wait_ge(dst_staged, g + 1)
                pool.wait_ge(y0_ready, g + 1 + START)
                pool.wait_ge(y1_ready, g + 1 + START)
                pool.sem_inc(pool_passed, 1)
                pool.indirect_dma_start(out=y_rows[:, :], out_offset=bass.IndirectOffsetOnAxis(ap=dst_idx_st[:, 0:1], axis=0),
                                        in_=y_sb[:], in_offset=None, bounds_check=last_row,
                                        oob_is_err=False).then_inc(y_stored, 16)
                pool.wait_ge(y_stored, g * 16 + 16)
                pool.sem_inc(y_free, 1)

            with pool.Fori(0, jobs - 1) as g:
                pool.wait_ge(idx_ready, g + 3)
                pool.wait_ge(rows_loaded, g * 16 + 32)
                nc.gpsimd.tensor_copy(src_st[:], tok_idx[:, bass.ds(g + 2, 1)]).then_inc(src_staged, 1)
                pool.wait_ge(src_staged, g + 3)
                pool.wait_ge(rows_T, g + 2)
                pool.sem_inc(pool_passed, 1)
                gather()
                scatter(g)
            with pool.Fori(jobs - 1, jobs) as g:
                scatter(g)

        @block.scalar
        def _(act):
            def split_high(n):
                act.wait_ge(unit_loaded[n % RING], loads_of(n))
                if n >= RING:
                    act.wait_ge(units_done, n - RING + 1)
                nc.scalar.activation(w_hi[n % RING][:], raw[n % RING][:], ACT.Copy).then_inc(hi_split, 1)

            for c in range(NC):
                act.wait_ge(x_loaded[c], 16)
                if c > 0:
                    act.wait_ge(squares, c)
                nc.scalar.activation(sq_junk[:], x[:, c, :], ACT.Square, accum_out=stat[:, 4 + c:5 + c]).then_inc(squares, 1)
                if c == 0:
                    act.wait_ge(eps_ready, 1)
                act.wait_ge(squares, c + 1)
                nc.scalar.activation(stat[:, 8 + c:9 + c], stat[:, 4 + c:5 + c], ACT.Sqrt, bias=stat[:, 0:1],
                                     scale=1.0 / D).then_inc(std_ready, 1)
            split_high(0)
            act.wait_ge(x_T, NC)
            act.wait_ge(par_ready, 1)
            for k in range(NK):
                nc.scalar.activation(hT_hi[:, k, :], bank[k][:], ACT.Copy,
                                     scale=par[:, pi["mix_norm"], k:k + 1]).then_inc(hT_hi_ready, 1)
            split_high(1)
            split_high(2)
            lam = par[:, pi["lru_lambda"], :]
            nc.scalar.activation(sp_t[:, 0, :], lam, ACT.Abs).then_inc(softplus_abs, 1)
            split_high(3)
            split_high(4)
            act.wait_ge(softplus_abs, 1)
            nc.scalar.activation(sp_t[:, 1, :], sp_t[:, 0, :], ACT.Exp, scale=-1.0).then_inc(softplus_exp, 1)

            def gelu_v(j):
                act.wait_ge(units_done, 4 * (j + 1))
                for c in range(NC):
                    dst = vm[:, 4 * j:4 * j + 4, c * P:(c + 1) * P]
                    nc.scalar.activation(dst, bank[4 * j + c][:].rearrange("p (g n) -> p g n", n=P),
                                         ACT.Gelu_apprx_tanh).then_inc(v_gelu, 1)

            split_high(5)
            gelu_v(0)
            split_high(6)
            split_high(7)
            split_high(8)
            split_high(9)
            gelu_v(1)

            def copy_z(b):
                act.wait_ge(units_done, b * N_BLK + (N_V + 1))
                act.wait_ge(conv_done, b + START)
                nc.scalar.activation(z[:, CONV - 1:], bank[0][:], ACT.Copy).then_inc(z_copied, 1)

            def channel_block(b, last):
                u0 = b * N_BLK + N_V

                def high(j):
                    m = N_V + j
                    act.wait_ge(unit_loaded[m % RING], b * 16 + loads_of(m))
                    act.wait_ge(units_done, u0 + (j - RING + 1))
                    nc.scalar.activation(w_hi[m % RING][:], raw[m % RING][:], ACT.Copy).then_inc(hi_split, 1)

                def par_of(n):
                    return st_par[:, pi[n]:pi[n] + 1]

                act.wait_ge(units_done, u0 + 2)
                act.wait_ge(merged_done, b + START)
                nc.scalar.activation(tmp["ga"][:], bank[1][:], ACT.Gelu_apprx_tanh).then_inc(gate_gelu, 1)
                high(3)
                act.wait_ge(units_done, u0 + 3)
                nc.scalar.activation(tmp["gu"][:], bank[2][:], ACT.Gelu_apprx_tanh).then_inc(u_gelu, 1)
                high(4)
                act.wait_ge(staged, b * 3 + 3)
                act.wait_ge(gates_done, b + 1 + START)
                nc.scalar.activation(tmp["r"][:], bank[5][:], ACT.Sigmoid, bias=par_of("lru_ba")).then_inc(ri_sig, 1)
                nc.scalar.activation(tmp["i"][:], bank[6][:], ACT.Sigmoid, bias=par_of("lru_bi")).then_inc(ri_sig, 1)
                act.wait_ge(ri_sig, b * 2 + 1 + START)
                nc.scalar.activation(tmp["th"][:], tmp["r"][:], ACT.Tanh, scale=par_of("half_c")).then_inc(tanh_done, 1)
                act.wait_ge(units_done, u0 + 4)
                nc.scalar.activation(tmp["sa"][:], bank[3][:], ACT.Sigmoid).then_inc(ma_sig, 1)
                high(5)
                nc.scalar.activation(tmp["a"][:], tmp["r"][:], ACT.Exp, scale=par_of("neg_c")).then_inc(decay_ready, 1)
                act.wait_ge(tanh_done, b + 1)
                nc.scalar.activation(tmp["th"][:], tmp["th"][:], ACT.Sqrt).then_inc(root_ready, 1)
                high(6)
                act.wait_ge(units_done, u0 + 5)
                nc.scalar.activation(tmp["sb"][:], bank[4][:], ACT.Sigmoid).then_inc(mb_sig, 1)
                if not last:
                    copy_z(b + 1)
                high(7)
                act.wait_ge(merged_done, b + 1 + START)
                nc.scalar.activation(m_hi[:, bass.ds(b, 1), :].rearrange("p a b -> p (a b)"), tmp["s"][:],
                                     ACT.Copy).then_inc(m_hi_ready, 1)

            act.wait_ge(z_pad_ready, 1)
            copy_z(0)
            split_high(N_V + 2)
            act.wait_ge(v_var, NC)
            nc.scalar.activation(stat[:, 16:16 + NC], bn_m[:, :, 1], ACT.Sqrt, bias=stat[:, 0:1]).then_inc(v_std, 1)
            with act.Fori(0, NB - 1) as b:
                channel_block(b, False)
            channel_block(NB - 1, True)
            for n in range(U_WOUT + 3, N_UNITS):
                split_high(n)

            for c in range(NC):
                act.wait_ge(x1_half, NC + c + 1)
                if c > 0:
                    act.wait_ge(squares2, c)
                nc.scalar.activation(junk2[:], x[:, c, :], ACT.Square, accum_out=stat[:, 24 + c:25 + c]).then_inc(squares2, 1)
                act.wait_ge(squares2, c + 1)
                nc.scalar.activation(stat[:, 28 + c:29 + c], stat[:, 24 + c:25 + c], ACT.Sqrt, bias=stat[:, 0:1],
                                     scale=1.0 / D).then_inc(std2_ready, 1)
                act.wait_ge(n2_ready, c + 1)
                act.dma_start(n2_rows[c * P:(c + 1) * P, :], n2[:, c, :, :].rearrange("p k n -> p (k n)")).then_inc(n2_stored, 16)
            act.wait_ge(group_shift, 1)
            nc.scalar.activation(t_g[:], t_g[:], ACT.Exp).then_inc(group_exp, 1)
            act.wait_ge(second_shift, 1)
            nc.scalar.activation(col[:, 5, :], col[:, 4, :], ACT.Exp).then_inc(second_exp, 1)
            act.wait_ge(jobs_ready, 1)

            def job(g):
                act.wait_ge(up_done, g + 1)
                act.wait_ge(hid_ready, g + START)
                nc.scalar.activation(sil[:], bank[0][:, 0:F], ACT.Silu).then_inc(silu_done, 1)
                act.wait_ge(hidT_done, g + 1 + START)
                nc.scalar.activation(hidT[:].rearrange("p c n -> p (c n)"), bank[3][:, 0:F], ACT.Copy).then_inc(hidT_ready, 1)
                act.wait_ge(down0_done, g + 1)
                act.wait_ge(y_free, g + START)
                nc.scalar.activation(y_sb[:, 0:HALF], bank[6][:], ACT.Copy).then_inc(y0_ready, 1)

            def split_high_ple(i):
                if i < NPK:
                    act.wait_ge(up_loaded, 16)
                    nc.scalar.activation(up_hi[:, i, :], up_raw[:, i, :], ACT.Copy).then_inc(ple_hi, 1)
                else:
                    k = i - NPK
                    act.wait_ge(gate_loaded[k // 2], 16)
                    nc.scalar.activation(gate_hi[:, k, :], gate_raw[:, k, :], ACT.Copy).then_inc(ple_hi, 1)

            last_pair = act.value_load(job_at_i[0:1, PAIRS - 1:PAIRS], min_val=PAIRS - 1, max_val=MAX_JOBS)
            with act.Fori(0, last_pair) as g:
                job(g)
            act.wait_ge(down1_done, last_pair)
            for i in range(N_MID):
                split_high_ple(i)
            jobs = act.value_load(job_at_i[0:1, PAIRS:PAIRS + 1], min_val=PAIRS, max_val=MAX_JOBS)
            with act.Fori(last_pair, jobs) as g:
                job(g)
            act.wait_ge(p_T, 1)
            for k in range(NPK):
                nc.scalar.activation(pT_hi[:, k, :], bank[4 + k][:], ACT.Copy).then_inc(pT_hi_ready, 1)
            for i in range(N_MID, N_PLE):
                split_high_ple(i)

            def square3(c):
                act.wait_ge(x2_ready, c + 1)
                if c > 0:
                    act.wait_ge(squares3, c)
                nc.scalar.activation(junk3[:], x[:, c, :], ACT.Square, accum_out=stat[:, 36 + c:37 + c]).then_inc(squares3, 1)

            def high3(c):
                act.wait_ge(h3_ready, 2 * c + 2)
                if c >= 2:
                    act.wait_ge(gate_done, 2 * (c - 1))
                nc.scalar.activation(h3T_hi[c % 2][:], h3[:], ACT.Copy).then_inc(h3T_hi_ready, 1)

            def finish(c):
                for j in range(2):
                    act.wait_ge(gate_done, 2 * c + j + 1)
                    if c > 0:
                        act.wait_ge(x3_ready, 2 * c + j - 1)
                    if c == 0:
                        act.wait_ge(rstd3_ready, 1)
                    nc.scalar.activation(sg[j][:], bank[2 * (c % 2) + j][:], ACT.Sigmoid,
                                         scale=stat[:, 52 + c:53 + c]).then_inc(gate_sig, 1)
                if c == NC - 1:
                    nc.scalar.activation(stat[:, 1:2], stat[:, 0:1], ACT.Sqrt).then_inc(root_loaded, 1)
                act.wait_ge(x3_ready, 2 * c + 2)
                act.wait_ge(squares3, NC)
                if c > 0:
                    act.wait_ge(squares4, c)
                nc.scalar.activation(junk3[:], x[:, c, :], ACT.Square, accum_out=stat[:, 44 + c:45 + c]).then_inc(squares4, 1)
                act.wait_ge(squares4, c + 1)
                first = ROOTS_OF[c]
                if first is not None:
                    nc.scalar.activation(stat[:, 48 + first:49 + c], stat[:, 44 + first:45 + c], ACT.Sqrt, bias=stat[:, 0:1],
                                         scale=1.0 / D).then_inc(std4_ready, 1)

            for c in range(NC):
                act.wait_ge(pu_done, c + 1)
                for j in range(2):
                    nc.scalar.activation(pu[:, c, HALF * j:HALF * (j + 1)], bank[2 * (c % 2) + j][:], ACT.Copy).then_inc(pu_ready, 1)
            high3(0)
            square3(0)
            high3(1)
            for c in range(1, NC):
                square3(c)
            act.wait_ge(squares3, NC)
            nc.scalar.activation(stat[:, 40:40 + NC], stat[:, 36:36 + NC], ACT.Sqrt, bias=stat[:, 0:1],
                                 scale=1.0 / D).then_inc(std3_ready, 1)
            for c in range(NC):
                if c + 2 < NC:
                    high3(c + 2)
                finish(c)

        @block.vector
        def _(dve):
            chain = [0]

            def link(ins):
                ins.then_inc(dve_chain, 1)
                chain[0] = chain[0] + 1
                dve.wait_ge(dve_chain, chain[0])

            tt, ts, stt = nc.vector.tensor_tensor, nc.vector.tensor_scalar, nc.vector.scalar_tensor_tensor
            for c in range(NC):
                dve.wait_ge(std_ready, c + 1)
                link(nc.vector.reciprocal(stat[:, 12 + c:13 + c], stat[:, 8 + c:9 + c]))
                ts(xn[:, c, :], x[:, c, :], stat[:, 12 + c:13 + c], None, ALU.mult).then_inc(xn_ready, 1)
                if c == 2:
                    dve.wait_ge(par_T, 1)
                    nc.vector.tensor_copy(par[:, 0:N_RAW, :].rearrange("p a b -> p (a b)"),
                                          bank[7][:, 0:N_RAW * NB]).then_inc(par_ready, 1)
            def evacuate_ws(h):
                dve.wait_ge(ws_T, h + 1)
                nc.vector.tensor_copy(wsT[:, 4 * h:4 * h + 4, :].rearrange("p a b -> p (a b)"), bank[4 + h][:]).then_inc(wsT_ready, 1)

            def evacuate_rs(h):
                dve.wait_ge(rs_done, h + 1)
                nc.vector.tensor_copy(rs_b[:, 4 * h:4 * h + 4, :].rearrange("p a b -> p (a b)"), bank[6 + h][:]).then_inc(rs_ready, 1)

            def split_low(slot, n_hi):
                dve.wait_ge(hi_split, n_hi)
                tt(w_lo[slot][:], raw[slot][:], w_hi[slot][:].bitcast(F32), ALU.subtract).then_inc(lo_split, 1)

            split_low(0, 1)
            for k in range(NK):
                dve.wait_ge(hT_hi_ready, k + 1)
                stt(hT_lo[:, k, :], bank[k][:], par[:, pi["mix_norm"], k:k + 1], hT_hi[:, k, :].bitcast(F32),
                    ALU.mult, ALU.subtract).then_inc(hT_lo_ready, 1)
            for n in range(1, 4):
                split_low(n, n + 1)
            evacuate_ws(0)
            evacuate_ws(1)
            split_low(4, 5)
            evacuate_rs(0)
            evacuate_rs(1)
            split_low(5 % RING, 6)
            dve.wait_ge(softplus_exp, 1)
            dve.wait_ge(par_ready, 1)
            e, s_, s2, q = sp_t[:, 1, :], sp_t[:, 2, :], sp_t[:, 3, :], sp_t[:, 4, :]
            link(ts(s_, e, 2.0, None, ALU.add))
            link(nc.vector.reciprocal(s_, s_))
            link(tt(s_, s_, e, ALU.mult))
            link(tt(s2, s_, s_, ALU.mult))
            link(ts(q, s2, 1.0 / 17, None, ALU.mult))
            for odd in (15, 13, 11, 9, 7, 5, 3):
                link(stt(q, q, 1.0 / odd, s2, ALU.add, ALU.mult))
            link(stt(q, q, 1.0, s_, ALU.add, ALU.mult))
            link(ts(s_, par[:, pi["lru_lambda"], :], -1.0, 0.0, ALU.mult, ALU.max))
            link(stt(q, q, 2.0, s_, ALU.mult, ALU.add))
            link(ts(par[:, pi["neg_c"], :], q, -LRU_C, None, ALU.mult))
            ts(par[:, pi["half_c"], :], q, LRU_C / 2, None, ALU.mult).then_inc(c_ready, 1)
            for n in range(6, N_V + 2):
                split_low(n % RING, n + 1)
            dve.wait_ge(v_gelu, 2 * NC)
            for c in range(NC):
                for h in range(2):
                    nc.vector.bn_stats(bn_s[:, c, h, :], vm[:, 4 * h:4 * h + 4, c * P:(c + 1) * P]).then_inc(dve_chain, 1)
                chain[0] += 2
                dve.wait_ge(dve_chain, chain[0])
                nc.vector.bn_aggr(bn_m[:, c, :], bn_s[:, c, :, :].rearrange("p h s -> p (h s)")).then_inc(v_var, 1)
            def convolve(b):
                xa = tmp["xa"]
                par_of = lambda n: st_par[:, pi[n]:pi[n] + 1]
                dve.wait_ge(staged, b * 3 + 1)
                dve.wait_ge(z_copied, b + 1 + START)
                dve.wait_ge(gates_done, b + START)
                link(ts(xa[:], z[:, CONV - 1:], par_of(f"conv_w{CONV - 1}"), par_of("conv_b"), ALU.mult, ALU.add))
                for t in (CONV - 2, CONV - 3):
                    link(stt(xa[:], z[:, t:t + T], par_of(f"conv_w{t}"), xa[:], ALU.mult, ALU.add))
                stt(xa[:], z[:, 0:T], par_of("conv_w0"), xa[:], ALU.mult, ALU.add).then_inc(conv_done, 1)

            dve.wait_ge(bs_loaded, 16)
            dve.wait_ge(rs_ready, 2)
            convolve(0)
            split_low((N_V + 2) % RING, N_V + 3)
            dve.wait_ge(v_std, 1)
            link(nc.vector.reciprocal(stat[:, 20:20 + NC], stat[:, 16:16 + NC]))
            for c in range(NC):
                vc = vm[:, :, c * P:(c + 1) * P]
                ts(vc, vc, bn_m[:, c, 0:1], stat[:, 20 + c:21 + c], ALU.subtract, ALU.mult).then_inc(v_normed, 1)

            before = chain[0]
            LINKS = 11

            def channel_block(b, last):
                u0 = b * N_BLK + N_V
                chain[0] = b * LINKS + before

                def low(j):
                    m = N_V + j
                    split_low(m % RING, u0 + (j + 1))

                def par_of(n):
                    return st_par[:, pi[n]:pi[n] + 1]

                xa, th, s = tmp["xa"], tmp["th"], tmp["s"]
                low(3)
                low(4)
                dve.wait_ge(ri_sig, b * 2 + 2 + START)
                link(tt(tmp["i"][:], tmp["i"][:], xa[:], ALU.mult))
                dve.wait_ge(sgu_done, b + 1 + START)
                cb = lambda w: w[:, bass.ds(b, 1), :].broadcast_to((P, NC, P))
                s3 = s[:].rearrange("p (c n) -> p c n", c=NC)
                ins = stt(s3, bank[7][:].rearrange("p (c n) -> p c n", c=NC), par_of("sgu_ln_g"), cb(bs_b), ALU.mult, ALU.add)
                ins.then_inc(sp_evac, 1)
                dve.wait_ge(sp_evac, b + 1 + START)
                ins = stt(s3, cb(rs_b), par_of("sgu_ln_b"), s3, ALU.mult, ALU.add)
                ins.then_inc(sp_params, 1)
                dve.wait_ge(sp_params, b + 1 + START)
                dve.wait_ge(u_gelu, b + 1 + START)
                link(tt(s[:], s[:], tmp["gu"][:], ALU.mult))
                low(5)
                dve.wait_ge(decay_ready, b + 1)
                dve.wait_ge(root_ready, b + 1 + START)
                link(stt(th[:], tmp["a"][:], 1.0, th[:], ALU.add, ALU.mult))
                low(6)
                link(tt(th[:], th[:], tmp["i"][:], ALU.mult))
                h = tmp["i"]
                link(nc.vector.tensor_tensor_scan(h[:], tmp["a"][:], th[:], 0.0, ALU.mult, ALU.add))
                if not last:
                    convolve(b + 1)
                low(7)
                link(tt(h[:], h[:], tmp["ga"][:], ALU.mult))
                link(tt(h[:], h[:], tmp["sa"][:], ALU.mult))
                dve.wait_ge(mb_sig, b + 1 + START)
                link(tt(s[:], s[:], tmp["sb"][:], ALU.mult))
                tt(s[:], h[:], s[:], ALU.add).then_inc(merged_done, 1)
                dve.wait_ge(m_hi_ready, b + 1)
                tt(m_lo[:, bass.ds(b, 1), :].rearrange("p a b -> p (a b)"), s[:],
                   m_hi[:, bass.ds(b, 1), :].rearrange("p a b -> p (a b)").bitcast(F32), ALU.subtract).then_inc(m_lo_ready, 1)

            def second_norm(c):
                dve.wait_ge(x1_T, c + 1)
                if c == 0:
                    dve.wait_ge(router_loaded, 16 * 5)
                    dve.wait_ge(tables_ready, 5)
                    dve.wait_ge(ones_ready, 1)
                    nc.vector.tensor_copy(upper_r[:], upper[:]).then_inc(counters_ready, 1)
                    nc.vector.tensor_copy(ones_r[:], ones[:]).then_inc(counters_ready, 1)
                for h in range(2):
                    src = bank[2 * (c % 2) + h][:].rearrange("p (k t) -> p k t", k=4)
                    tt(h2T[:, 4 * h:4 * h + 4, c * P:(c + 1) * P], src,
                       par[:, pi["ffn_norm"], 4 * h:4 * h + 4].unsqueeze(2).broadcast_to((P, 4, P)), ALU.mult).then_inc(h2T_ready, 1)
                dve.wait_ge(std2_ready, c + 1)
                link(nc.vector.reciprocal(stat[:, 32 + c:33 + c], stat[:, 28 + c:29 + c]))
                ts(n2[:, c, :, :], x[:, c, :].rearrange("t (p k) -> t k p", k=NK), stat[:, 32 + c:33 + c], None,
                   ALU.mult).then_inc(n2_ready, 1)

            def first_of(one, score, top, ranks, v, vmax, n):
                bc = lambda a: a.unsqueeze(2).broadcast_to((P, NC, n))
                link(tt(score, v, bc(vmax), ALU.is_equal))
                link(tt(score, score, ranks.unsqueeze(1).broadcast_to((P, NC, n)), ALU.mult))
                link(nc.vector.tensor_reduce(top, score, axis=AX.X, op=ALU.max))
                link(tt(one, score, bc(top), ALU.is_equal))

            def indices(g):
                dve.wait_ge(idx_summed, g + 1)
                for e in range(2):
                    rows = slice(e * CAP, (e + 1) * CAP)
                    ts(row_z[rows, 0:1], bank[4][rows, e:e + 1], 0.0, float(4 * T), ALU.is_equal, ALU.mult).then_inc(row_z_ready, 1)
                    dve.wait_ge(row_z_ready, g * 2 + (e + 1))
                    stt(row_idx[rows, bass.ds(g, 1)], bank[4][rows, e:e + 1], -1.0, row_z[rows, 0:1],
                        ALU.add, ALU.add).then_inc(row_idx_ready, 1)
                dve.wait_ge(row_idx_ready, g * 2 + 2)
                ts(tok_idx[:, bass.ds(g, 1)], row_idx[:, bass.ds(g, 1)], 3 * T - 1, None, ALU.bitwise_and).then_inc(idx_ready, 1)

            def route():
                red = nc.vector.tensor_reduce
                dve.wait_ge(router_done, NC)
                for c in range(NC):
                    ins = stt(lg[:, c, :], bank[4][:, c * NR:(c + 1) * NR], stat[:, 32 + c:33 + c], b_r[:], ALU.mult, ALU.add)
                    ins.then_inc(dve_chain, 1)
                chain[0] += NC
                dve.wait_ge(dve_chain, chain[0])
                gl = lg[:, :, 0:NG]
                link(red(col[:, 0, :], gl, axis=AX.X, op=ALU.max))
                tt(t_g[:], gl, col[:, 0, :].unsqueeze(2).broadcast_to((P, NC, NG)), ALU.subtract).then_inc(group_shift, 1)
                first_of(one_g[:], t_eg[:, :, 0, :], col[:, 1, :], rank_row[:, EG - NG:EG], gl, col[:, 0, :], NG)
                link(tt(t_eg[:], lg[:, :, NG:NR].rearrange("p c (g e) -> p c e g", g=NG),
                        one_g[:].unsqueeze(2).broadcast_to((P, NC, EG, NG)), ALU.mult))
                link(red(es[:], t_eg[:], axis=AX.X, op=ALU.add))
                link(red(col[:, 2, :], es[:], axis=AX.X, op=ALU.max))
                first_of(one1[:], t_e[:], col[:, 1, :], rank_row[:], es[:], col[:, 2, :], EG)
                link(stt(es2[:], one1[:], -1e30, es[:], ALU.mult, ALU.add))
                link(red(col[:, 3, :], es2[:], axis=AX.X, op=ALU.max))
                tt(col[:, 4, :], col[:, 3, :], col[:, 2, :], ALU.subtract).then_inc(second_shift, 1)
                first_of(one2[:], t_e[:], col[:, 1, :], rank_row[:], es2[:], col[:, 3, :], EG)
                for one, M in ((one1, M1), (one2, M2)):
                    link(tt(M[:].rearrange("p c (g e) -> p c g e", g=NG), one_g[:].unsqueeze(3).broadcast_to((P, NC, NG, EG)),
                            one[:].unsqueeze(2).broadcast_to((P, NC, NG, EG)), ALU.mult))
                tt(MM[:], M1[:], M2[:], ALU.add).then_inc(masks_ready, 1)
                dve.wait_ge(group_exp, 1)
                link(red(col[:, 6, :], t_g[:], axis=AX.X, op=ALU.add))
                link(nc.vector.reciprocal(col[:, 7, :], col[:, 6, :]))
                dve.wait_ge(second_exp, 1)
                link(ts(col[:, 8, :], col[:, 5, :], 1.0, None, ALU.add))
                link(nc.vector.reciprocal(col[:, 9, :], col[:, 8, :]))
                link(tt(col[:, 10, :], col[:, 7, :], col[:, 9, :], ALU.mult))
                link(tt(col[:, 11, :], col[:, 10, :], col[:, 5, :], ALU.mult))
                dve.wait_ge(pos_done, 1)
                dve.wait_ge(masks_ready, 1)
                link(stt(prod[:], bank[5][:, 0:NC * E].rearrange("p (c e) -> p c e", c=NC), 1.0, MM[:].bitcast(F32), ALU.add, ALU.mult))
                by_pair = lambda w: w[:].rearrange("p c (i t) -> p c i t", t=2)
                link(ts(posr[:].rearrange("p i c t -> p c i t"), by_pair(prod), -1.0, None, ALU.add))
                link(tt(prod[:], MM[:].bitcast(F32), tok_col[:].unsqueeze(2).broadcast_to((P, NC, E)), ALU.mult))
                link(stt(prod[:], M2[:], float(T), prod[:], ALU.mult, ALU.add))
                link(nc.vector.tensor_copy(dstr[:].rearrange("p i c t -> p c i t"), by_pair(prod)))
                select(0, 0)
                counts = bank[5][:, NC * E:(NC + 1) * E].rearrange("p (i t) -> p i t", t=2)
                link(red(reps_f[:], counts, axis=AX.X, op=ALU.max))
                link(ts(reps_i[:], reps_f[:], float(CAP - 1), None, ALU.add))
                link(ts(reps_i[:], reps_i[:], 6, None, ALU.arith_shift_right))
                link(nc.vector.tensor_copy(reps_f[:], reps_i[:]))
                link(ts(reps_f[:], reps_f[:], 1.0, None, ALU.max))
                indices(0)
                link(nc.vector.memset(job_at[:, 0:1], 0.0))
                link(ts(pair_f[:, 0:PAIRS], reps_f[:], 0.0, 1.0, ALU.mult, ALU.add))
                link(nc.vector.tensor_tensor_scan(job_at[:, 1:], pair_f[:, 0:PAIRS], reps_f[:], 0.0, ALU.mult, ALU.add))
                link(nc.vector.tensor_copy(job_at_i[:], job_at[:]))
                bj = lambda a: a.unsqueeze(2).broadcast_to((P, JOBS, PAIRS))
                bp = lambda a: a.unsqueeze(1).broadcast_to((P, JOBS, PAIRS))
                link(tt(job_cmp[:], bj(job_row[:]), bp(job_at[:, 1:]), ALU.is_ge))
                link(red(pair_f[:], job_cmp[:], axis=AX.X, op=ALU.add))
                link(ts(pair_i[:], pair_f[:], float(PAIRS - 1), None, ALU.min))
                link(tt(job_cmp[:], job_cmp[:], bp(reps_f[:]), ALU.mult))
                link(red(job_off[:], job_cmp[:], axis=AX.X, op=ALU.add))
                link(tt(job_off[:], job_row[:], job_off[:], ALU.subtract))
                ts(job_off[:], job_off[:], float(CAP), None, ALU.mult).then_inc(jobs_ready, 1)

            def select(g, pair):
                if pair is None:
                    pair = dve.value_load(pair_i[0:1, bass.ds(g, 1)], min_val=0, max_val=PAIRS - 1)
                    ins = ts(iota_off[:], iota_row[:], job_off[:, bass.ds(g, 1)], None, ALU.add)
                    row = iota_off
                    ins.then_inc(off_ready, 1)
                    dve.wait_ge(off_ready, g)
                else:
                    row = iota_row
                at_pair = lambda w: w[:, bass.ds(pair, 1), :, :].rearrange("p i c t -> p (i c t)")
                nc.vector.tensor_copy(dst_st[:].rearrange("p c t -> p (c t)"), at_pair(dstr)).then_inc(sel_ready, 1)
                tt(sel[:], row[:].unsqueeze(1).broadcast_to((P, 2 * NC, CAP)),
                   at_pair(posr).unsqueeze(2).broadcast_to((P, 2 * NC, CAP)), ALU.is_equal).then_inc(sel_ready, 1)

            def evacuate_gathered(g):
                dve.wait_ge(rows_T, g + 1)
                for h in range(2):
                    tt(gT[:, 4 * h:4 * h + 4, :], bank[1 + h][:].rearrange("p (k t) -> p k t", k=4),
                       g2[:, 4 * h:4 * h + 4].unsqueeze(2).broadcast_to((P, 4, P)), ALU.mult).then_inc(gT_ready, 1)

            def job(g):
                dve.wait_ge(silu_done, g + 1)
                dve.wait_ge(hidT_done, g + START)
                tt(hid[:], sil[:], bank[0][:, F:2 * F], ALU.mult).then_inc(hid_ready, 1)
                evacuate_gathered(g + 1)
                indices(g + 2)
                select(g + 3, None)
                dve.wait_ge(down1_done, g + 1)
                dve.wait_ge(y_free, g + START)
                nc.vector.tensor_copy(y_sb[:, HALF:D], bank[7][:]).then_inc(y1_ready, 1)

            def split_low_ple(i):
                dve.wait_ge(ple_hi, i + 1)
                k = i - NPK
                raw_w, hi, lo = (up_raw[:, i, :], up_hi[:, i, :], up_lo[:, i, :]) if i < NPK else (
                    gate_raw[:, k, :], gate_hi[:, k, :], gate_lo[:, k, :])
                tt(lo, raw_w, hi.bitcast(F32), ALU.subtract).then_inc(ple_lo, 1)

            def experts():
                dve.wait_ge(jobs_ready, 1)
                select(1, None)
                indices(1)
                evacuate_gathered(0)
                select(2, None)
                last_pair = dve.value_load(job_at_i[0:1, PAIRS - 1:PAIRS], min_val=PAIRS - 1, max_val=MAX_JOBS)
                with dve.Fori(0, last_pair) as g:
                    job(g)
                for i in range(N_MID):
                    split_low_ple(i)
                jobs = dve.value_load(job_at_i[0:1, PAIRS:PAIRS + 1], min_val=PAIRS, max_val=MAX_JOBS)
                with dve.Fori(last_pair, jobs) as g:
                    job(g)

            def ple():
                for k in range(NPK):
                    dve.wait_ge(pT_hi_ready, k + 1)
                    tt(pT_lo[:, k, :], bank[4 + k][:], pT_hi[:, k, :].bitcast(F32), ALU.subtract).then_inc(pT_lo_ready, 1)
                for i in range(N_MID, N_PLE):
                    split_low_ple(i)

                def add_experts(c):
                    dve.wait_ge(yg_loaded[c], 32)
                    link(stt(x[:, c, :], yg[c][0][:], col[:, 10, c:c + 1], x[:, c, :], ALU.mult, ALU.add))
                    stt(x[:, c, :], yg[c][1][:], col[:, 11, c:c + 1], x[:, c, :], ALU.mult, ALU.add).then_inc(x2_ready, 1)

                def low3(c):
                    dve.wait_ge(x2_T, c + 1)
                    if c > 0:
                        dve.wait_ge(h3T_lo_ready, c)
                    for h in range(2):
                        g3 = par[:, pi["ple_norm"], 4 * h:4 * h + 4]
                        tt(h3[:, 4 * h:4 * h + 4, :], bank[6 + h][:].rearrange("p (k t) -> p k t", k=4),
                           g3.unsqueeze(2).broadcast_to((P, 4, P)), ALU.mult).then_inc(h3_ready, 1)
                    dve.wait_ge(h3T_hi_ready, c + 1)
                    tt(h3T_lo[c % 2][:], h3[:], h3T_hi[c % 2][:].bitcast(F32), ALU.subtract).then_inc(h3T_lo_ready, 1)

                def finish(c):
                    dve.wait_ge(pu_ready, 2 * c + 2)
                    for j in range(2):
                        dve.wait_ge(gate_sig, 2 * c + j + 1)
                        ps = pu[:, c, HALF * j:HALF * (j + 1)]
                        xs = x[:, c, HALF * j:HALF * (j + 1)]
                        link(tt(ps, sg[j][:], ps, ALU.mult))
                        tt(xs, xs, ps, ALU.add).then_inc(x3_ready, 1)

                def final_norm(c):
                    dve.wait_ge(std4_ready, max(c, 1))
                    dve.wait_ge(fn_loaded, 16)
                    link(nc.vector.reciprocal(stat[:, 56 + c:57 + c], stat[:, 48 + c:49 + c]))
                    stt(o_sb[c][:], x[:, c, :], stat[:, 56 + c:57 + c], fn_b[:], ALU.mult, ALU.mult).then_inc(out_ready, 1)

                add_experts(0)
                low3(0)
                add_experts(1)
                add_experts(2)
                low3(1)
                add_experts(3)
                dve.wait_ge(std3_ready, 1)
                nc.vector.reciprocal(stat[:, 52:52 + NC], stat[:, 40:40 + NC]).then_inc(rstd3_ready, 1)
                for c in range(NC):
                    if c + 2 < NC:
                        low3(c + 2)
                    finish(c)
                    if ROOTS_OF[c] is not None:
                        for cc in range(ROOTS_OF[c], c + 1):
                            final_norm(cc)

            with dve.Fori(0, NB - 1) as b:
                channel_block(b, False)
            channel_block(NB - 1, True)
            for n in range(U_WOUT + 3, N_UNITS):
                split_low(n % RING, n + 1)
            for j in range(2):
                for c in range(NC):
                    if j == 0:
                        dve.wait_ge(units_done, U_WOUT + 4)
                    else:
                        dve.wait_ge(wout_done, c + 1)
                    xs = x[:, c, HALF * j:HALF * (j + 1)]
                    tt(xs, xs, bank[4 * j + c][:], ALU.add).then_inc(x1_half, 1)
                    if j == 1:
                        second_norm(c)
            route()
            experts()
            ple()

        @block.tensor
        def _(pe):
            mm, tr = nc.tensor.matmul, nc.tensor.transpose

            pe.wait_ge(ident_ready, 1)
            pe.wait_ge(par_loaded, 16 * len(PAR_INPUTS))
            tr(bank[7][:, 0:N_RAW * NB], par_raw[:], ident[0:N_RAW * NB, 0:N_RAW * NB]).then_inc(par_T, 1)
            for c in range(NC):
                pe.wait_ge(xn_ready, c + 1)
                for k in range(NK):
                    if c == 0 and k == NK - 1:
                        pe.wait_ge(par_ready, 1)
                    last = tr(bank[k][:, c * P:(c + 1) * P], xn[:, c, k * P:(k + 1) * P], ident[:])
                last.then_inc(x_T, 1)

            def transpose_ws():
                pe.wait_ge(ws_masked, 1)
                for g in range(NB):
                    last = tr(bank[4 + g // 4][:, (g % 4) * P:(g % 4 + 1) * P], ws_raw[:, g, :], ident[:])
                    if g % 4 == 3:
                        last.then_inc(ws_T, 1)

            def sum_ws_rows():
                pe.wait_ge(ones_ready, 1)
                for h in range(2):
                    pe.wait_ge(wsT_ready, h + 1)
                    mm(bank[6 + h][:], ones[:], wsT[:, 4 * h:4 * h + 4, :].rearrange("p a b -> p (a b)"),
                       start=True, stop=True).then_inc(rs_done, 1)

            def products(dst, hi_s, lo_s, hi_m, lo_m, start, stop):
                mm(dst, hi_s, hi_m, start=start, stop=False)
                mm(dst, hi_s, lo_m, start=False, stop=False)
                return mm(dst, lo_s, hi_m, start=False, stop=stop)

            for n in range(N_V):
                j, q = n // 4, n % 4
                pe.wait_ge(lo_split, n + 1)
                if n == 0:
                    pe.wait_ge(hT_lo_ready, 4)
                if n in (1, 2, 3, 4):
                    pe.wait_ge(hT_lo_ready, min(2 * n + 2, NK))
                if n == 4:
                    pe.wait_ge(wsT_ready, 2)
                    pe.wait_ge(rs_ready, 2)
                s = n % RING
                for c in range(NC):
                    for kk in range(2):
                        k = 2 * q + kk
                        cs = slice(c * P, (c + 1) * P)
                        ms = slice(kk * HALF, (kk + 1) * HALF)
                        last = products(bank[4 * j + c][:], hT_hi[:, k, cs], hT_lo[:, k, cs], w_hi[s][:, ms], w_lo[s][:, ms],
                                        k == 0, k == NK - 1)
                last.then_inc(units_done, 1)
                if n == 1:
                    pe.wait_ge(hT_lo_ready, NK)
                    transpose_ws()
                if n == 2:
                    sum_ws_rows()

            freed = [z_copied, gate_gelu, u_gelu, ma_sig, mb_sig]
            pe.wait_ge(v_gelu, NC)
            with pe.Fori(0, NB) as b:
                u0 = b * N_BLK + N_V
                for j in range(N_BLK):
                    pe.wait_ge(lo_split, u0 + (j + 1))
                    pe.wait_ge(freed[j], b + START)
                    s = (N_V + j) % RING
                    for k in range(NK):
                        cs = slice(k * P, (k + 1) * P)
                        last = products(bank[j][:], w_hi[s][:, cs], w_lo[s][:, cs], hT_hi[:, k, :], hT_lo[:, k, :],
                                        k == 0, k == NK - 1)
                    last.then_inc(units_done, 1)
                    if j == 1:
                        pe.wait_ge(v_gelu, 2 * NC)
                        pe.wait_ge(conv_done, b + 1 + START)
                        pe.wait_ge(staged, b * 3 + 3)
                        pe.wait_ge(ri_sig, b * 2 + START)
                        mm(bank[5][:], st_wa[:], tmp["xa"][:], start=True, stop=True)
                        mm(bank[6][:], st_wi[:], tmp["xa"][:], start=True, stop=True).then_inc(gates_done, 1)
                    if j == 2:
                        pe.wait_ge(staged_v, b * 2 + 2)
                        pe.wait_ge(sp_evac, b + START)
                        for c in range(NC):
                            last = mm(bank[7][:, c * P:(c + 1) * P], st_v[:, c, :], st_ws[:], start=True, stop=True)
                        last.then_inc(sgu_done, 1)
            def w_out_products(n, c, half):
                q = (n - U_WOUT) % 4
                for kk in range(2):
                    k = 2 * q + kk
                    cs, ms = slice(c * P, (c + 1) * P), slice(kk * HALF, (kk + 1) * HALF)
                    last = products(bank[4 * half + c][:], m_hi[:, k, cs], m_lo[:, k, cs], w_hi[n % RING][:, ms],
                                    w_lo[n % RING][:, ms], k == 0, k == NK - 1)
                return last

            for s in freed[:4]:
                pe.wait_ge(s, NB + START)
            for q in range(4):
                n = U_WOUT + q
                pe.wait_ge(lo_split, n + 1)
                pe.wait_ge(m_lo_ready, 2 * q + 2 + START)
                for c in range(NC):
                    last = w_out_products(n, c, 0)
                last.then_inc(units_done, 1)
            pe.wait_ge(mb_sig, NB + START)
            pe.wait_ge(ri_sig, 2 * NB + START)
            pe.wait_ge(sp_evac, NB + START)

            def second_half(c):
                for n in range(U_WOUT + 4, N_UNITS):
                    if c == 0:
                        pe.wait_ge(lo_split, n + 1)
                    last = w_out_products(n, c, 1)
                last.then_inc(wout_done, 1)

            def transpose_x1(c):
                pe.wait_ge(x1_half, NC + c + 1)
                if c >= 2:
                    pe.wait_ge(h2T_ready, 2 * (c - 1))
                for k in range(NK):
                    last = tr(bank[2 * (c % 2) + k // 4][:, (k % 4) * P:(k % 4 + 1) * P], x[:, c, k * P:(k + 1) * P], ident[:])
                last.then_inc(x1_T, 1)

            def router(c):
                pe.wait_ge(h2T_ready, 2 * c + 2)
                for k in range(NK):
                    last = mm(bank[4][:, c * NR:(c + 1) * NR], h2T[:, k, c * P:(c + 1) * P], w_r[:, k, :],
                              start=(k == 0), stop=(k == NK - 1))
                last.then_inc(router_done, 1)

            second_half(0)
            second_half(1)
            transpose_x1(0)
            second_half(2)
            transpose_x1(1)
            second_half(3)
            for c in range(NC):
                if c >= 2:
                    transpose_x1(c)
                router(c)
            pe.wait_ge(masks_ready, 1)
            pe.wait_ge(counters_ready, 2)
            pe.wait_ge(x1_half, NC + 2)
            for c in range(NC + 1):
                for cc in range(min(c + 1, NC)):
                    m = upper_r if cc == c else ones_r
                    last = mm(bank[5][:, c * E:(c + 1) * E], m[:], MM[:, cc, :], start=(cc == 0), stop=(cc == min(c, NC - 1)))
            last.then_inc(pos_done, 1)

            def index_sums(g):
                pe.wait_ge(sel_ready, g * 2 + 2)
                if not isinstance(g, int) or g > 0:
                    pe.wait_ge(idx_ready, g)
                for c in range(NC):
                    last = mm(bank[4][:, 0:2], sel[:, 2 * c:2 * c + 2, :].rearrange("p e n -> p (e n)"), dst_st[:, c, :],
                              start=(c == 0), stop=(c == NC - 1))
                last.then_inc(idx_summed, 1)

            def transpose_rows(g):
                pe.wait_ge(rows_loaded, g * 16 + 16)
                if not isinstance(g, int):
                    pe.wait_ge(gT_ready, g * 2)
                for k in range(NK):
                    last = tr(bank[1 + k // 4][:, (k % 4) * P:(k % 4 + 1) * P], rows_sb[:, k, :], ident[:])
                last.then_inc(rows_T, 1)

            pe.wait_ge(h2T_ready, 2 * NC)
            index_sums(0)
            transpose_rows(0)
            index_sums(1)
            pe.wait_ge(jobs_ready, 1)
            rows = [slice(0, CAP), slice(CAP, P)]

            def job(g, s, h):
                pe.wait_ge(gT_ready, g * 2 + 2)
                pe.wait_ge(hid_ready, g + START)
                for i in range(4):
                    pe.wait_ge(pair_loaded[s][i], h * 16 + 16)
                for k in range(NK):
                    for e in range(2):
                        last = mm(bank[0][rows[e], :], gT[:, k, rows[e]], w13[s][e][:, :, k, :],
                                  start=(k == 0), stop=(k == NK - 1))
                last.then_inc(up_done, 1)
                index_sums(g + 2)
                transpose_rows(g + 1)
                pe.wait_ge(hid_ready, g + 1 + START)
                pe.wait_ge(hidT_ready, g + START)
                for f in range(FC):
                    last = tr(bank[3][:, f * P:(f + 1) * P], hid[:, f * P:(f + 1) * P], ident[:])
                last.then_inc(hidT_done, 1)
                pe.wait_ge(hidT_ready, g + 1 + START)
                for i in (4, 5):
                    pe.wait_ge(pair_loaded[s][i], h * 16 + 16)
                for j in range(2):
                    pe.wait_ge((y0_ready, y1_ready)[j], g + START)
                    for f in range(FC):
                        for e in range(2):
                            last = mm(bank[6 + j][rows[e], :], hidT[:, f, rows[e]], w2[s][:, e, f, HALF * j:HALF * (j + 1)],
                                      start=(f == 0), stop=(f == FC - 1))
                    last.then_inc((down0_done, down1_done)[j], 1)

            def pair_jobs(s, pair, h):
                first, end = (pe.value_load(job_at_i[0:1, bass.ds(pair + i, 1)], min_val=0, max_val=MAX_JOBS) for i in range(2))
                with pe.Fori(first, end) as g:
                    job(g, s, h)

            with pe.Fori(0, PAIRS // 3) as h:
                for s in range(3):
                    pair_jobs(s, h * 3 + s, h)
            pair_jobs(LAST_SLOT, PAIRS - 1, PAIRS // 3)
            jobs = pe.value_load(job_at_i[0:1, PAIRS:PAIRS + 1], min_val=PAIRS, max_val=MAX_JOBS)
            pe.wait_ge(p_loaded, 16)
            pe.wait_ge(idx_ready, jobs + 2)
            for k in range(NPK):
                for c in range(NC):
                    last = tr(bank[4 + k][:, c * P:(c + 1) * P], p_sb[:, c, k * P:(k + 1) * P], ident[:])
            last.then_inc(p_T, 1)
            pe.wait_ge(hid_ready, jobs + START)
            pe.wait_ge(gT_ready, jobs * 2 + 2)
            pe.wait_ge(hidT_ready, jobs + START)
            pe.wait_ge(pT_lo_ready, NPK)
            pe.wait_ge(ple_lo, NPK)
            for c in range(NC):
                if c >= 2:
                    pe.wait_ge(pu_ready, 2 * (c - 1))
                for j in range(2):
                    for k in range(NPK):
                        cs, ms = slice(c * P, (c + 1) * P), slice(j * HALF, (j + 1) * HALF)
                        last = products(bank[2 * (c % 2) + j][:], pT_hi[:, k, cs], pT_lo[:, k, cs], up_hi[:, k, ms],
                                        up_lo[:, k, ms], k == 0, k == NPK - 1)
                last.then_inc(pu_done, 1)
            pe.wait_ge(y0_ready, jobs + START)
            pe.wait_ge(y1_ready, jobs + START)

            def transpose_x2(c):
                pe.wait_ge(x2_ready, c + 1)
                if c > 0:
                    pe.wait_ge(h3_ready, 2 * c)
                for k in range(NK):
                    last = tr(bank[6 + k // 4][:, (k % 4) * P:(k % 4 + 1) * P], x[:, c, k * P:(k + 1) * P], ident[:])
                last.then_inc(x2_T, 1)

            transpose_x2(0)
            for c in range(NC):
                if c == 0:
                    pe.wait_ge(ple_lo, N_PLE)
                pe.wait_ge(h3T_lo_ready, c + 1)
                if c < 2:
                    pe.wait_ge(pu_ready, 2 * (c + 3))
                else:
                    pe.wait_ge(gate_sig, 2 * (c - 1))
                if 0 < c < NC - 1:
                    transpose_x2(c + 1)
                for j in range(2):
                    for k in range(NK):
                        ms = slice(j * HALF, (j + 1) * HALF)
                        last = products(bank[2 * (c % 2) + j][:], h3T_hi[c % 2][:, k, :], h3T_lo[c % 2][:, k, :],
                                        gate_hi[:, k, ms], gate_lo[:, k, ms], k == 0, k == NK - 1)
                    last.then_inc(gate_done, 1)
                    if j == 0 and c == 0:
                        transpose_x2(1)

def kernel(**inputs):
    import numpy as _np
    import concourse.bacc as _bacc
    from concourse import mybir as _mybir
    from concourse.bass_utils import run_bass_kernel_spmd as _run

    nc = _bacc.Bacc("TRN2", target_bir_lowering=False, num_devices=1)
    arrays, args = {}, {}
    for name, a in inputs.items():
        a = _np.ascontiguousarray(a)
        arrays[f"in_{name}_dram"] = a
        args[name] = nc.dram_tensor(f"in_{name}_dram", a.shape, _mybir.dt.from_np(a.dtype), kind="ExternalInput").ap()
    shape = inputs["x"].shape
    out = nc.dram_tensor("out_dram", shape, _mybir.dt.float32, kind="ExternalOutput").ap()
    y_rows = nc.dram_tensor("y_rows", (2 * shape[1], shape[2]), _mybir.dt.float32).ap()
    n2_rows = nc.dram_tensor("n2_rows", shape[1:], _mybir.dt.float32).ap()
    hybrid_block_program(nc, args, n2_rows, y_rows, out)
    r = _run(nc, [arrays], core_ids=[0])
    return r.results[0]["out_dram"]
```
